# Optimizing a Trainium2 kernel written in Bass

```python
import math
import jax, jax.numpy as jnp
from jax import lax
import numpy as np

D_MODEL = 1024
BATCH = 1
SEQ = 256
DEPTH = 2

N_A_LAYERS = DEPTH // 2
N_B_LAYERS = DEPTH - N_A_LAYERS
N_DENSE = (DEPTH + 1) // 2
N_MOE = DEPTH // 2

D_RNN = D_MODEL
N_LRU_BLOCKS = 8
LRU_BW = D_RNN // N_LRU_BLOCKS
CONV_W = 4
LRU_C = 8.0

N_HEADS = 16
HEAD_DIM = 64
D_ATTN = N_HEADS * HEAD_DIM
Q_BLOCK = 128

D_FF = 2816
N_EXPERTS = 8
TOP_K = 2
D_EXP = 3584

EPS = 1e-6

kernel_name = "yoco_rglru_fox_moe_hybrid"

def _rmsnorm(x, g):
    x32 = x.astype(jnp.float32)
    y = x32 * lax.rsqrt(jnp.mean(x32 * x32, axis=-1, keepdims=True) + EPS)
    return (y * g.astype(jnp.float32)).astype(x.dtype)

def _swiglu(xn, w_gu, w_down):
    gate, up = jnp.split(xn @ w_gu, 2, axis=-1)
    return (jax.nn.silu(gate) * up) @ w_down

def _lru_combine(left, right):
    a1, b1 = left
    a2, b2 = right
    return a1 * a2, a2 * b1 + b2

def _rg_lru_block(xn, w_in, conv_w, conv_b, gate_w, gate_b, lam, w_out):
    B, S, _ = xn.shape
    xb, gb = jnp.split(xn @ w_in, 2, axis=-1)
    xc = lax.conv_general_dilated(
        xb, conv_w[:, None, :], window_strides=(1,), padding=[(CONV_W - 1, 0)],
        dimension_numbers=('NWC', 'WIO', 'NWC'), feature_group_count=D_RNN) + conv_b
    xh = xc.reshape(B, S, N_LRU_BLOCKS, LRU_BW)
    gates = jnp.einsum('bsnd,gnde->gbsne', xh, gate_w).reshape(2, B, S, D_RNN) + gate_b[:, None, None, :]
    gates = gates.astype(jnp.float32)
    r = jax.nn.sigmoid(gates[0])
    i = jax.nn.sigmoid(gates[1])
    log_a = LRU_C * r * jax.nn.log_sigmoid(lam.astype(jnp.float32))
    a = jnp.exp(log_a)
    b = jnp.sqrt(-jnp.expm1(2.0 * log_a)) * (i * xc.astype(jnp.float32))
    _, h = lax.associative_scan(_lru_combine, (a, b), axis=1)
    y = jax.nn.gelu(gb) * h.astype(xn.dtype)
    return y @ w_out

def _shared_kv(x, kv_norm_g, w_kvf, b_f):
    B, S, _ = x.shape
    kvf = _rmsnorm(x, kv_norm_g) @ w_kvf
    k = kvf[..., :D_ATTN].reshape(B, S, N_HEADS, HEAD_DIM).transpose(0, 2, 1, 3)
    v = kvf[..., D_ATTN:2 * D_ATTN].reshape(B, S, N_HEADS, HEAD_DIM).transpose(0, 2, 1, 3)
    log_f = jax.nn.log_sigmoid((kvf[..., 2 * D_ATTN:] + b_f).astype(jnp.float32))
    cf = jnp.cumsum(log_f, axis=1).transpose(0, 2, 1)
    return k, v, cf

def _fox_attention(xn, w_qg, w_o, k, v, cf):
    B, S, _ = xn.shape
    q, g = jnp.split(xn @ w_qg, 2, axis=-1)
    q = q.reshape(B, S, N_HEADS, HEAD_DIM).transpose(0, 2, 1, 3) * (HEAD_DIM ** -0.5)
    k_pos = jnp.arange(S)

    def _block(blk):
        start = blk * Q_BLOCK
        qb = lax.dynamic_slice_in_dim(q, start, Q_BLOCK, axis=2)
        cq = lax.dynamic_slice_in_dim(cf, start, Q_BLOCK, axis=2)
        s = jnp.einsum('bhqd,bhkd->bhqk', qb, k).astype(jnp.float32)
        s = s + cq[..., :, None] - cf[..., None, :]
        q_pos = start + jnp.arange(Q_BLOCK)
        s = jnp.where(k_pos[None, :] <= q_pos[:, None], s, -jnp.inf)
        p = jax.nn.softmax(s, axis=-1)
        return jnp.einsum('bhqk,bhkd->bhqd', p.astype(v.dtype), v)

    o = lax.map(_block, jnp.arange(S // Q_BLOCK))
    o = o.transpose(1, 0, 3, 2, 4).reshape(B, S, D_ATTN)
    o = o * jax.nn.sigmoid(g)
    return o @ w_o

def _moe(xn, router, w_gu, w_down):
    logits = (xn @ router).astype(jnp.float32)
    top_v, top_i = lax.top_k(logits, TOP_K)
    w = jax.nn.softmax(top_v, axis=-1)
    gates = jnp.sum(w[..., None] * jax.nn.one_hot(top_i, N_EXPERTS, dtype=jnp.float32), axis=-2)
    y = jnp.zeros_like(xn)
    for e in range(N_EXPERTS):
        y = y + gates[..., e:e + 1].astype(xn.dtype) * _swiglu(xn, w_gu[e], w_down[e])
    return y

def setup_inputs(seed: int = 0) -> dict:
    key = jax.random.key(seed)
    ks = jax.random.split(key, 24)
    f32 = jnp.float32

    def nrm(k, shape, fan_in):
        return jax.random.normal(k, shape, f32) * (fan_in ** -0.5)

    x = jax.random.normal(ks[0], (BATCH, SEQ, D_MODEL), f32)
    norm_g = 1.0 + 0.02 * jax.random.normal(ks[1], (DEPTH, 2, D_MODEL), f32)
    lru_w_in = nrm(ks[2], (N_A_LAYERS, D_MODEL, 2 * D_RNN), D_MODEL)
    lru_conv_w = nrm(ks[3], (N_A_LAYERS, CONV_W, D_RNN), CONV_W)
    lru_conv_b = 0.02 * jax.random.normal(ks[4], (N_A_LAYERS, D_RNN), f32)
    lru_gate_w = nrm(ks[5], (N_A_LAYERS, 2, N_LRU_BLOCKS, LRU_BW, LRU_BW), LRU_BW)
    lru_gate_b = 0.1 * jax.random.normal(ks[6], (N_A_LAYERS, 2, D_RNN), f32)
    u = jax.random.uniform(ks[7], (N_A_LAYERS, D_RNN), f32, minval=0.9, maxval=0.999)
    s = u ** (1.0 / LRU_C)
    lru_lambda = jnp.log(s) - jnp.log1p(-s)
    lru_w_out = nrm(ks[8], (N_A_LAYERS, D_RNN, D_MODEL), D_RNN)
    kv_norm_g = 1.0 + 0.02 * jax.random.normal(ks[9], (D_MODEL,), f32)
    w_kvf = nrm(ks[10], (D_MODEL, 2 * D_ATTN + N_HEADS), D_MODEL)
    b_f = 3.0 + 0.5 * jax.random.normal(ks[11], (N_HEADS,), f32)
    fox_w_qg = nrm(ks[12], (N_B_LAYERS, D_MODEL, 2 * D_ATTN), D_MODEL)
    fox_w_o = nrm(ks[13], (N_B_LAYERS, D_ATTN, D_MODEL), D_ATTN)
    mlp_w_gu = nrm(ks[14], (N_DENSE, D_MODEL, 2 * D_FF), D_MODEL)
    mlp_w_down = nrm(ks[15], (N_DENSE, D_FF, D_MODEL), D_FF)
    moe_router = nrm(ks[16], (N_MOE, D_MODEL, N_EXPERTS), D_MODEL)
    moe_w_gu = nrm(ks[17], (N_MOE, N_EXPERTS, D_MODEL, 2 * D_EXP), D_MODEL)
    moe_w_down = nrm(ks[18], (N_MOE, N_EXPERTS, D_EXP, D_MODEL), D_EXP)
    final_norm_g = 1.0 + 0.02 * jax.random.normal(ks[19], (D_MODEL,), f32)
    return {"x": x, "norm_g": norm_g, "lru_w_in": lru_w_in, "lru_conv_w": lru_conv_w,
            "lru_conv_b": lru_conv_b, "lru_gate_w": lru_gate_w, "lru_gate_b": lru_gate_b,
            "lru_lambda": lru_lambda, "lru_w_out": lru_w_out, "kv_norm_g": kv_norm_g,
            "w_kvf": w_kvf, "b_f": b_f, "fox_w_qg": fox_w_qg, "fox_w_o": fox_w_o,
            "mlp_w_gu": mlp_w_gu, "mlp_w_down": mlp_w_down, "moe_router": moe_router,
            "moe_w_gu": moe_w_gu, "moe_w_down": moe_w_down, "final_norm_g": final_norm_g}

def reference(x, norm_g, lru_w_in, lru_conv_w, lru_conv_b, lru_gate_w, lru_gate_b, lru_lambda,
              lru_w_out, kv_norm_g, w_kvf, b_f, fox_w_qg, fox_w_o, mlp_w_gu, mlp_w_down,
              moe_router, moe_w_gu, moe_w_down, final_norm_g):
    k = v = cf = None
    for l in range(DEPTH):
        xn = _rmsnorm(x, norm_g[l, 0])
        if l < N_A_LAYERS:
            a = l
            x = x + _rg_lru_block(xn, lru_w_in[a], lru_conv_w[a], lru_conv_b[a], lru_gate_w[a],
                                  lru_gate_b[a], lru_lambda[a], lru_w_out[a])
        else:
            if l == N_A_LAYERS:
                k, v, cf = _shared_kv(_rmsnorm(x, 1.0) if False else x, kv_norm_g, w_kvf, b_f) if False else _shared_kv(x, kv_norm_g, w_kvf, b_f)
                xn = _rmsnorm(x, norm_g[l, 0])
            bi = l - N_A_LAYERS
            x = x + _fox_attention(xn, fox_w_qg[bi], fox_w_o[bi], k, v, cf)
        hn = _rmsnorm(x, norm_g[l, 1])
        if l % 2 == 0:
            x = x + _swiglu(hn, mlp_w_gu[l // 2], mlp_w_down[l // 2])
        else:
            x = x + _moe(hn, moe_router[l // 2], moe_w_gu[l // 2], moe_w_down[l // 2])
    return _rmsnorm(x, final_norm_g)


_drawn_inputs = setup_inputs


def setup_inputs(seed=0):
    import zlib

    import numpy as np

    out = dict(_drawn_inputs(seed))
    spreads = {}
    factors = {'kv_norm_g': 3.728, 'final_norm_g': 2.83}
    for name, (base, spread) in spreads.items():
        noise = np.random.default_rng([zlib.crc32(name.encode()), seed]).standard_normal(out[name].shape)
        drawn = base * np.exp(spread * noise) if base else spread * noise
        out[name] = __import__('jax').numpy.asarray(drawn.astype(out[name].dtype))
    for name, factor in factors.items():
        out[name] = (out[name] * factor).astype(out[name].dtype)
    return out
```

```python
from contextlib import ExitStack

import concourse.bass as bass
from concourse import mybir

P = 128
D = 1024
T = 256
NT = T // P
KD = D // P
NHEADS = 16
HD = D // NHEADS
D_FF = 2816
D_EXP = 3584
NE = 8
EPS = 1e-6
LRU_C = 8.0
CONV_W = 4
NEG = -1e30

UW = 2048
RAW = 6
SPL = 3
HALF = D // 2

U_XB, U_GB, U_OUT = 0, 4, 8
PAIRS = D_FF // (2 * P)
U_FF = 12
U_K = U_FF + 3 * PAIRS
U_V, U_Q, U_G, U_O = U_K + 4, U_K + 8, U_K + 12, U_K + 16
U_MOE = U_O + 4
CH = D_EXP // 512
JU = 6 * CH
J6 = JU // RAW

R_NORM, R_KVN, R_CB, R_CW, R_GB, R_LAM, R_END = 0, 32, 40, 48, 80, 96, 104
SLOT_COLS = 2 * NE + 1


def yoco_kernel(nc, x_in, norm_g, lru_w_in, lru_conv_w, lru_conv_b, lru_gate_w, lru_gate_b, lru_lambda,
                lru_w_out, kv_norm_g, w_kvf, b_f, fox_w_qg, fox_w_o, mlp_w_gu, mlp_w_down,
                moe_router, moe_w_gu, moe_w_down, final_norm_g, cf_dram, out):
    f32, f32r, bf16, i32 = mybir.dt.float32, mybir.dt.float32r, mybir.dt.bfloat16, mybir.dt.int32
    ALU, ACT, AX = mybir.AluOpType, mybir.ActivationFunctionType, mybir.AxisListType

    ctx = ExitStack()
    with ctx:
        def sb(name, shape, dt=f32, into=ctx):
            return into.enter_context(nc.sbuf_tensor(name, shape, dt))

        def sem(name):
            return ctx.enter_context(nc.semaphore(name))

        raw = sb("raw", [P, RAW, UW])
        w_hi = sb("w_hi", [P, SPL, UW], f32r)
        w_lo = sb("w_lo", [P, SPL, UW], f32r)
        act_hi = sb("act_hi", [P, KD, T], f32r)
        act_lo = sb("act_lo", [P, KD, T], f32r)
        alt_hi = sb("alt_hi", [P, KD, T], f32r)
        alt_lo = sb("alt_lo", [P, KD, T], f32r)
        x = sb("x", [P, NT, D])
        xs = sb("xs", [P, NT, D])
        ident = sb("ident", [P, P])
        ident_bf = sb("ident_bf", [P, P], bf16)
        ones = sb("ones", [P, P])
        upto = sb("upto", [P, P])
        before = sb("before", [P, P])
        maskf = sb("maskf", [P, P])
        mask_bf = sb("mask_bf", [P, P], bf16)
        iota = sb("iota", [P, P])
        rows = sb("rows", [P, P])
        cols = sb("cols", [P, R_END])
        wf_raw = sb("wf_raw", [P, KD, NHEADS])
        wf_hi = sb("wf_hi", [P, KD, NHEADS], f32r)
        wf_lo = sb("wf_lo", [P, KD, NHEADS], f32r)
        rt_raw = sb("rt_raw", [P, KD, NE])
        rt_hi = sb("rt_hi", [P, KD, NE], f32r)
        rt_lo = sb("rt_lo", [P, KD, NE], f32r)
        bf_bc = sb("bf_bc", [P, NHEADS])
        ss = sb("ss", [P, 5, NT])
        msq = sb("msq", [P, 5, NT])
        rstd = sb("rstd", [P, 5, NT])
        neghalf = sb("neghalf", [P, NT])
        lam_s = sb("lam_s", [P, 8, KD])
        m4ls = sb("m4ls", [P, KD])
        f_s = sb("f_s", [P, 9, NT * NHEADS])
        c_t = sb("c_t", [P, NT, NHEADS])
        c_T = sb("c_T", [NHEADS, T])
        negmax = sb("negmax", [P, 2, NT])
        psums = sb("psums", [P, 2, NT])
        pinv = sb("pinv", [P, 2, NT])
        route = sb("route", [P, 12, NT, NE])
        top8 = sb("top8", [P, NT, 8])
        rcol = sb("rcol", [P, 8, NT])
        slot_of = sb("slot_of", [P, NT, SLOT_COLS])
        gate_of = sb("gate_of", [P, NT, SLOT_COLS])
        njobs_f = sb("njobs_f", [P, 2])
        njobs = sb("njobs", [P, 1], i32)
        gslot = sb("gslot", [P, 1])

        with ExitStack() as lru:
            xb_pad = sb("xb_pad", [P, KD, T + CONV_W - 1], f32, lru)
            xc = sb("xc", [P, KD, T], f32, lru)
            rc = sb("rc", [P, KD, T], f32, lru)
            gelu = sb("gelu", [P, KD, T], f32, lru)
            gate_w = sb("gate_w", [P, 2 * KD, P], f32, lru)
            i_sb = sb("i_sb", [P, 2, 2, T], f32, lru)
        th = xs[:, :, :].rearrange("p t d -> p (t d)").rearrange("p (c n) -> p c n", c=KD)
        with ExitStack() as att:
            k_T = sb("k_T", [P, KD, T], f32, att)
            q_T = sb("q_T", [P, KD, T], f32, att)
            v_sb = sb("v_sb", [P, NT, D], f32, att)
            c_bc = sb("c_bc", [P, NHEADS, T], f32, att)
            prob = sb("prob", [P, 2, 3 * P], f32, att)
            prob_T = sb("prob_T", [P, 2, 3 * P], f32, att)
        tg = th
        with ExitStack() as ffn:
            hid_hi = sb("hid_hi", [P, 2, 512], f32r, ffn)
            hid_lo = sb("hid_lo", [P, 2, 512], f32r, ffn)
            silu = sb("silu", [P, 512], f32, ffn)
            hid = sb("hid", [P, 512], f32, ffn)
            y_hi = sb("y_hi", [P, D], f32r, ffn)
            y_lo = sb("y_lo", [P, D], f32r, ffn)
            sel = sb("sel", [P, NT, P], f32r, ffn)
            sel_g = sb("sel_g", [P, NT, P], f32, ffn)
            sel_T = sb("sel_T", [P, T], f32r, ffn)
            gfin_bc = sb("gfin_bc", [P, D], f32, ffn)

        bank = [ctx.enter_context(nc.psum_tensor(f"bank{i}", [P, 512], f32)) for i in range(8)]

        raw_full = [sem(f"raw_full{i}") for i in range(RAW)]
        hi_done, lo_done, unit_used = sem("hi_done"), sem("lo_done"), sem("unit_used")
        x_loaded, rows_loaded, bcast_loaded, gatew_loaded = (sem(n) for n in ("x_loaded", "rows_loaded", "bcast_loaded", "gatew_loaded"))
        smallw_loaded, cf_stored, cbc_loaded, gfin_loaded, stored = (sem(n) for n in ("smallw_loaded", "cf_stored", "cbc_loaded", "gfin_loaded", "stored"))
        blank, consts, consts_v = sem("blank"), sem("consts"), sem("consts_v")
        rows_T, cols_ready = sem("rows_T"), sem("cols_ready")
        small_hi, small_lo = sem("small_hi"), sem("small_lo")
        lam_abs, lam_exp, lam_ready = sem("lam_abs"), sem("lam_exp"), sem("lam_ready")
        sq_act, sq_dve, msq_ready, rstd_ready, xs_ready = (sem(n) for n in ("sq_act", "sq_dve", "msq_ready", "rstd_ready", "xs_ready"))
        norm_T, act_hi_done, act_lo_done = sem("norm_T"), sem("act_hi_done"), sem("act_lo_done")
        link_v = sem("link_v")
        pad_ready, xb_ready, xc_ready, gates_done = (sem(n) for n in ("pad_ready", "xb_ready", "xc_ready", "gates_done"))
        sig_done, tanh_done, bx_done, sqrt_done, gelu_done = (sem(n) for n in ("sig_done", "tanh_done", "bx_done", "sqrt_done", "gelu_done"))
        yl_ready, alt_hi_done, alt_lo_done, x_added = (sem(n) for n in ("yl_ready", "alt_hi_done", "alt_lo_done", "x_added"))
        silu_done, h_done, hid_hi_done, hid_lo_done = (sem(n) for n in ("silu_done", "h_done", "hid_hi_done", "hid_lo_done"))
        f_done, f_abs, f_exp, logf_ready, cf_done, cT_ready = (sem(n) for n in ("f_done", "f_abs", "f_exp", "logf_ready", "cf_done", "cT_ready"))
        k_ready, v_ready, q_ready, tg_ready = (sem(n) for n in ("k_ready", "v_ready", "q_ready", "tg_ready"))
        s_done, s_ready, p_exp, p_norm, pt_done, pt_ready, pv_done, o_ready = (sem(n) for n in ("s_done", "s_ready", "p_exp", "p_norm", "pt_done", "pt_ready", "pv_done", "o_ready"))
        logits_done, v1_ready, e_ready, mask_ready, rank_done, njobs_ready = (sem(n) for n in ("logits_done", "v1_ready", "e_ready", "mask_ready", "rank_done", "njobs_ready"))
        xs_hi_done, src_ready, moe_blank = sem("xs_hi_done"), sem("src_ready"), sem("moe_blank")
        sel_built, gathered, tok_hi_done, tok_lo_done = (sem(n) for n in ("sel_built", "gathered", "tok_hi_done", "tok_lo_done"))
        selg_T, selT_ready, yhi_done, ylo_done, scattered, moe_added = (sem(n) for n in ("selg_T", "selT_ready", "yhi_done", "ylo_done", "scattered", "moe_added"))
        e_silu, e_h, e_T, e_hid_hi, e_hid_lo = (sem(n) for n in ("e_silu", "e_h", "e_T", "e_hid_hi", "e_hid_lo"))
        out_ready = sem("out_ready")

        def cols256(w, c):
            return w.rearrange("(k p) n -> p k n", p=P)[:, :, bass.ds(c * 256, 256)]

        def square(w, col_half, k_half):
            return w.rearrange("(k p) n -> p k n", p=P)[:, 4 * k_half:4 * k_half + 4, HALF * col_half:HALF * col_half + HALF]

        w_in, w_out, w_gu, w_dn = lru_w_in[0], lru_w_out[0], mlp_w_gu[0], mlp_w_down[0]
        w_qg, w_o = fox_w_qg[0], fox_w_o[0]
        dn_v = w_dn.rearrange("(k p) n -> p k n", p=P)
        e_gu = moe_w_gu[0].rearrange("e (k p) n -> e p k n", p=P)
        e_dn = moe_w_down[0].rearrange("e (k p) n -> e p k n", p=P)

        def raw_count(u, n):
            return 16 * (u // RAW + 1 + n)

        def units(u, n=0):
            return u + RAW * n

        block = ctx.enter_context(nc.Block())

        @block.sync
        def _(sp):
            def load(u, n, width, src):
                if not (isinstance(n, int) and u + RAW * n < RAW):
                    sp.wait_ge(lo_done, units(u, n) - RAW + 1)
                dst = raw[:, u % RAW, :].rearrange("p (k n) -> p k n", n=width)
                sp.dma_start(dst, src).then_inc(raw_full[u % RAW], 16)

            for c in range(8):
                load(U_XB + c, 0, 256, cols256(w_in, c))
            for c in range(4):
                load(U_OUT + c, 0, HALF, square(w_out, c // 2, c % 2))
            load(U_FF, 0, 256, cols256(w_gu, 0))
            load(U_FF + 1, 0, 256, cols256(w_gu, PAIRS))
            with sp.Fori(0, (PAIRS - 1) // 2) as i:
                for m in range(2):
                    u = U_FF + 2 + 3 * m
                    load(u, i, 256, cols256(w_gu, 2 * i + 1 + m))
                    load(u + 1, i, 256, cols256(w_gu, 2 * i + 1 + m + PAIRS))
                    load(u + 2, i, D, dn_v[:, bass.ds(4 * i + 2 * m, 2), :])
            load(U_K - 1, 0, D, dn_v[:, 2 * PAIRS - 2:2 * PAIRS, :])
            for c in range(4):
                load(U_K + c, 0, 256, cols256(w_kvf, c))
            for c in range(4):
                load(U_V + c, 0, HALF, square(w_kvf[:, D:2 * D], c // 2, c % 2))
            for c in range(8):
                load(U_Q + c, 0, 256, cols256(w_qg, c))
            for c in range(4):
                load(U_O + c, 0, HALF, square(w_o, c // 2, c % 2))

            def expert_unit(e, k):
                c, part = (0, k // 2) if k < 4 else ((k - 4) // 6 + 1, (k - 4) % 6 // 2)
                if k >= JU - 2:
                    c, part = CH, 2
                half = k % 2
                if part < 2:
                    lo = part * D_EXP + 512 * c
                    return e_gu[e][:, 4 * half:4 * half + 4, lo:lo + 512], 512
                lo = 4 * (c - 1) + 2 * half
                return e_dn[e][:, lo:lo + 2, :], D

            def expert(j, e, first, last):
                for k in range(first, last):
                    src, width = expert_unit(e, k)
                    load(U_MOE + k, J6 * j, width, src)

            with sp.Fori(0, NE) as j:
                expert(j, j, 0, JU)
            expert(NE, 0, 0, SPL)
            sp.wait_ge(njobs_ready, 1)
            jobs = sp.value_load(njobs[0:1, 0:1], min_val=NE, max_val=2 * NE)
            with sp.If(jobs > NE):
                with sp.Fori(NE, 2 * NE - 1) as j:
                    expert(j, j - NE, SPL, JU)
                    expert(j + 1, j - NE + 1, 0, SPL)
                expert(2 * NE - 1, NE - 1, SPL, JU)
                expert(2 * NE, 0, 0, SPL)
            sp.wait_ge(out_ready, NT)
            sp.dma_start(out[0].rearrange("(t p) d -> p t d", p=P), xs[:, :, :]).then_inc(stored, 16)
            sp.wait_ge(stored, 16)

        @block.gpsimd
        def _(pool):
            g = nc.gpsimd
            for row, src in ((R_NORM, norm_g.rearrange("l s (c p) -> (l s c) p", p=P)),
                             (R_KVN, kv_norm_g.rearrange("(c p) -> c p", p=P)),
                             (R_CB, lru_conv_b[0].rearrange("(c p) -> c p", p=P)),
                             (R_CW, lru_conv_w[0].rearrange("w (c p) -> (w c) p", p=P)),
                             (R_GB, lru_gate_b[0].rearrange("g (c p) -> (g c) p", p=P)),
                             (R_LAM, lru_lambda[0].rearrange("(c p) -> c p", p=P))):
                pool.dma_start(rows[row:row + src.shape[0], :], src).then_inc(rows_loaded, 16)
            g.memset(ident[:], 0.0).then_inc(blank, 1)
            g.memset(ones[:], 1.0).then_inc(blank, 1)
            g.memset(maskf[:], 0.0).then_inc(blank, 1)
            g.memset(neghalf[:], -0.5).then_inc(blank, 1)
            g.memset(xb_pad[:, :, 0:CONV_W - 1], 0.0).then_inc(pad_ready, 1)
            g.iota(iota[:], [[1, P]], base=0, channel_multiplier=0,
                   allow_small_or_imprecise_dtypes=True).then_inc(consts, 1)
            pool.wait_ge(blank, 4)
            g.affine_select(out=ident[:], in_=ident[:], compare_op=ALU.not_equal, fill=1.0, base=0,
                            pattern=[[-1, P]], channel_multiplier=1).then_inc(consts, 1)
            g.affine_select(out=upto[:], in_=ones[:], compare_op=ALU.is_ge, fill=0.0, base=0,
                            pattern=[[1, P]], channel_multiplier=-1).then_inc(consts, 1)
            g.affine_select(out=before[:], in_=ones[:], compare_op=ALU.is_ge, fill=0.0, base=-1,
                            pattern=[[1, P]], channel_multiplier=-1).then_inc(consts, 1)
            g.affine_select(out=maskf[:], in_=maskf[:], compare_op=ALU.is_ge, fill=NEG, base=0,
                            pattern=[[-1, P]], channel_multiplier=1).then_inc(consts, 1)

            def norm_scale(n):
                pool.wait_ge(sq_act, n + 1)
                pool.wait_ge(sq_dve, n + 1)
                g.tensor_scalar(msq[:, n, :], ss[:, n, :], 1.0 / D, EPS, ALU.mult, ALU.add).then_inc(msq_ready, 1)
                pool.wait_ge(msq_ready, n + 1)
                g.tensor_tensor(rstd[:, n, :], msq[:, n, :], neghalf[:], ALU.pow).then_inc(rstd_ready, 1)

            norm_scale(0)
            for j in range(KD // 2):
                pool.wait_ge(sig_done, 4 * (j + 1))
                part = xc[:, 2 * j:2 * j + 2, :]
                g.tensor_tensor(part, i_sb[:, j % 2, :, :], part, ALU.mult).then_inc(bx_done, 1)
            norm_scale(1)
            norm_scale(2)
            pool.wait_ge(cT_ready, 2)
            pool.dma_start(cf_dram, c_T[:]).then_inc(cf_stored, 16)
            pool.wait_ge(cf_stored, 16)
            pool.dma_start(c_bc[:].rearrange("p h t -> p (h t)"),
                           cf_dram.rearrange("h t -> (h t)").partition_broadcast(P)).then_inc(cbc_loaded, 16)
            norm_scale(3)
            pool.dma_start(gfin_bc[:], final_norm_g.partition_broadcast(P)).then_inc(gfin_loaded, 16)
            norm_scale(4)

        @block.scalar
        def _(act):
            a = nc.scalar
            act.dma_start(x[:, 0, :], x_in[0, 0:P, :]).then_inc(x_loaded, 16)
            act.dma_start(x[:, 1, :], x_in[0, P:T, :]).then_inc(x_loaded, 16)
            act.dma_start(gate_w[:, :, :], lru_gate_w[0].rearrange("g n d e -> d (g n) e")).then_inc(gatew_loaded, 16)
            act.dma_start(wf_raw[:], w_kvf.rearrange("(k p) n -> p k n", p=P)[:, :, 2 * D:]).then_inc(smallw_loaded, 16)
            act.dma_start(rt_raw[:], moe_router[0].rearrange("(k p) n -> p k n", p=P)).then_inc(smallw_loaded, 16)
            act.dma_start(bf_bc[:], b_f.partition_broadcast(P)).then_inc(bcast_loaded, 16)

            def split_hi(u, n=0):
                act.wait_ge(raw_full[u % RAW], raw_count(u, n))
                if not (isinstance(n, int) and u + RAW * n < SPL):
                    act.wait_ge(unit_used, units(u, n) - SPL + 1)
                a.activation(w_hi[:, u % SPL, :], raw[:, u % RAW, :], ACT.Copy).then_inc(hi_done, 1)

            def squares(n):
                a.activation(xs[:, 0, :], x[:, 0, :], ACT.Square, accum_out=ss[:, n, 0:1]).then_inc(sq_act, 1)

            def norm_hi(m, gain, hi, lo_before=None):
                for c in range(KD):
                    if lo_before is not None:
                        if c % 2 == 0:
                            act.wait_ge(act_lo_done, lo_before + c + 2)
                    elif c % 2 == 0:
                        act.wait_ge(norm_T, 4 * m + c // 2 + 1)
                    a.activation(hi[:, c, :], bank[c // 2][:, (c % 2) * T:(c % 2 + 1) * T], ACT.Copy,
                                 scale=cols[:, gain + c:gain + c + 1]).then_inc(act_hi_done, 1)

            act.wait_ge(x_loaded, 32)
            squares(0)
            act.wait_ge(lam_abs, 1)
            a.activation(lam_s[:, 1, :], lam_s[:, 0, :], ACT.Exp, scale=-1.0).then_inc(lam_exp, 1)
            for u in range(SPL):
                split_hi(u)
            act.wait_ge(smallw_loaded, 32)
            a.activation(wf_hi[:], wf_raw[:], ACT.Copy).then_inc(small_hi, 1)
            a.activation(rt_hi[:], rt_raw[:], ACT.Copy).then_inc(small_hi, 1)
            act.wait_ge(cols_ready, 1)
            norm_hi(0, R_NORM, act_hi)

            act.wait_ge(lam_ready, 1)
            for k in range(U_FF):
                if 1 <= k <= 4:
                    act.wait_ge(unit_used, k)
                    a.activation(xb_pad[:, 2 * k - 2:2 * k, CONV_W - 1:], bank[4 + (k - 1) % 4][:].rearrange("p (c n) -> p c n", c=2),
                                 ACT.Copy).then_inc(xb_ready, 1)
                if 3 <= k <= 6:
                    j = k - 3
                    for c in (2 * j, 2 * j + 1):
                        act.wait_ge(gates_done, c + 1)
                        if j >= 2:
                            act.wait_ge(bx_done, j - 1)
                        a.activation(th[:, c, :], bank[c % 4][:, 0:T], ACT.Sigmoid,
                                     bias=cols[:, R_GB + c:R_GB + c + 1]).then_inc(sig_done, 1)
                        a.activation(i_sb[:, j % 2, c % 2, :], bank[c % 4][:, T:2 * T], ACT.Sigmoid,
                                     bias=cols[:, R_GB + KD + c:R_GB + KD + c + 1]).then_inc(sig_done, 1)
                    for c in (2 * j, 2 * j + 1):
                        act.wait_ge(sig_done, 2 * c + 1)
                        a.activation(th[:, c, :], th[:, c, :], ACT.Tanh, scale=m4ls[:, c:c + 1]).then_inc(tanh_done, 1)
                if k == 7:
                    act.wait_ge(tanh_done, KD)
                    act.wait_ge(yl_ready, 1)
                    a.activation(th[:, :, :], th[:, :, :], ACT.Sqrt).then_inc(sqrt_done, 1)
                if k == 8:
                    for c in range(4):
                        act.wait_ge(unit_used, U_GB + c + 1)
                        a.activation(gelu[:, 2 * c:2 * c + 2, :], bank[4 + c][:].rearrange("p (c n) -> p c n", c=2),
                                     ACT.Gelu_apprx_tanh).then_inc(gelu_done, 1)
                    for h in range(2):
                        act.wait_ge(yl_ready, 2 + h)
                        a.activation(alt_hi[:, 4 * h:4 * h + 4, :], gelu[:, 4 * h:4 * h + 4, :], ACT.Copy).then_inc(alt_hi_done, 1)
                split_hi(k + SPL)

            act.wait_ge(x_added, 4)
            squares(1)
            norm_hi(1, R_NORM + KD, act_hi)
            split_hi(U_FF + SPL)

            def ff_silu(u_gate, n, p, m):
                act.wait_ge(unit_used, units(u_gate, n) + 1)
                if not (isinstance(p, int) and p == 0):
                    act.wait_ge(h_done, p)
                a.activation(silu[:], bank[4 + 2 * (m % 2)][:], ACT.Silu).then_inc(silu_done, 1)

            def ff_hid(p, m):
                act.wait_ge(h_done, p + 1)
                a.activation(hid_hi[:, m % 2, :], hid[:], ACT.Copy).then_inc(hid_hi_done, 1)

            ff_silu(U_FF, 0, 0, 0)
            split_hi(U_FF + 1 + SPL)
            ff_hid(0, 0)
            split_hi(U_FF + 2 + SPL)
            with act.Fori(0, (PAIRS - 1) // 2) as i:
                for m in (1, 2):
                    u = U_FF + 3 * m - 1
                    p = 2 * i + m
                    ff_silu(u, i, p, m)
                    split_hi(u + 1 + SPL, i)
                    act.wait_ge(unit_used, units(u, i))
                    ff_hid(p, m)
                    split_hi(u + 2 + SPL, i)
                    split_hi(u + 3 + SPL, i)

            act.wait_ge(x_added, 8)
            squares(2)
            norm_hi(2, R_KVN, alt_hi)
            norm_hi(2, R_NORM + 2 * KD, act_hi, 2 * KD)
            act.wait_ge(f_abs, 1)
            a.activation(f_s[:, 2, :], f_s[:, 1, :], ACT.Exp, scale=-1.0).then_inc(f_exp, 1)
            split_hi(U_K + SPL)
            for k in range(1, 16):
                if 1 <= k <= 4:
                    act.wait_ge(unit_used, U_K + k)
                    a.activation(k_T[:, 2 * k - 2:2 * k, :], bank[4 + (k - 1) % 2][:].rearrange("p (c n) -> p c n", c=2),
                                 ACT.Copy).then_inc(k_ready, 1)
                if k in (6, 8):
                    half = (k - 6) // 2
                    act.wait_ge(unit_used, U_K + k)
                    for t in range(NT):
                        a.activation(v_sb[:, t, HALF * half:HALF * half + HALF], bank[2 * half + t][:], ACT.Copy).then_inc(v_ready, 1)
                if 9 <= k <= 12:
                    act.wait_ge(unit_used, U_K + k)
                    a.activation(q_T[:, 2 * (k - 9):2 * (k - 9) + 2, :], bank[4 + (k - 9) % 2][:].rearrange("p (c n) -> p c n", c=2),
                                 ACT.Copy, scale=HD ** -0.5).then_inc(q_ready, 1)
                if k < 12:
                    split_hi(U_K + k + SPL)
            for i in range(NHEADS + 3):
                if i < NHEADS:
                    act.wait_ge(s_ready, i + 1)
                    for t in range(NT):
                        part = prob[:, i % 2, 0:P] if t == 0 else prob[:, i % 2, P:3 * P]
                        a.activation(part, part, ACT.Exp, bias=negmax[:, i % 2, t:t + 1],
                                     accum_out=psums[:, i % 2, t:t + 1]).then_inc(p_exp, 1)
                if 1 <= i <= NHEADS:
                    act.wait_ge(pt_done, i)
                    if i >= 3:
                        act.wait_ge(pv_done, i - 2)
                    a.activation(prob_T[:, (i - 1) % 2, :], bank[2 + (i - 1) % 2][:, 0:3 * P], ACT.Copy).then_inc(pt_ready, 1)
                if i % 4 == 2 and i // 4 < 4:
                    c = i // 4
                    act.wait_ge(unit_used, U_G + c + 1)
                    a.activation(tg[:, 2 * c:2 * c + 2, :], bank[6 + c % 2][:].rearrange("p (c n) -> p c n", c=2),
                                 ACT.Tanh, scale=0.5).then_inc(tg_ready, 1)
                    split_hi(U_G + c + SPL)
                if i >= 4 and i % 2 == 0:
                    hp = (i - 4) // 2
                    act.wait_ge(o_ready, hp + 1)
                    a.activation(alt_hi[:, hp, :], q_T[:, hp, :], ACT.Copy, scale=0.5).then_inc(alt_hi_done, 1)
            for k in range(4):
                split_hi(U_O + k + SPL)

            act.wait_ge(x_added, 12)
            squares(3)
            norm_hi(3, R_NORM + 3 * KD, act_hi)
            act.wait_ge(xs_ready, 2 * 3 + 2)
            a.activation(alt_hi[:].rearrange("p c n -> p (c n)"), xs[:].rearrange("p t d -> p (t d)"), ACT.Copy).then_inc(xs_hi_done, 1)
            for t in range(NT):
                act.wait_ge(v1_ready, t + 1)
                a.activation(route[:, 5, t, :], route[:, 0, t, :], ACT.Exp, bias=rcol[:, 0, t:t + 1]).then_inc(e_ready, 1)

            def tokens_hi(j):
                act.wait_ge(gathered, j + 1)
                for c in range(KD):
                    a.activation(act_hi[:, c // 2, (c % 2) * P:(c % 2 + 1) * P], bank[6 + c // 4][:, (c % 4) * P:(c % 4 + 1) * P],
                                 ACT.Copy, scale=cols[:, R_NORM + 3 * KD + c:R_NORM + 3 * KD + c + 1]).then_inc(tok_hi_done, 1)

            def y_hi_part(j):
                act.wait_ge(unit_used, U_MOE + JU * j)
                act.wait_ge(selT_ready, j + 1)
                for half in range(2):
                    a.activation(y_hi[:, HALF * half:HALF * half + HALF], bank[half][:], ACT.Copy, scale=gslot[:, 0:1]).then_inc(yhi_done, 1)

            tokens_hi(0)
            act.wait_ge(moe_blank, 2)
            act.wait_ge(njobs_ready, 1)
            jobs = act.value_load(njobs[0:1, 0:1], min_val=NE, max_val=2 * NE)
            with act.Fori(0, jobs) as j:
                for k in range(JU):
                    c = (k - 2) // 6 if k >= 2 else 0
                    if k == 0:
                        y_hi_part(j)
                    if k == 2 or (k >= 6 and k % 6 == 0 and k // 6 < CH):
                        c = k // 6
                        act.wait_ge(unit_used, U_MOE + JU * j + k)
                        if c:
                            act.wait_ge(e_h, CH * j + c)
                        a.activation(silu[:], bank[2][:], ACT.Silu).then_inc(e_silu, 1)
                    if (k >= 6 and k % 6 == 0) or k == JU - 3:
                        c = k // 6 - 1 if k < JU - 3 else CH - 1
                        act.wait_ge(e_T, CH * j + c + 1)
                        a.activation(hid_hi[:, c % 2, :], bank[4 + c % 2][:], ACT.Copy).then_inc(e_hid_hi, 1)
                    if k == JU - 2:
                        tokens_hi(j + 1)
                    split_hi(U_MOE + k + SPL, J6 * j)
            y_hi_part(jobs)
            act.wait_ge(moe_added, 4 * jobs + 4)
            squares(4)

        @block.vector
        def _(dve):
            v = nc.vector
            chain = [0]

            def link(ins):
                chain[0] += 1
                ins.then_inc(link_v, 1)
                dve.wait_ge(link_v, chain[0])

            def split_lo(u, n=0):
                dve.wait_ge(hi_done, units(u, n) + 1)
                v.tensor_tensor(w_lo[:, u % SPL, :], raw[:, u % RAW, :], w_hi[:, u % SPL, :].bitcast(f32),
                                ALU.subtract).then_inc(lo_done, 1)

            def squares(n):
                v.tensor_tensor_reduce(out=xs[:, 1, :], in0=x[:, 1, :], in1=x[:, 1, :], scale=1.0, scalar=0.0,
                                       op0=ALU.mult, op1=ALU.add, accum_out=ss[:, n, 1:2]).then_inc(sq_dve, 1)

            def scale_x(n):
                dve.wait_ge(rstd_ready, n + 1)
                for t in range(NT):
                    v.tensor_scalar(xs[:, t, :], x[:, t, :], rstd[:, n, t:t + 1], None, ALU.mult).then_inc(xs_ready, 1)

            def norm_lo(i, gain, hi, lo):
                for c in range(KD):
                    if c % 2 == 0:
                        dve.wait_ge(act_hi_done, KD * i + c + 2)
                    v.scalar_tensor_tensor(out=lo[:, c, :], in0=bank[c // 2][:, (c % 2) * T:(c % 2 + 1) * T],
                                           scalar=cols[:, gain + c:gain + c + 1], in1=hi[:, c, :].bitcast(f32),
                                           op0=ALU.mult, op1=ALU.subtract).then_inc(act_lo_done, 1)

            def log1p_terms(s, z_min, out_scale, out):
                link(v.tensor_scalar(s(3), s(2), 2.0, None, ALU.add))
                link(v.reciprocal(s(4), s(3)))
                link(v.tensor_tensor(s(3), s(2), s(4), ALU.mult))
                link(v.tensor_tensor(s(4), s(3), s(3), ALU.mult))
                link(v.tensor_scalar(s(5), s(4), 1.0 / 15, None, ALU.mult))
                for n in (13, 11, 9, 7, 5, 3):
                    link(v.scalar_tensor_tensor(out=s(5), in0=s(5), scalar=1.0 / n, in1=s(4), op0=ALU.add, op1=ALU.mult))
                link(v.scalar_tensor_tensor(out=s(5), in0=s(5), scalar=1.0, in1=s(3), op0=ALU.add, op1=ALU.mult))
                link(v.scalar_tensor_tensor(out=s(5), in0=s(5), scalar=-2.0, in1=z_min, op0=ALU.mult, op1=ALU.add))
                return v.tensor_scalar(out, s(5), out_scale, None, ALU.mult)

            def add_to_x(count_sem, banks, halves=(0, 1)):
                for half in halves:
                    for t in range(NT):
                        part = x[:, t, HALF * half:HALF * half + HALF]
                        v.tensor_tensor(part, part, banks(t, half), ALU.add).then_inc(count_sem, 1)

            dve.wait_ge(x_loaded, 32)
            squares(0)
            dve.wait_ge(consts, 5)
            v.tensor_copy(ident_bf[:], ident[:]).then_inc(consts_v, 1)
            v.tensor_copy(mask_bf[:], maskf[:]).then_inc(consts_v, 1)
            dve.wait_ge(rows_T, 1)
            link(v.tensor_copy(cols[:], bank[7][:, 0:R_END]))
            lam = cols[:, R_LAM:R_LAM + KD]
            v.scalar_tensor_tensor(out=lam_s[:, 0, :], in0=lam, scalar=-1.0, in1=lam, op0=ALU.mult,
                                   op1=ALU.max).then_inc(lam_abs, 1)
            v.tensor_scalar(lam_s[:, 6, :], lam, 0.0, None, ALU.min).then_inc(cols_ready, 1)
            scale_x(0)
            dve.wait_ge(lam_exp, 1)
            log1p_terms(lambda n: {2: lam_s[:, 1, :]}.get(n, lam_s[:, n - 1, :]), lam_s[:, 6, :],
                        -LRU_C / 2, m4ls[:]).then_inc(lam_ready, 1)
            for u in range(SPL):
                split_lo(u)
            norm_lo(0, R_NORM, act_hi, act_lo)
            dve.wait_ge(small_hi, 2)
            v.tensor_tensor(wf_lo[:], wf_raw[:], wf_hi[:].bitcast(f32), ALU.subtract).then_inc(small_lo, 1)
            v.tensor_tensor(rt_lo[:], rt_raw[:], rt_hi[:].bitcast(f32), ALU.subtract).then_inc(small_lo, 1)

            dve.wait_ge(pad_ready, 1)
            for k in range(U_FF):
                if 1 <= k <= 4:
                    dve.wait_ge(xb_ready, k)
                    for c in (2 * k - 2, 2 * k - 1):
                        def tap(w):
                            return cols[:, R_CW + KD * w + c:R_CW + KD * w + c + 1]
                        link(v.tensor_scalar(xc[:, c, :], xb_pad[:, c, 0:T], tap(0), cols[:, R_CB + c:R_CB + c + 1], ALU.mult, ALU.add))
                        for w in range(1, CONV_W):
                            last = v.scalar_tensor_tensor(out=xc[:, c, :], in0=xb_pad[:, c, w:w + T], scalar=tap(w),
                                                          in1=xc[:, c, :], op0=ALU.mult, op1=ALU.add)
                            if w < CONV_W - 1:
                                link(last)
                        last.then_inc(xc_ready, 1)
                if 3 <= k <= 6:
                    j = k - 3
                    pair = slice(2 * j, 2 * j + 2)
                    dve.wait_ge(tanh_done, 2 * j + 2)
                    link(v.tensor_scalar(rc[:, pair, :], th[:, pair, :], 1.0, None, ALU.add))
                    link(v.reciprocal(rc[:, pair, :], rc[:, pair, :]))
                    last = v.tensor_scalar(xb_pad[:, pair, 0:T], rc[:, pair, :], 2.0, -1.0, ALU.mult, ALU.add)
                    if k == 6:
                        last.then_inc(yl_ready, 1)
                if k == 8:
                    dve.wait_ge(sqrt_done, 1)
                    dve.wait_ge(yl_ready, 1)
                    for h in range(2):
                        part = slice(4 * h, 4 * h + 4)
                        dve.wait_ge(bx_done, 2 * h + 2)
                        link(v.scalar_tensor_tensor(out=rc[:, part, :], in0=th[:, part, :], scalar=2.0, in1=rc[:, part, :],
                                                    op0=ALU.mult, op1=ALU.mult))
                        link(v.tensor_tensor(xc[:, part, :], rc[:, part, :], xc[:, part, :], ALU.mult))
                        for c in range(4 * h, 4 * h + 4):
                            last = v.tensor_tensor_scan(rc[:, c, :], xb_pad[:, c, 0:T], xc[:, c, :], 0.0, ALU.mult, ALU.add)
                            if c % 4 == 3:
                                link(last)
                        dve.wait_ge(gelu_done, 2 * h + 2)
                        v.tensor_tensor(gelu[:, part, :], gelu[:, part, :], rc[:, part, :], ALU.mult).then_inc(yl_ready, 1)
                        dve.wait_ge(alt_hi_done, h + 1)
                        v.tensor_tensor(alt_lo[:, part, :], gelu[:, part, :], alt_hi[:, part, :].bitcast(f32), ALU.subtract).then_inc(alt_lo_done, 1)
                if k == 10:
                    dve.wait_ge(unit_used, U_OUT + 2)
                    add_to_x(x_added, lambda t, half: bank[2 * half + t][:], (0,))
                split_lo(k + SPL)
            dve.wait_ge(unit_used, U_OUT + 4)
            add_to_x(x_added, lambda t, half: bank[2 * half + t][:], (1,))

            dve.wait_ge(x_added, 4)
            squares(1)
            scale_x(1)
            norm_lo(1, R_NORM + KD, act_hi, act_lo)
            split_lo(U_FF + SPL)
            split_lo(U_FF + 1 + SPL)

            def ff_hid(u_up, n, p, m):
                dve.wait_ge(silu_done, p + 1)
                dve.wait_ge(unit_used, units(u_up, n) + 1)
                if not (isinstance(p, int) and p == 0):
                    dve.wait_ge(hid_lo_done, p)
                v.tensor_tensor(hid[:], silu[:], bank[5 + 2 * (m % 2)][:], ALU.mult).then_inc(h_done, 1)
                dve.wait_ge(hid_hi_done, p + 1)
                v.tensor_tensor(hid_lo[:, m % 2, :], hid[:], hid_hi[:, m % 2, :].bitcast(f32), ALU.subtract).then_inc(hid_lo_done, 1)

            ff_hid(U_FF + 1, 0, 0, 0)
            split_lo(U_FF + 2 + SPL)
            with dve.Fori(0, (PAIRS - 1) // 2) as i:
                for m in (1, 2):
                    u = U_FF + 3 * m - 1
                    split_lo(u + 1 + SPL, i)
                    ff_hid(u + 1, i, 2 * i + m, m)
                    split_lo(u + 2 + SPL, i)
                    split_lo(u + 3 + SPL, i)
            dve.wait_ge(unit_used, U_K)
            add_to_x(x_added, lambda t, half: bank[2 * half + t][:])

            dve.wait_ge(x_added, 8)
            squares(2)
            scale_x(2)
            norm_lo(2, R_KVN, alt_hi, alt_lo)
            norm_lo(3, R_NORM + 2 * KD, act_hi, act_lo)
            dve.wait_ge(f_done, 1)
            dve.wait_ge(bcast_loaded, 16)
            for t in range(NT):
                link(v.tensor_tensor(f_s[:, 0, t * NHEADS:(t + 1) * NHEADS], bank[6][:, t * NHEADS:(t + 1) * NHEADS], bf_bc[:], ALU.add))
            v.scalar_tensor_tensor(out=f_s[:, 1, :], in0=f_s[:, 0, :], scalar=-1.0, in1=f_s[:, 0, :], op0=ALU.mult,
                                   op1=ALU.max).then_inc(f_abs, 1)
            link(v.tensor_scalar(f_s[:, 6, :], f_s[:, 0, :], 0.0, None, ALU.min))
            dve.wait_ge(f_exp, 1)
            log1p_terms(lambda n: f_s[:, n, :], f_s[:, 6, :], 1.0, f_s[:, 7, :]).then_inc(logf_ready, 1)
            split_lo(U_K + SPL)
            split_lo(U_K + 1 + SPL)
            dve.wait_ge(cf_done, 1)
            v.tensor_copy(c_t[:].rearrange("p t h -> p (t h)"), bank[7][:, 0:NT * NHEADS]).then_inc(cT_ready, 1)
            v.tensor_copy(c_T[:], bank[7][0:NHEADS, 64:64 + T]).then_inc(cT_ready, 1)
            for k in range(2, 12):
                split_lo(U_K + k + SPL)

            dve.wait_ge(cT_ready, 2)
            dve.wait_ge(cbc_loaded, 16)
            for i in range(NHEADS + 3):
                if i < NHEADS:
                    dve.wait_ge(s_done, i + 1)
                    if i >= 2:
                        dve.wait_ge(pt_done, i - 1)
                    for t in range(NT):
                        cut = slice(0, P) if t == 0 else slice(P, 3 * P)
                        link(v.scalar_tensor_tensor(out=prob[:, i % 2, cut], in0=bank[i % 2][:, cut], scalar=c_t[:, t, i:i + 1],
                                                    in1=c_bc[:, i, 0:P * (t + 1)], op0=ALU.add, op1=ALU.subtract))
                        last = v.tensor_reduce(negmax[:, i % 2, t:t + 1], prob[:, i % 2, cut], AX.X, ALU.max, negate=True)
                    last.then_inc(s_ready, 1)
                if 1 <= i <= NHEADS:
                    b = (i - 1) % 2
                    dve.wait_ge(p_exp, 2 * i)
                    link(v.reciprocal(pinv[:, b, :], psums[:, b, :]))
                    v.tensor_scalar(prob[:, b, 0:P], prob[:, b, 0:P], pinv[:, b, 0:1], None, ALU.mult)
                    v.tensor_scalar(prob[:, b, P:3 * P], prob[:, b, P:3 * P], pinv[:, b, 1:2], None, ALU.mult).then_inc(p_norm, 1)
                if i % 4 == 2 and i // 4 < 4:
                    split_lo(U_G + i // 4 + SPL)
                if i >= 3 and i % 2 == 1:
                    hp = (i - 3) // 2
                    dve.wait_ge(pv_done, 2 * hp + 2)
                    dve.wait_ge(tg_ready, hp // 2 + 1)
                    v.scalar_tensor_tensor(out=q_T[:, hp, :], in0=tg[:, hp, :], scalar=1.0, in1=bank[4 + hp % 2][:, 0:T],
                                           op0=ALU.add, op1=ALU.mult).then_inc(o_ready, 1)
                if i >= 4 and i % 2 == 0:
                    hp = (i - 4) // 2
                    dve.wait_ge(alt_hi_done, 2 + hp + 1)
                    v.scalar_tensor_tensor(out=alt_lo[:, hp, :], in0=q_T[:, hp, :], scalar=0.5, in1=alt_hi[:, hp, :].bitcast(f32),
                                           op0=ALU.mult, op1=ALU.subtract).then_inc(alt_lo_done, 1)
            for k in range(4):
                if k == 2:
                    dve.wait_ge(unit_used, U_O + 2)
                    add_to_x(x_added, lambda t, half: bank[2 * half + t][:], (0,))
                split_lo(U_O + k + SPL)
            dve.wait_ge(unit_used, U_O + 4)
            add_to_x(x_added, lambda t, half: bank[2 * half + t][:], (1,))

            dve.wait_ge(x_added, 12)
            squares(3)
            scale_x(3)
            norm_lo(4, R_NORM + 3 * KD, act_hi, act_lo)
            dve.wait_ge(xs_hi_done, 1)
            v.tensor_tensor(alt_lo[:].rearrange("p c n -> p (c n)"), xs[:].rearrange("p t d -> p (t d)"),
                            alt_hi[:].rearrange("p c n -> p (c n)").bitcast(f32), ALU.subtract).then_inc(src_ready, 1)
            LOG, GT, EQ, INC, MASK, EXP, GATE, OFF = range(8)
            dve.wait_ge(logits_done, 1)
            link(v.tensor_copy(route[:, LOG, :, :], bank[4][:, 0:NT * NE].rearrange("p (t e) -> p t e", t=NT)))
            for t in range(NT):
                r = lambda n: route[:, n, t, :]
                link(v.max(top8[:, t, :], r(LOG)))
                v.tensor_scalar(rcol[:, 0, t:t + 1], top8[:, t, 0:1], -1.0, None, ALU.mult).then_inc(v1_ready, 1)
                v.tensor_scalar(r(GT), r(LOG), top8[:, t, 1:2], None, ALU.is_gt)
                link(v.tensor_scalar(r(EQ), r(LOG), top8[:, t, 1:2], None, ALU.is_equal))
                link(v.tensor_tensor_scan(r(INC), ones[:, 0:NE], r(EQ), 0.0, ALU.mult, ALU.add))
                link(v.tensor_reduce(rcol[:, 1, t:t + 1], r(GT), AX.X, ALU.add))
                link(v.tensor_scalar(rcol[:, 2, t:t + 1], rcol[:, 1, t:t + 1], -1.0, 2.0, ALU.mult, ALU.add))
                link(v.scalar_tensor_tensor(out=r(INC), in0=r(INC), scalar=rcol[:, 2, t:t + 1], in1=r(EQ), op0=ALU.is_le, op1=ALU.mult))
                v.tensor_tensor(r(MASK), r(INC), r(GT), ALU.add).then_inc(mask_ready, 1)
            dve.wait_ge(mask_ready, 2)
            for t in range(NT):
                r = lambda n: route[:, n, t, :]
                dve.wait_ge(e_ready, t + 1)
                link(v.tensor_tensor(r(GATE), r(EXP), r(MASK), ALU.mult))
                link(v.tensor_reduce(rcol[:, 3, t:t + 1], r(GATE), AX.X, ALU.add))
                link(v.reciprocal(rcol[:, 4, t:t + 1], rcol[:, 3, t:t + 1]))
                link(v.tensor_scalar(gate_of[:, t, 0:NE], r(GATE), rcol[:, 4, t:t + 1], None, ALU.mult))
                link(v.tensor_scalar(gate_of[:, t, NE:2 * NE], r(GATE), rcol[:, 4, t:t + 1], None, ALU.mult))
                link(v.tensor_scalar(r(OFF), r(MASK), 1000.0, -1000.0, ALU.mult, ALU.add))
            link(v.memset(gate_of[:, :, 2 * NE:], 0.0))
            link(v.memset(slot_of[:, :, 2 * NE:], -1000.0))
            dve.wait_ge(rank_done, 1)
            for t in range(NT):
                link(v.tensor_tensor(slot_of[:, t, 0:NE], route[:, OFF, t, :], bank[5][:, t * NE:(t + 1) * NE], ALU.add))
                link(v.tensor_scalar(slot_of[:, t, NE:2 * NE], slot_of[:, t, 0:NE], float(P), None, ALU.subtract))
            link(v.tensor_reduce(njobs_f[:, 0:1], bank[5][:, NT * NE:NT * NE + NE], AX.X, ALU.max))
            link(v.tensor_scalar(njobs_f[:, 1:2], njobs_f[:, 0:1], float(P), float(NE), ALU.is_gt, ALU.mult))
            v.tensor_scalar(njobs[:], njobs_f[:, 1:2], float(NE), None, ALU.add).then_inc(njobs_ready, 1)

            def build_sel(j):
                for t in range(NT):
                    slot, gate = slot_of[:, t, bass.ds(j, 1)], gate_of[:, t, bass.ds(j, 1)]
                    v.tensor_scalar(sel[:, t, :], iota[:], slot, None, ALU.is_equal)
                    last = v.tensor_scalar(sel_g[:, t, :], iota[:], slot, gate, ALU.is_equal, ALU.mult)
                last.then_inc(sel_built, 1)

            def tokens_lo(j):
                for c in range(KD):
                    if c % 4 == 0:
                        dve.wait_ge(tok_hi_done, KD * j + c + 4)
                    part = (slice(None), c // 2, slice((c % 2) * P, (c % 2 + 1) * P))
                    v.scalar_tensor_tensor(out=act_lo[part], in0=bank[6 + c // 4][:, (c % 4) * P:(c % 4 + 1) * P],
                                           scalar=cols[:, R_NORM + 3 * KD + c:R_NORM + 3 * KD + c + 1],
                                           in1=act_hi[part].bitcast(f32), op0=ALU.mult, op1=ALU.subtract).then_inc(tok_lo_done, 1)

            def y_lo_part(j):
                for half in range(2):
                    dve.wait_ge(yhi_done, 2 * j + half + 1)
                    cut = slice(HALF * half, HALF * half + HALF)
                    v.scalar_tensor_tensor(out=y_lo[:, cut], in0=bank[half][:], scalar=gslot[:, 0:1],
                                           in1=y_hi[:, cut].bitcast(f32), op0=ALU.mult, op1=ALU.subtract).then_inc(ylo_done, 1)

            def add_scattered(j):
                for half in range(2):
                    for t in range(NT):
                        dve.wait_ge(scattered, 4 * j + 2 * half + t + 1)
                        part = x[:, t, HALF * half:HALF * half + HALF]
                        v.tensor_tensor(part, part, bank[4 + 2 * half + t][:], ALU.add).then_inc(moe_added, 1)

            build_sel(0)
            v.memset(sel_T[:].bitcast(i32), 0)
            v.memset(gslot[:], 0.0).then_inc(selT_ready, 1)
            v.memset(bank[0][:], 0.0).then_inc(moe_blank, 1)
            v.memset(bank[1][:], 0.0).then_inc(moe_blank, 1)
            tokens_lo(0)
            jobs = dve.value_load(njobs[0:1, 0:1], min_val=NE, max_val=2 * NE)
            with dve.Fori(0, jobs) as j:
                for k in range(JU):
                    if k == 0:
                        y_lo_part(j)
                    if k == 4 or (k >= 8 and k % 6 == 2 and k // 6 < CH):
                        c = 0 if k == 4 else k // 6
                        dve.wait_ge(e_silu, CH * j + c + 1)
                        dve.wait_ge(unit_used, U_MOE + JU * j + k)
                        if c:
                            dve.wait_ge(e_T, CH * j + c)
                        v.tensor_tensor(hid[:], silu[:], bank[3][:], ALU.mult).then_inc(e_h, 1)
                    if k == 5:
                        add_scattered(j)
                    if (k >= 6 and k % 6 == 0) or k == JU - 3:
                        c = k // 6 - 1 if k < JU - 3 else CH - 1
                        dve.wait_ge(e_hid_hi, CH * j + c + 1)
                        v.tensor_tensor(hid_lo[:, c % 2, :], bank[4 + c % 2][:], hid_hi[:, c % 2, :].bitcast(f32),
                                        ALU.subtract).then_inc(e_hid_lo, 1)
                    if k == 9:
                        dve.wait_ge(selg_T, j + 1)
                        v.tensor_reduce(gslot[:], bank[6][:, 0:T], AX.X, ALU.add)
                        v.tensor_scalar(sel_T[:], bank[6][:, 0:T], 0.0, None, ALU.is_gt).then_inc(selT_ready, 1)
                    if k == 20:
                        build_sel(j + 1)
                    if k == JU - 2:
                        tokens_lo(j + 1)
                    split_lo(U_MOE + k + SPL, J6 * j)
            y_lo_part(jobs)
            add_scattered(jobs)
            dve.wait_ge(moe_added, 4 * jobs + 4)
            squares(4)
            dve.wait_ge(rstd_ready, 5)
            dve.wait_ge(gfin_loaded, 16)
            for t in range(NT):
                v.scalar_tensor_tensor(out=xs[:, t, :], in0=x[:, t, :], scalar=rstd[:, 4, t:t + 1], in1=gfin_bc[:],
                                       op0=ALU.mult, op1=ALU.mult).then_inc(out_ready, 1)

        @block.tensor
        def _(pe):
            t_ = nc.tensor

            def mm3(dst, l_hi, l_lo, r_hi, r_lo, start, stop):
                t_.matmul(dst, l_lo, r_hi, start=start, stop=False)
                t_.matmul(dst, l_hi, r_lo, start=False, stop=False)
                return t_.matmul(dst, l_hi, r_hi, start=False, stop=stop)

            def unit_ready(u, n=0):
                pe.wait_ge(lo_done, units(u, n) + 1)

            def stationary_unit(u, n, a_hi, a_lo, dst, first_count=None):
                unit_ready(u, n)
                for f in range(2):
                    for k in range(KD):
                        if first_count is not None and f == 0:
                            pe.wait_ge(act_lo_done, first_count + k + 1)
                        w = slice(k * 256 + f * P, k * 256 + f * P + P)
                        last = mm3(dst[:, f * T:(f + 1) * T], w_hi[:, u % SPL, w], w_lo[:, u % SPL, w],
                                   a_hi[:, k, :], a_lo[:, k, :], k == 0, k == KD - 1)
                last.then_inc(unit_used, 1)

            def moving_unit(u, a_hi, a_lo, k_half, dst, before_k=None):
                unit_ready(u)
                for k in range(4):
                    kk = 4 * k_half + k
                    if before_k:
                        before_k(kk)
                    for t in range(NT):
                        w = slice(k * 512, k * 512 + 512)
                        last = mm3(dst[t][:], a_hi[:, kk, t * P:(t + 1) * P], a_lo[:, kk, t * P:(t + 1) * P],
                                   w_hi[:, u % SPL, w], w_lo[:, u % SPL, w], kk == 0, kk == KD - 1)
                last.then_inc(unit_used, 1)

            def transpose_x(n):
                for t in range(NT):
                    pe.wait_ge(xs_ready, 2 * n + t + 1)
                    for c in range(KD):
                        dst = bank[c // 2][:, (c % 2) * T + t * P:(c % 2) * T + (t + 1) * P]
                        last = t_.transpose(dst, xs[:, t, c * P:(c + 1) * P], ident[:])
                        if t == NT - 1 and c % 2:
                            last.then_inc(norm_T, 1)

            pe.wait_ge(rows_loaded, 6 * 16)
            pe.wait_ge(consts, 5)
            t_.transpose(bank[7][:, 0:R_END], rows[0:R_END, :], ident[0:R_END, 0:R_END]).then_inc(rows_T, 1)

            transpose_x(0)
            pe.wait_ge(gatew_loaded, 16)
            pe.wait_ge(cols_ready, 1)

            def lru_gates(c):
                pe.wait_ge(xc_ready, c + 1)
                if c >= 4:
                    pe.wait_ge(sig_done, 2 * (c - 4) + 2)
                else:
                    pe.wait_ge(act_lo_done, KD)
                for g in range(2):
                    last = t_.matmul(bank[c % 4][:, g * T:(g + 1) * T], gate_w[:, g * KD + c, :], xc[:, c, :], start=True, stop=True)
                last.then_inc(gates_done, 1)

            for u in range(8):
                if u >= 4:
                    pe.wait_ge(xb_ready, u - 3)
                stationary_unit(u, 0, act_hi, act_lo, bank[4 + u % 4], 0 if u == 0 else None)
                if 1 <= u <= 4:
                    lru_gates(2 * u - 2)
                    lru_gates(2 * u - 1)
            pe.wait_ge(sig_done, 2 * KD)
            for c in range(4):
                moving_unit(U_OUT + c, alt_hi, alt_lo, c % 2, [bank[2 * (c // 2)], bank[2 * (c // 2) + 1]],
                            (lambda kk: pe.wait_ge(alt_lo_done, kk // 4 + 1)) if c < 2 else None)

            pe.wait_ge(x_added, 4)
            pe.wait_ge(gelu_done, 4)
            transpose_x(1)

            def ff_gate_up(u, n, m, first_count=None):
                stationary_unit(u, n, act_hi, act_lo, bank[4 + 2 * (m % 2)], first_count)
                stationary_unit(u + 1, n, act_hi, act_lo, bank[5 + 2 * (m % 2)])

            def ff_down(u, n, p, m, first, last_one):
                unit_ready(u, n)
                pe.wait_ge(hid_lo_done, p + 1)
                for k in range(2):
                    for t in range(NT):
                        h = slice(k * T + t * P, k * T + (t + 1) * P)
                        for half in range(2):
                            w = slice(k * D + half * HALF, k * D + half * HALF + HALF)
                            last = mm3(bank[2 * half + t][:], hid_hi[:, m % 2, h], hid_lo[:, m % 2, h],
                                       w_hi[:, u % SPL, w], w_lo[:, u % SPL, w], first and k == 0, last_one and k == 1)
                last.then_inc(unit_used, 1)

            ff_gate_up(U_FF, 0, 0, KD)
            ff_gate_up(U_FF + 2, 0, 1)
            pe.wait_ge(act_lo_done, 2 * KD)
            ff_down(U_FF + 4, 0, 0, 0, True, False)
            with pe.Fori(0, (PAIRS - 3) // 2) as i:
                for m in (2, 3):
                    u = U_FF + 3 * m - 1
                    pe.wait_ge(h_done, 2 * i + m - 1)
                    ff_gate_up(u, i, m)
                    ff_down(u + 2, i, 2 * i + m - 1, m - 1, False, False)
            u = U_FF + 3 * (PAIRS - 1) - 1
            pe.wait_ge(h_done, PAIRS - 2)
            ff_gate_up(u, 0, PAIRS - 1)
            ff_down(u + 2, 0, PAIRS - 2, PAIRS - 2, False, False)
            ff_down(u + 3, 0, PAIRS - 1, PAIRS - 1, False, True)

            pe.wait_ge(x_added, 8)
            transpose_x(2)
            pe.wait_ge(small_lo, 2)
            pe.wait_ge(act_lo_done, 3 * KD)
            for t in range(NT):
                for k in range(KD):
                    last = mm3(bank[6][:, t * NHEADS:(t + 1) * NHEADS], alt_hi[:, k, t * P:(t + 1) * P], alt_lo[:, k, t * P:(t + 1) * P],
                               wf_hi[:, k, :], wf_lo[:, k, :], k == 0, k == KD - 1)
            last.then_inc(f_done, 1)
            for c in range(4):
                if c >= 2:
                    pe.wait_ge(k_ready, c - 1)
                stationary_unit(U_K + c, 0, alt_hi, alt_lo, bank[4 + c % 2])
                if c == 1:
                    pe.wait_ge(logf_ready, 1)
                    lf = [f_s[:, 7, t * NHEADS:(t + 1) * NHEADS] for t in range(NT)]
                    t_.matmul(bank[7][:, 0:NHEADS], upto[:], lf[0], start=True, stop=True)
                    t_.matmul(bank[7][:, NHEADS:2 * NHEADS], ones[:], lf[0], start=True, stop=False)
                    t_.matmul(bank[7][:, NHEADS:2 * NHEADS], upto[:], lf[1], start=False, stop=True)
                    t_.matmul(bank[7][0:NHEADS, 64:64 + P], lf[0], upto[:], start=True, stop=True)
                    t_.matmul(bank[7][0:NHEADS, 64 + P:64 + T], lf[0], ones[:], start=True, stop=False)
                    t_.matmul(bank[7][0:NHEADS, 64 + P:64 + T], lf[1], upto[:], start=False, stop=True).then_inc(cf_done, 1)
            pe.wait_ge(act_lo_done, 4 * KD)
            for c in range(4):
                moving_unit(U_V + c, alt_hi, alt_lo, c % 2, [bank[2 * (c // 2)], bank[2 * (c // 2) + 1]])
            for c in range(4):
                pe.wait_ge(k_ready if c < 2 else q_ready, 3 + c if c < 2 else c - 1)
                stationary_unit(U_Q + c, 0, act_hi, act_lo, bank[4 + c % 2])

            pe.wait_ge(v_ready, 4)
            pe.wait_ge(consts_v, 2)
            pe.wait_ge(cT_ready, 2)
            for i in range(NHEADS + 2):
                if i < NHEADS:
                    rows_h = slice(HD * (i % 2), HD * (i % 2) + HD)
                    hp = i // 2
                    if i % 4 == 0:
                        pe.wait_ge(q_ready, i // 4 + 1)
                    if i >= 2:
                        pe.wait_ge(s_ready, i - 1)
                    s0, s1 = bank[i % 2][:, 0:P], bank[i % 2][:, P:3 * P]
                    t_.matmul(s0, ident_bf[:], mask_bf[:], start=True, stop=False)
                    t_.matmul(s0, q_T[rows_h, hp, 0:P], k_T[rows_h, hp, 0:P], start=False, stop=True)
                    t_.matmul(s1, q_T[rows_h, hp, P:T], k_T[rows_h, hp, 0:T], start=True, stop=False)
                    t_.matmul(bank[i % 2][:, 2 * P:3 * P], ident_bf[:], mask_bf[:], start=False, stop=True).then_inc(s_done, 1)
                if i % 4 == 1 and i // 4 < 4:
                    c = i // 4
                    if c >= 2:
                        pe.wait_ge(tg_ready, c - 1)
                    stationary_unit(U_G + c, 0, act_hi, act_lo, bank[6 + c % 2])
                if 1 <= i <= NHEADS:
                    h = i - 1
                    pe.wait_ge(p_norm, h + 1)
                    if h >= 2:
                        pe.wait_ge(pt_ready, h - 1)
                    for n in range(3):
                        last = t_.transpose(bank[2 + h % 2][:, n * P:(n + 1) * P], prob[:, h % 2, n * P:(n + 1) * P], ident[:])
                    last.then_inc(pt_done, 1)
                if i >= 2:
                    h = i - 2
                    hp = h // 2
                    pe.wait_ge(pt_ready, h + 1)
                    if h % 2 == 0 and hp >= 2:
                        pe.wait_ge(o_ready, hp - 1)
                    o = bank[4 + hp % 2][HD * (h % 2):HD * (h % 2) + HD, :]
                    t_.matmul(o[:, 0:T], v_sb[:, 0, h * HD:(h + 1) * HD], prob_T[:, h % 2, 0:T], start=True, stop=False)
                    t_.matmul(o[:, P:T], v_sb[:, 1, h * HD:(h + 1) * HD], prob_T[:, h % 2, T:3 * P], start=False, stop=True).then_inc(pv_done, 1)
            for c in range(4):
                moving_unit(U_O + c, alt_hi, alt_lo, c % 2, [bank[2 * (c // 2)], bank[2 * (c // 2) + 1]],
                            (lambda kk: pe.wait_ge(alt_lo_done, 2 + kk + 1)) if c < 2 else None)

            pe.wait_ge(x_added, 12)
            transpose_x(3)
            pe.wait_ge(act_lo_done, 5 * KD)
            for t in range(NT):
                for k in range(KD):
                    last = mm3(bank[4][:, t * NE:(t + 1) * NE], act_hi[:, k, t * P:(t + 1) * P], act_lo[:, k, t * P:(t + 1) * P],
                               rt_hi[:, k, :], rt_lo[:, k, :], k == 0, k == KD - 1)
            last.then_inc(logits_done, 1)
            pe.wait_ge(mask_ready, 2)
            m0, m1 = route[:, 4, 0, :], route[:, 4, 1, :]
            t_.matmul(bank[5][:, 0:NE], before[:], m0, start=True, stop=True)
            t_.matmul(bank[5][:, NE:2 * NE], ones[:], m0, start=True, stop=False)
            t_.matmul(bank[5][:, NE:2 * NE], before[:], m1, start=False, stop=True)
            t_.matmul(bank[5][:, 2 * NE:3 * NE], ones[:], m0, start=True, stop=False)
            t_.matmul(bank[5][:, 2 * NE:3 * NE], ones[:], m1, start=False, stop=True).then_inc(rank_done, 1)

            src_hi = alt_hi[:].rearrange("p c n -> p (c n)")
            src_lo = alt_lo[:].rearrange("p c n -> p (c n)")

            def gather():
                for c in range(KD):
                    dst = bank[6 + c // 4][:, (c % 4) * P:(c % 4 + 1) * P]
                    for t in range(NT):
                        w = slice(t * D + c * P, t * D + (c + 1) * P)
                        t_.matmul(dst, src_lo[:, w], sel[:, t, :], start=(t == 0), stop=False)
                        last = t_.matmul(dst, src_hi[:, w], sel[:, t, :], start=False, stop=(t == NT - 1))
                last.then_inc(gathered, 1)

            def scatter(j):
                pe.wait_ge(ylo_done, 2 * j + 2)
                for half in range(2):
                    w = slice(HALF * half, HALF * half + HALF)
                    for t in range(NT):
                        dst = bank[4 + 2 * half + t][:]
                        t_.matmul(dst, sel_T[:, t * P:(t + 1) * P], y_lo[:, w], start=True, stop=False)
                        t_.matmul(dst, sel_T[:, t * P:(t + 1) * P], y_hi[:, w], start=False, stop=True).then_inc(scattered, 1)

            def expert_in(u, n, dst, k_half):
                unit_ready(u, n)
                for k in range(4):
                    kk = 4 * k_half + k
                    s = (slice(None), kk // 2, slice((kk % 2) * P, (kk % 2 + 1) * P))
                    w = slice(k * 512, k * 512 + 512)
                    last = mm3(dst[:], act_hi[s], act_lo[s], w_hi[:, u % SPL, w], w_lo[:, u % SPL, w], kk == 0, kk == KD - 1)
                last.then_inc(unit_used, 1)

            def expert_out(u, n, c, k_half):
                unit_ready(u, n)
                for k in range(2):
                    h = slice((2 * k_half + k) * P, (2 * k_half + k + 1) * P)
                    for half in range(2):
                        w = slice(k * D + half * HALF, k * D + half * HALF + HALF)
                        first, final = c == 0 and k_half == 0 and k == 0, c == CH - 1 and k_half == 1 and k == 1
                        last = mm3(bank[half][:], hid_hi[:, c % 2, h], hid_lo[:, c % 2, h],
                                   w_hi[:, u % SPL, w], w_lo[:, u % SPL, w], first, final)
                last.then_inc(unit_used, 1)

            def hidden_T(j, c):
                pe.wait_ge(e_h, CH * j + c + 1)
                for n in range(4):
                    last = t_.transpose(bank[4 + c % 2][:, n * P:(n + 1) * P], hid[:, n * P:(n + 1) * P], ident[:])
                last.then_inc(e_T, 1)

            pe.wait_ge(src_ready, 1)
            pe.wait_ge(sel_built, 1)
            gather()
            pe.wait_ge(njobs_ready, 1)
            jobs = pe.value_load(njobs[0:1, 0:1], min_val=NE, max_val=2 * NE)
            with pe.Fori(0, jobs) as j:
                n = J6 * j
                pe.wait_ge(tok_lo_done, KD * j + KD)
                for c in range(CH):
                    u = U_MOE + (6 * c - 2 if c else 0)
                    if c:
                        pe.wait_ge(e_silu, CH * j + c)
                    expert_in(u, n, bank[2], 0)
                    expert_in(u + 1, n, bank[2], 1)
                    if c == 1:
                        pe.wait_ge(moe_added, 4 * j + 4)
                    if c:
                        hidden_T(j, c - 1)
                    expert_in(u + 2, n, bank[3], 0)
                    expert_in(u + 3, n, bank[3], 1)
                    if c == 0:
                        scatter(j)
                    if c == 1:
                        for t in range(NT):
                            last = t_.transpose(bank[6][:, t * P:(t + 1) * P], sel_g[:, t, :], ident[:])
                        last.then_inc(selg_T, 1)
                    if c:
                        pe.wait_ge(e_hid_lo, CH * j + c)
                        expert_out(u + 4, n, c - 1, 0)
                        if c == CH - 1:
                            hidden_T(j, c)
                            pe.wait_ge(sel_built, j + 2)
                            pe.wait_ge(selT_ready, j + 2)
                            gather()
                        expert_out(u + 5, n, c - 1, 1)
                pe.wait_ge(e_hid_lo, CH * j + CH)
                expert_out(U_MOE + JU - 2, n, CH - 1, 0)
                expert_out(U_MOE + JU - 1, n, CH - 1, 1)
            pe.wait_ge(tok_lo_done, KD * jobs + KD)
            scatter(jobs)


_INS = ["x", "norm_g", "lru_w_in", "lru_conv_w", "lru_conv_b", "lru_gate_w", "lru_gate_b", "lru_lambda", "lru_w_out",
        "kv_norm_g", "w_kvf", "b_f", "fox_w_qg", "fox_w_o", "mlp_w_gu", "mlp_w_down", "moe_router", "moe_w_gu",
        "moe_w_down", "final_norm_g"]


def kernel(**inputs):
    import numpy as _np
    import concourse.bacc as _bacc
    from concourse.bass_utils import run_bass_kernel_spmd as _run

    nc = _bacc.Bacc("TRN2", target_bir_lowering=False, num_devices=1)
    arrays, args = {}, []
    for name in _INS:
        a = _np.ascontiguousarray(inputs[name])
        arrays[f"in_{name}"] = a
        args.append(nc.dram_tensor(f"in_{name}", a.shape, mybir.dt.from_np(a.dtype), kind="ExternalInput").ap())
    cf = nc.dram_tensor("cf_dram", (NHEADS, T), mybir.dt.float32).ap()
    out = nc.dram_tensor("out_0", (1, T, D), mybir.dt.float32, kind="ExternalOutput").ap()
    yoco_kernel(nc, *args, cf, out)
    r = _run(nc, [arrays], core_ids=[0])
    return r.results[0]["out_0"]
```

```python
from contextlib import ExitStack

import concourse.bass as bass
from concourse import mybir

P = 128
D = 1024
T = 256
NT = T // P
KD = D // P
NHEADS = 16
HD = D // NHEADS
D_FF = 2816
D_EXP = 3584
NE = 8
EPS = 1e-6
LRU_C = 8.0
CONV_W = 4
NEG = -1e30

UW = 2048
RAW = 6
SPL = 3
LEAD = SPL - 1
HALF = D // 2
PS = 3

U_XB, U_GB, U_OUT = 0, 4, 8
PAIRS = D_FF // (2 * P)
U_FF = 12
U_K = U_FF + 3 * PAIRS
U_V, U_Q, U_G, U_O = U_K + 4, U_K + 8, U_K + 12, U_K + 16
U_MOE = U_O + 4
CH = D_EXP // 512
JU = 6 * CH
J6 = JU // RAW

R_NORM, R_KVN, R_CB, R_CW, R_GB, R_LAM, R_END = 0, 32, 40, 48, 80, 96, 104
SLOT_COLS = 2 * NE + 1


def yoco_kernel(nc, x_in, norm_g, lru_w_in, lru_conv_w, lru_conv_b, lru_gate_w, lru_gate_b, lru_lambda,
                lru_w_out, kv_norm_g, w_kvf, b_f, fox_w_qg, fox_w_o, mlp_w_gu, mlp_w_down,
                moe_router, moe_w_gu, moe_w_down, final_norm_g, out):
    f32, f32r, bf16, i32 = mybir.dt.float32, mybir.dt.float32r, mybir.dt.bfloat16, mybir.dt.int32
    ALU, ACT, AX = mybir.AluOpType, mybir.ActivationFunctionType, mybir.AxisListType

    ctx = ExitStack()
    with ctx:
        def sb(name, shape, dt=f32, into=ctx):
            return into.enter_context(nc.sbuf_tensor(name, shape, dt))

        def sem(name):
            return ctx.enter_context(nc.semaphore(name))

        raw = sb("raw", [P, RAW, UW])
        w_hi = sb("w_hi", [P, SPL, UW], f32r)
        w_lo = sb("w_lo", [P, SPL, UW], f32r)
        act_hi = sb("act_hi", [P, KD, T], f32r)
        act_lo = sb("act_lo", [P, KD, T], f32r)
        alt_hi = sb("alt_hi", [P, KD, T], f32r)
        alt_lo = sb("alt_lo", [P, KD, T], f32r)
        x = sb("x", [P, NT, D])
        xs = sb("xs", [P, NT, D])
        ident = sb("ident", [P, P])
        ident_bf = sb("ident_bf", [P, P], bf16)
        ones = sb("ones", [P, T])
        upto = sb("upto", [P, P])
        before = sb("before", [P, P])
        maskf = sb("maskf", [P, P])
        mask_bf = sb("mask_bf", [P, P], bf16)
        iota = sb("iota", [P, P])
        rows = sb("rows", [P, P])
        cols = sb("cols", [P, R_END])
        wf_raw = sb("wf_raw", [P, KD, NHEADS])
        wf_hi = sb("wf_hi", [P, KD, NHEADS], f32r)
        wf_lo = sb("wf_lo", [P, KD, NHEADS], f32r)
        rt_raw = sb("rt_raw", [P, KD, NE])
        rt_hi = sb("rt_hi", [P, KD, NE], f32r)
        rt_lo = sb("rt_lo", [P, KD, NE], f32r)
        bf_col = sb("bf_col", [NHEADS, 1])
        head_1 = sb("head_1", [P, NHEADS], f32r)
        ss = sb("ss", [P, 5, NT])
        msq = sb("msq", [P, 5, NT])
        rstd = sb("rstd", [P, 5, NT])
        neghalf = sb("neghalf", [P, NT])
        lam_s = sb("lam_s", [P, 8, KD])
        m4ls = sb("m4ls", [P, KD])
        p8ls = sb("p8ls", [P, KD])
        negmax = sb("negmax", [P, PS, NT])
        psums = sb("psums", [P, PS, NT])
        pinv = sb("pinv", [P, PS, NT])
        route = sb("route", [P, 12, NT, NE])
        top8 = sb("top8", [P, NT, 8])
        rcol = sb("rcol", [P, 4, NT])
        logit_T = sb("logit_T", [NE, T])
        slot_of = sb("slot_of", [P, NT, SLOT_COLS])
        gate_of = sb("gate_of", [P, NT, SLOT_COLS])
        njobs_f = sb("njobs_f", [P, 2])
        njobs = sb("njobs", [P, 1], i32)
        gslot = sb("gslot", [P, 1])

        with ExitStack() as lru:
            xb_pad = sb("xb_pad", [P, KD, T + CONV_W - 1], f32, lru)
            xc = sb("xc", [P, KD, T], f32, lru)
            rc = sb("rc", [P, KD, T], f32, lru)
            gelu = sb("gelu", [P, KD, T], f32, lru)
            gate_w = sb("gate_w", [P, 2 * KD, P], f32, lru)
            i_sb = sb("i_sb", [P, 2, 2, T], f32, lru)
        th = xs[:, :, :].rearrange("p t d -> p (t d)").rearrange("p (c n) -> p c n", c=KD)
        with ExitStack() as att:
            k_T = sb("k_T", [P, KD, T], f32, att)
            q_T = sb("q_T", [P, KD, T], f32, att)
            v_sb = sb("v_sb", [P, NT, D], f32, att)
            f_s = sb("f_s", [NHEADS, 8, T], f32, att)
            c_pos = sb("c_pos", [P, T], f32r, att)
            c_neg = sb("c_neg", [P, T], f32r, att)
            prob = sb("prob", [P, PS, 3 * P], f32, att)
            prob_T = sb("prob_T", [P, 2, 3 * P], f32, att)
        tg = th
        with ExitStack() as ffn:
            hid_hi = sb("hid_hi", [P, 2, 512], f32r, ffn)
            hid_lo = sb("hid_lo", [P, 2, 512], f32r, ffn)
            silu = sb("silu", [P, 512], f32, ffn)
            hid = sb("hid", [P, 512], f32, ffn)
            y_hi = sb("y_hi", [P, D], f32r, ffn)
            y_lo = sb("y_lo", [P, D], f32r, ffn)
            sel = sb("sel", [P, NT, P], f32r, ffn)
            sel_g = sb("sel_g", [P, NT, P], f32, ffn)
            sel_T = sb("sel_T", [P, T], f32r, ffn)
            gfin_bc = sb("gfin_bc", [P, D], f32, ffn)

        bank = [ctx.enter_context(nc.psum_tensor(f"bank{i}", [P, 512], f32)) for i in range(8)]

        raw_full = [sem(f"raw_full{i}") for i in range(RAW)]
        hi_done, lo_done, unit_used = sem("hi_done"), sem("lo_done"), sem("unit_used")
        x_loaded, rows_loaded, bf_loaded, gatew_loaded = (sem(n) for n in ("x_loaded", "rows_loaded", "bf_loaded", "gatew_loaded"))
        smallw_loaded, gfin_loaded, stored = (sem(n) for n in ("smallw_loaded", "gfin_loaded", "stored"))
        blank, consts, consts_v = sem("blank"), sem("consts"), sem("consts_v")
        rows_T, cols_ready = sem("rows_T"), sem("cols_ready")
        small_hi, small_lo = sem("small_hi"), sem("small_lo")
        lam_abs, lam_exp, lam_ready = sem("lam_abs"), sem("lam_exp"), sem("lam_ready")
        sq_act, sq_dve, msq_ready, rstd_ready, xs_ready = (sem(n) for n in ("sq_act", "sq_dve", "msq_ready", "rstd_ready", "xs_ready"))
        norm_T, act_hi_done, act_lo_done = sem("norm_T"), sem("act_hi_done"), sem("act_lo_done")
        link_v = sem("link_v")
        pad_ready, xb_ready, xc_ready, gates_done = (sem(n) for n in ("pad_ready", "xb_ready", "xc_ready", "gates_done"))
        sig_done, decay_done, bx_done, sqrt_done, gelu_done = (sem(n) for n in ("sig_done", "decay_done", "bx_done", "sqrt_done", "gelu_done"))
        yl_ready, alt_hi_done, alt_lo_done, x_added = (sem(n) for n in ("yl_ready", "alt_hi_done", "alt_lo_done", "x_added"))
        silu_done, h_done, hid_hi_done, hid_lo_done = (sem(n) for n in ("silu_done", "h_done", "hid_hi_done", "hid_lo_done"))
        f_done, f_abs, f_exp, c_blank, c_ready, c_hi_done, c_lo_done = (sem(n) for n in ("f_done", "f_abs", "f_exp", "c_blank", "c_ready", "c_hi_done", "c_lo_done"))
        k_ready, v_ready, q_ready, tg_ready = (sem(n) for n in ("k_ready", "v_ready", "q_ready", "tg_ready"))
        s_done, s_ready, p_exp, p_norm, pt_done, pt_ready, pv_done, o_ready = (sem(n) for n in ("s_done", "s_ready", "p_exp", "p_norm", "pt_done", "pt_ready", "pv_done", "o_ready"))
        logits_done, logitT_ready, v1_ready, e_ready, mask_ready, rank_done, njobs_ready = (sem(n) for n in ("logits_done", "logitT_ready", "v1_ready", "e_ready", "mask_ready", "rank_done", "njobs_ready"))
        xs_hi_done, src_ready, moe_blank = sem("xs_hi_done"), sem("src_ready"), sem("moe_blank")
        sel_built, gathered, tok_hi_done, tok_lo_done = (sem(n) for n in ("sel_built", "gathered", "tok_hi_done", "tok_lo_done"))
        selg_T, selT_ready, yhi_done, ylo_done, scattered, moe_added = (sem(n) for n in ("selg_T", "selT_ready", "yhi_done", "ylo_done", "scattered", "moe_added"))
        e_silu, e_h, e_T, e_hid_hi, e_hid_lo = (sem(n) for n in ("e_silu", "e_h", "e_T", "e_hid_hi", "e_hid_lo"))
        out_ready = sem("out_ready")

        def cols256(w, c):
            return w.rearrange("(k p) n -> p k n", p=P)[:, :, bass.ds(c * 256, 256)]

        def square(w, col_half, k_half):
            return w.rearrange("(k p) n -> p k n", p=P)[:, 4 * k_half:4 * k_half + 4, HALF * col_half:HALF * col_half + HALF]

        w_in, w_out, w_gu, w_dn = lru_w_in[0], lru_w_out[0], mlp_w_gu[0], mlp_w_down[0]
        w_qg, w_o = fox_w_qg[0], fox_w_o[0]
        dn_v = w_dn.rearrange("(k p) n -> p k n", p=P)
        e_gu = moe_w_gu[0].rearrange("e (k p) n -> e p k n", p=P)
        e_dn = moe_w_down[0].rearrange("e (k p) n -> e p k n", p=P)

        def raw_count(u, n):
            return 16 * (u // RAW + 1 + n)

        def units(u, n=0):
            return u + RAW * n

        block = ctx.enter_context(nc.Block())

        @block.sync
        def _(sp):
            def load(u, n, width, src):
                if not (isinstance(n, int) and u + RAW * n < RAW):
                    sp.wait_ge(lo_done, units(u, n) - RAW + 1)
                dst = raw[:, u % RAW, :].rearrange("p (k n) -> p k n", n=width)
                sp.dma_start(dst, src).then_inc(raw_full[u % RAW], 16)

            for t in range(NT):
                sp.dma_start(x[:, t, :], x_in[0, t * P:(t + 1) * P, :]).then_inc(x_loaded, 16)
            for c in range(8):
                load(U_XB + c, 0, 256, cols256(w_in, c))
            for c in range(4):
                load(U_OUT + c, 0, HALF, square(w_out, c // 2, c % 2))
            load(U_FF, 0, 256, cols256(w_gu, 0))
            load(U_FF + 1, 0, 256, cols256(w_gu, PAIRS))
            with sp.Fori(0, (PAIRS - 1) // 2) as i:
                for m in range(2):
                    u = U_FF + 2 + 3 * m
                    load(u, i, 256, cols256(w_gu, 2 * i + 1 + m))
                    load(u + 1, i, 256, cols256(w_gu, 2 * i + 1 + m + PAIRS))
                    load(u + 2, i, D, dn_v[:, bass.ds(4 * i + 2 * m, 2), :])
            load(U_K - 1, 0, D, dn_v[:, 2 * PAIRS - 2:2 * PAIRS, :])
            for c in range(4):
                load(U_K + c, 0, 256, cols256(w_kvf, c))
            for c in range(4):
                load(U_V + c, 0, HALF, square(w_kvf[:, D:2 * D], c // 2, c % 2))
            for c in range(8):
                load(U_Q + c, 0, 256, cols256(w_qg, c))
            for c in range(4):
                load(U_O + c, 0, HALF, square(w_o, c // 2, c % 2))

            def expert_unit(e, k):
                c, part = (0, k // 2) if k < 4 else ((k - 4) // 6 + 1, (k - 4) % 6 // 2)
                if k >= JU - 2:
                    c, part = CH, 2
                half = k % 2
                if part < 2:
                    lo = part * D_EXP + 512 * c
                    return e_gu[e][:, 4 * half:4 * half + 4, lo:lo + 512], 512
                lo = 4 * (c - 1) + 2 * half
                return e_dn[e][:, lo:lo + 2, :], D

            def expert(j, e, first, last):
                for k in range(first, last):
                    src, width = expert_unit(e, k)
                    load(U_MOE + k, J6 * j, width, src)

            with sp.Fori(0, NE) as j:
                expert(j, j, 0, JU)
            expert(NE, 0, 0, LEAD)
            sp.wait_ge(njobs_ready, 1)
            jobs = sp.value_load(njobs[0:1, 0:1], min_val=NE, max_val=2 * NE)
            with sp.If(jobs > NE):
                with sp.Fori(NE, 2 * NE - 1) as j:
                    expert(j, j - NE, LEAD, JU)
                    expert(j + 1, j - NE + 1, 0, LEAD)
                expert(2 * NE - 1, NE - 1, LEAD, JU)
                expert(2 * NE, 0, 0, LEAD)
            sp.wait_ge(out_ready, NT)
            sp.dma_start(out[0].rearrange("(t p) d -> p t d", p=P), xs[:, :, :]).then_inc(stored, 16)
            sp.wait_ge(stored, 16)

        @block.gpsimd
        def _(pool):
            g = nc.gpsimd
            g.memset(ident[:], 0.0).then_inc(blank, 1)
            g.memset(ones[:], 1.0).then_inc(blank, 1)
            g.memset(maskf[:], 0.0).then_inc(blank, 1)
            g.memset(neghalf[:], -0.5).then_inc(blank, 1)
            g.memset(xb_pad[:, :, 0:CONV_W - 1], 0.0).then_inc(pad_ready, 1)
            g.iota(iota[:], [[1, P]], base=0, channel_multiplier=0,
                   allow_small_or_imprecise_dtypes=True).then_inc(consts, 1)
            pool.wait_ge(blank, 4)
            g.affine_select(out=ident[:], in_=ident[:], compare_op=ALU.not_equal, fill=1.0, base=0,
                            pattern=[[-1, P]], channel_multiplier=1).then_inc(consts, 1)
            g.affine_select(out=upto[:], in_=ones[:, 0:P], compare_op=ALU.is_ge, fill=0.0, base=0,
                            pattern=[[1, P]], channel_multiplier=-1).then_inc(consts, 1)
            g.affine_select(out=before[:], in_=ones[:, 0:P], compare_op=ALU.is_ge, fill=0.0, base=-1,
                            pattern=[[1, P]], channel_multiplier=-1).then_inc(consts, 1)
            g.affine_select(out=maskf[:], in_=maskf[:], compare_op=ALU.is_ge, fill=NEG, base=0,
                            pattern=[[-1, P]], channel_multiplier=1).then_inc(consts, 1)

            def norm_scale(n):
                pool.wait_ge(sq_act, n + 1)
                pool.wait_ge(sq_dve, n + 1)
                g.tensor_scalar(msq[:, n, :], ss[:, n, :], 1.0 / D, EPS, ALU.mult, ALU.add).then_inc(msq_ready, 1)
                pool.wait_ge(msq_ready, n + 1)
                g.tensor_tensor(rstd[:, n, :], msq[:, n, :], neghalf[:], ALU.pow).then_inc(rstd_ready, 1)

            norm_scale(0)
            for j in range(KD // 2):
                pool.wait_ge(sig_done, 4 * (j + 1))
                part = xc[:, 2 * j:2 * j + 2, :]
                g.tensor_tensor(part, i_sb[:, j % 2, :, :], part, ALU.mult).then_inc(bx_done, 1)
            norm_scale(1)
            norm_scale(2)
            norm_scale(3)
            pool.dma_start(gfin_bc[:], final_norm_g.partition_broadcast(P)).then_inc(gfin_loaded, 16)
            norm_scale(4)

        @block.scalar
        def _(act):
            a = nc.scalar
            for row, src in ((R_NORM, norm_g.rearrange("l s (c p) -> (l s c) p", p=P)),
                             (R_KVN, kv_norm_g.rearrange("(c p) -> c p", p=P)),
                             (R_CB, lru_conv_b[0].rearrange("(c p) -> c p", p=P)),
                             (R_CW, lru_conv_w[0].rearrange("w (c p) -> (w c) p", p=P)),
                             (R_GB, lru_gate_b[0].rearrange("g (c p) -> (g c) p", p=P)),
                             (R_LAM, lru_lambda[0].rearrange("(c p) -> c p", p=P))):
                act.dma_start(rows[row:row + src.shape[0], :], src).then_inc(rows_loaded, 16)
            act.dma_start(gate_w[:, :, :], lru_gate_w[0].rearrange("g n d e -> d (g n) e")).then_inc(gatew_loaded, 16)
            act.dma_start(wf_raw[:], w_kvf.rearrange("(k p) n -> p k n", p=P)[:, :, 2 * D:]).then_inc(smallw_loaded, 16)
            act.dma_start(rt_raw[:], moe_router[0].rearrange("(k p) n -> p k n", p=P)).then_inc(smallw_loaded, 16)
            act.dma_start(bf_col[:], b_f.rearrange("(h o) -> h o", o=1)).then_inc(bf_loaded, 16)

            def split_hi(u, n=0):
                act.wait_ge(raw_full[u % RAW], raw_count(u, n))
                if not (isinstance(n, int) and u + RAW * n < SPL):
                    act.wait_ge(unit_used, units(u, n) - SPL + 1)
                a.activation(w_hi[:, u % SPL, :], raw[:, u % RAW, :], ACT.Copy).then_inc(hi_done, 1)

            def squares(n):
                a.activation(xs[:, 0, :], x[:, 0, :], ACT.Square, accum_out=ss[:, n, 0:1]).then_inc(sq_act, 1)

            def norm_hi(m, gain, hi, lo_before=None):
                for c in range(KD):
                    if lo_before is not None:
                        if c % 2 == 0:
                            act.wait_ge(act_lo_done, lo_before + c + 2)
                    elif c % 2 == 0:
                        act.wait_ge(norm_T, 4 * m + c // 2 + 1)
                    a.activation(hi[:, c, :], bank[c // 2][:, (c % 2) * T:(c % 2 + 1) * T], ACT.Copy,
                                 scale=cols[:, gain + c:gain + c + 1]).then_inc(act_hi_done, 1)

            act.wait_ge(x_loaded, 32)
            squares(0)
            for u in range(LEAD):
                split_hi(u)
            act.wait_ge(lam_abs, 1)
            a.activation(lam_s[:, 1, :], lam_s[:, 0, :], ACT.Exp, scale=-1.0).then_inc(lam_exp, 1)
            act.wait_ge(smallw_loaded, 32)
            a.activation(wf_hi[:], wf_raw[:], ACT.Copy).then_inc(small_hi, 1)
            a.activation(rt_hi[:], rt_raw[:], ACT.Copy).then_inc(small_hi, 1)
            act.wait_ge(cols_ready, 1)
            norm_hi(0, R_NORM, act_hi)

            for k in range(U_FF):
                if 1 <= k <= 4:
                    act.wait_ge(unit_used, k)
                    a.activation(xb_pad[:, 2 * k - 2:2 * k, CONV_W - 1:], bank[4 + (k - 1) % 4][:].rearrange("p (c n) -> p c n", c=2),
                                 ACT.Copy).then_inc(xb_ready, 1)
                def decays(h):
                    act.wait_ge(lam_ready, 1)
                    act.wait_ge(sig_done, 8 * h + 8)
                    for c in range(4 * h, 4 * h + 4):
                        a.activation(xb_pad[:, c, 0:T], th[:, c, :], ACT.Exp, scale=p8ls[:, c:c + 1]).then_inc(decay_done, 1)
                    act.wait_ge(decay_done, 8 * h + 4)
                    for c in range(4 * h, 4 * h + 4):
                        a.activation(th[:, c, :], th[:, c, :], ACT.Tanh, scale=m4ls[:, c:c + 1]).then_inc(decay_done, 1)
                if k == 5:
                    decays(0)
                if 3 <= k <= 6:
                    j = k - 3
                    for c in (2 * j, 2 * j + 1):
                        act.wait_ge(gates_done, c + 1)
                        if j >= 2:
                            act.wait_ge(bx_done, j - 1)
                        a.activation(th[:, c, :], bank[c % 4][:, 0:T], ACT.Sigmoid,
                                     bias=cols[:, R_GB + c:R_GB + c + 1]).then_inc(sig_done, 1)
                        a.activation(i_sb[:, j % 2, c % 2, :], bank[c % 4][:, T:2 * T], ACT.Sigmoid,
                                     bias=cols[:, R_GB + KD + c:R_GB + KD + c + 1]).then_inc(sig_done, 1)
                if k == 6:
                    decays(1)
                if k == 7:
                    act.wait_ge(decay_done, 2 * KD)
                    for h in range(2):
                        a.activation(th[:, 4 * h:4 * h + 4, :], th[:, 4 * h:4 * h + 4, :], ACT.Sqrt).then_inc(sqrt_done, 1)
                if k in (7, 8):
                    for c in range(3) if k == 7 else (3,):
                        act.wait_ge(unit_used, U_GB + c + 1)
                        a.activation(gelu[:, 2 * c:2 * c + 2, :], bank[4 + c][:].rearrange("p (c n) -> p c n", c=2),
                                     ACT.Gelu_apprx_tanh).then_inc(gelu_done, 1)
                if k == 8:
                    for h in range(2):
                        act.wait_ge(yl_ready, 1 + h)
                        a.activation(alt_hi[:, 4 * h:4 * h + 4, :], gelu[:, 4 * h:4 * h + 4, :], ACT.Copy).then_inc(alt_hi_done, 1)
                split_hi(k + LEAD)

            act.wait_ge(x_added, 3)
            squares(1)
            norm_hi(1, R_NORM + KD, act_hi)
            split_hi(U_FF + LEAD)

            def ff_silu(u_gate, n, p, m):
                act.wait_ge(unit_used, units(u_gate, n) + 1)
                if not (isinstance(p, int) and p == 0):
                    act.wait_ge(h_done, p)
                a.activation(silu[:], bank[4 + 2 * (m % 2)][:], ACT.Silu).then_inc(silu_done, 1)

            def ff_hid(p, m):
                act.wait_ge(h_done, p + 1)
                a.activation(hid_hi[:, m % 2, :], hid[:], ACT.Copy).then_inc(hid_hi_done, 1)

            ff_silu(U_FF, 0, 0, 0)
            split_hi(U_FF + 1 + LEAD)
            ff_hid(0, 0)
            split_hi(U_FF + 2 + LEAD)
            with act.Fori(0, (PAIRS - 1) // 2) as i:
                for m in (1, 2):
                    u = U_FF + 3 * m - 1
                    p = 2 * i + m
                    ff_silu(u, i, p, m)
                    split_hi(u + 1 + LEAD, i)
                    act.wait_ge(unit_used, units(u, i))
                    ff_hid(p, m)
                    split_hi(u + 2 + LEAD, i)
                    split_hi(u + 3 + LEAD, i)

            act.wait_ge(x_added, 6)
            squares(2)
            norm_hi(2, R_KVN, alt_hi)
            norm_hi(2, R_NORM + 2 * KD, act_hi, 2 * KD)
            act.wait_ge(f_abs, 1)
            a.activation(f_s[:, 2, :], f_s[:, 1, :], ACT.Exp, scale=-1.0).then_inc(f_exp, 1)
            split_hi(U_K + LEAD)
            for k in range(1, 13):
                if k == 3:
                    act.wait_ge(c_ready, 1)
                    act.wait_ge(c_blank, 2)
                    a.activation(c_pos[0:NHEADS, :], f_s[:, 0, :], ACT.Copy).then_inc(c_hi_done, 1)
                    a.activation(c_neg[0:NHEADS, :], f_s[:, 0, :], ACT.Copy, scale=-1.0).then_inc(c_hi_done, 1)
                if 1 <= k <= 4:
                    act.wait_ge(unit_used, U_K + k)
                    a.activation(k_T[:, 2 * k - 2:2 * k, :], bank[4 + (k - 1) % 2][:].rearrange("p (c n) -> p c n", c=2),
                                 ACT.Copy).then_inc(k_ready, 1)
                if k in (6, 8):
                    half = (k - 6) // 2
                    act.wait_ge(unit_used, U_K + k)
                    for t in range(NT):
                        a.activation(v_sb[:, t, HALF * half:HALF * half + HALF], bank[2 * half + t][:], ACT.Copy).then_inc(v_ready, 1)
                if 9 <= k <= 12:
                    act.wait_ge(unit_used, U_K + k)
                    a.activation(q_T[:, 2 * (k - 9):2 * (k - 9) + 2, :], bank[4 + (k - 9) % 2][:].rearrange("p (c n) -> p c n", c=2),
                                 ACT.Copy, scale=HD ** -0.5).then_inc(q_ready, 1)
                if k < 12:
                    split_hi(U_K + k + LEAD)
            for i in range(NHEADS + 5):
                if i < NHEADS:
                    act.wait_ge(s_ready, i + 1)
                    if i >= PS:
                        act.wait_ge(pt_done, i - PS + 1)
                    for t, cut in enumerate((slice(0, P), slice(P, 3 * P))):
                        a.activation(prob[:, i % PS, cut], bank[i % 2][:, cut], ACT.Exp, bias=negmax[:, i % PS, t:t + 1],
                                     accum_out=psums[:, i % PS, t:t + 1]).then_inc(p_exp, 1)
                if 2 <= i <= NHEADS + 1:
                    h = i - 2
                    act.wait_ge(pt_done, h + 1)
                    if h >= 2:
                        act.wait_ge(pv_done, h - 1)
                    a.activation(prob_T[:, h % 2, :], bank[2 + h % 2][:, 0:3 * P], ACT.Copy).then_inc(pt_ready, 1)
                if i % 4 == 2 and i // 4 < 4:
                    c = i // 4
                    act.wait_ge(unit_used, U_G + c + 1)
                    a.activation(tg[:, 2 * c:2 * c + 2, :], bank[6 + c % 2][:].rearrange("p (c n) -> p c n", c=2),
                                 ACT.Tanh, scale=0.5).then_inc(tg_ready, 1)
                    split_hi(U_G + c + LEAD)
                if i >= 6 and i % 2 == 0:
                    hp = (i - 6) // 2
                    act.wait_ge(o_ready, hp + 1)
                    a.activation(alt_hi[:, hp, :], q_T[:, hp, :], ACT.Copy, scale=0.5).then_inc(alt_hi_done, 1)
            for k in range(4):
                split_hi(U_O + k + LEAD)

            act.wait_ge(x_added, 11)
            squares(3)
            norm_hi(3, R_NORM + 3 * KD, act_hi)
            act.wait_ge(xs_ready, 2 * 3 + 2)
            a.activation(alt_hi[:].rearrange("p c n -> p (c n)"), xs[:].rearrange("p t d -> p (t d)"), ACT.Copy).then_inc(xs_hi_done, 1)
            act.wait_ge(v1_ready, 1)
            for t in range(NT):
                a.activation(route[:, 5, t, :], route[:, 0, t, :], ACT.Exp, bias=rcol[:, 0, t:t + 1]).then_inc(e_ready, 1)

            def tokens_hi(j):
                act.wait_ge(gathered, j + 1)
                for c in range(KD):
                    a.activation(act_hi[:, c // 2, (c % 2) * P:(c % 2 + 1) * P], bank[6 + c // 4][:, (c % 4) * P:(c % 4 + 1) * P],
                                 ACT.Copy, scale=cols[:, R_NORM + 3 * KD + c:R_NORM + 3 * KD + c + 1]).then_inc(tok_hi_done, 1)

            def y_hi_part(j):
                act.wait_ge(unit_used, U_MOE + JU * j)
                act.wait_ge(selT_ready, j + 1)
                for half in range(2):
                    a.activation(y_hi[:, HALF * half:HALF * half + HALF], bank[half][:], ACT.Copy, scale=gslot[:, 0:1]).then_inc(yhi_done, 1)

            tokens_hi(0)
            act.wait_ge(moe_blank, 2)
            act.wait_ge(njobs_ready, 1)
            jobs = act.value_load(njobs[0:1, 0:1], min_val=NE, max_val=2 * NE)
            with act.Fori(0, jobs) as j:
                for k in range(JU):
                    c = (k - 2) // 6 if k >= 2 else 0
                    if k == 0:
                        y_hi_part(j)
                    if k == 2 or (k >= 6 and k % 6 == 0 and k // 6 < CH):
                        c = k // 6
                        act.wait_ge(unit_used, U_MOE + JU * j + k)
                        if c:
                            act.wait_ge(e_h, CH * j + c)
                        a.activation(silu[:], bank[2][:], ACT.Silu).then_inc(e_silu, 1)
                    if (k >= 6 and k % 6 == 0) or k == JU - 3:
                        c = k // 6 - 1 if k < JU - 3 else CH - 1
                        act.wait_ge(e_T, CH * j + c + 1)
                        a.activation(hid_hi[:, c % 2, :], bank[4 + c % 2][:], ACT.Copy).then_inc(e_hid_hi, 1)
                    if k == JU - 2:
                        tokens_hi(j + 1)
                    split_hi(U_MOE + k + LEAD, J6 * j)
            y_hi_part(jobs)
            act.wait_ge(moe_added, 4 * jobs + 4)
            squares(4)

        @block.vector
        def _(dve):
            v = nc.vector
            chain = [0]

            def link(ins):
                chain[0] += 1
                ins.then_inc(link_v, 1)
                dve.wait_ge(link_v, chain[0])

            def split_lo(u, n=0):
                dve.wait_ge(hi_done, units(u, n) + 1)
                v.tensor_tensor(w_lo[:, u % SPL, :], raw[:, u % RAW, :], w_hi[:, u % SPL, :].bitcast(f32),
                                ALU.subtract).then_inc(lo_done, 1)

            def squares(n):
                v.tensor_tensor_reduce(out=xs[:, 1, :], in0=x[:, 1, :], in1=x[:, 1, :], scale=1.0, scalar=0.0,
                                       op0=ALU.mult, op1=ALU.add, accum_out=ss[:, n, 1:2]).then_inc(sq_dve, 1)

            def scale_x(n):
                dve.wait_ge(rstd_ready, n + 1)
                for t in range(NT):
                    v.tensor_scalar(xs[:, t, :], x[:, t, :], rstd[:, n, t:t + 1], None, ALU.mult).then_inc(xs_ready, 1)

            def norm_lo(i, gain, hi, lo):
                for c in range(KD):
                    if c % 2 == 0:
                        dve.wait_ge(act_hi_done, KD * i + c + 2)
                    v.scalar_tensor_tensor(out=lo[:, c, :], in0=bank[c // 2][:, (c % 2) * T:(c % 2 + 1) * T],
                                           scalar=cols[:, gain + c:gain + c + 1], in1=hi[:, c, :].bitcast(f32),
                                           op0=ALU.mult, op1=ALU.subtract).then_inc(act_lo_done, 1)

            def log1p_terms(s, z_min, out_scale, out):
                link(v.tensor_scalar(s(3), s(2), 2.0, None, ALU.add))
                link(v.reciprocal(s(4), s(3)))
                link(v.tensor_tensor(s(3), s(2), s(4), ALU.mult))
                link(v.tensor_tensor(s(4), s(3), s(3), ALU.mult))
                link(v.tensor_scalar(s(5), s(4), 1.0 / 15, None, ALU.mult))
                for n in (13, 11, 9, 7, 5, 3):
                    link(v.scalar_tensor_tensor(out=s(5), in0=s(5), scalar=1.0 / n, in1=s(4), op0=ALU.add, op1=ALU.mult))
                link(v.scalar_tensor_tensor(out=s(5), in0=s(5), scalar=1.0, in1=s(3), op0=ALU.add, op1=ALU.mult))
                link(v.scalar_tensor_tensor(out=s(5), in0=s(5), scalar=-2.0, in1=z_min, op0=ALU.mult, op1=ALU.add))
                return v.tensor_scalar(out, s(5), out_scale, None, ALU.mult)

            def add_to_x(count_sem, banks, halves=(0, 1)):
                for t in range(NT):
                    for half in halves:
                        part = x[:, t, HALF * half:HALF * half + HALF]
                        v.tensor_tensor(part, part, banks(t, half), ALU.add).then_inc(count_sem, 1)

            dve.wait_ge(x_loaded, 32)
            squares(0)
            dve.wait_ge(consts, 5)
            v.tensor_copy(ident_bf[:], ident[:]).then_inc(consts_v, 1)
            v.tensor_copy(mask_bf[:], maskf[:]).then_inc(consts_v, 1)
            link(v.memset(head_1[:].bitcast(i32), 0))
            for row in (0, 32):
                v.tensor_copy(head_1[row:row + NHEADS, :], ident[row:row + NHEADS, row:row + NHEADS]).then_inc(consts_v, 1)
            dve.wait_ge(rows_T, 1)
            link(v.tensor_copy(cols[:], bank[7][:, 0:R_END]))
            lam = cols[:, R_LAM:R_LAM + KD]
            v.scalar_tensor_tensor(out=lam_s[:, 0, :], in0=lam, scalar=-1.0, in1=lam, op0=ALU.mult,
                                   op1=ALU.max).then_inc(lam_abs, 1)
            v.tensor_scalar(lam_s[:, 6, :], lam, 0.0, None, ALU.min).then_inc(cols_ready, 1)
            scale_x(0)
            for u in range(LEAD):
                split_lo(u)
            norm_lo(0, R_NORM, act_hi, act_lo)
            dve.wait_ge(lam_exp, 1)
            link(log1p_terms(lambda n: {2: lam_s[:, 1, :]}.get(n, lam_s[:, n - 1, :]), lam_s[:, 6, :], -LRU_C / 2, m4ls[:]))
            v.tensor_scalar(p8ls[:], m4ls[:], -2.0, None, ALU.mult).then_inc(lam_ready, 1)
            dve.wait_ge(small_hi, 2)
            v.tensor_tensor(wf_lo[:], wf_raw[:], wf_hi[:].bitcast(f32), ALU.subtract).then_inc(small_lo, 1)
            v.tensor_tensor(rt_lo[:], rt_raw[:], rt_hi[:].bitcast(f32), ALU.subtract).then_inc(small_lo, 1)

            dve.wait_ge(pad_ready, 1)
            for k in range(U_FF):
                if 1 <= k <= 4:
                    dve.wait_ge(xb_ready, k)
                    pair = (2 * k - 2, 2 * k - 1)
                    for w in range(CONV_W):
                        for c in pair:
                            tap = cols[:, R_CW + KD * w + c:R_CW + KD * w + c + 1]
                            if w == 0:
                                last = v.tensor_scalar(xc[:, c, :], xb_pad[:, c, 0:T], tap, cols[:, R_CB + c:R_CB + c + 1], ALU.mult, ALU.add)
                            else:
                                last = v.scalar_tensor_tensor(out=xc[:, c, :], in0=xb_pad[:, c, w:w + T], scalar=tap,
                                                              in1=xc[:, c, :], op0=ALU.mult, op1=ALU.add)
                            if w == CONV_W - 1:
                                last.then_inc(xc_ready, 1)
                        if w < CONV_W - 1:
                            link(last)
                if k == 7:
                    for h in range(2):
                        part = slice(4 * h, 4 * h + 4)
                        dve.wait_ge(sqrt_done, h + 1)
                        dve.wait_ge(bx_done, 2 * h + 2)
                        link(v.scalar_tensor_tensor(out=rc[:, part, :], in0=xb_pad[:, part, 0:T], scalar=1.0, in1=th[:, part, :],
                                                    op0=ALU.add, op1=ALU.mult))
                        link(v.tensor_tensor(xc[:, part, :], rc[:, part, :], xc[:, part, :], ALU.mult))
                        for c in range(4 * h, 4 * h + 4):
                            last = v.tensor_tensor_scan(rc[:, c, :], xb_pad[:, c, 0:T], xc[:, c, :], 0.0, ALU.mult, ALU.add)
                        link(last)
                if k == 8:
                    for h in range(2):
                        part = slice(4 * h, 4 * h + 4)
                        dve.wait_ge(gelu_done, 2 * h + 2)
                        v.tensor_tensor(gelu[:, part, :], gelu[:, part, :], rc[:, part, :], ALU.mult).then_inc(yl_ready, 1)
                    for h in range(2):
                        part = slice(4 * h, 4 * h + 4)
                        dve.wait_ge(alt_hi_done, h + 1)
                        v.tensor_tensor(alt_lo[:, part, :], gelu[:, part, :], alt_hi[:, part, :].bitcast(f32), ALU.subtract).then_inc(alt_lo_done, 1)
                if k == 10:
                    dve.wait_ge(unit_used, U_OUT + 2)
                    add_to_x(x_added, lambda t, half: bank[2 * half + t][:], (0,))
                split_lo(k + LEAD)
            dve.wait_ge(unit_used, U_OUT + 4)
            add_to_x(x_added, lambda t, half: bank[2 * half + t][:], (1,))

            dve.wait_ge(x_added, 4)
            squares(1)
            scale_x(1)
            norm_lo(1, R_NORM + KD, act_hi, act_lo)
            split_lo(U_FF + LEAD)
            split_lo(U_FF + 1 + LEAD)

            def ff_hid(u_up, n, p, m):
                dve.wait_ge(silu_done, p + 1)
                dve.wait_ge(unit_used, units(u_up, n) + 1)
                if not (isinstance(p, int) and p == 0):
                    dve.wait_ge(hid_lo_done, p)
                v.tensor_tensor(hid[:], silu[:], bank[5 + 2 * (m % 2)][:], ALU.mult).then_inc(h_done, 1)
                dve.wait_ge(hid_hi_done, p + 1)
                v.tensor_tensor(hid_lo[:, m % 2, :], hid[:], hid_hi[:, m % 2, :].bitcast(f32), ALU.subtract).then_inc(hid_lo_done, 1)

            ff_hid(U_FF + 1, 0, 0, 0)
            split_lo(U_FF + 2 + LEAD)
            with dve.Fori(0, (PAIRS - 1) // 2) as i:
                for m in (1, 2):
                    u = U_FF + 3 * m - 1
                    split_lo(u + 1 + LEAD, i)
                    ff_hid(u + 1, i, 2 * i + m, m)
                    split_lo(u + 2 + LEAD, i)
                    split_lo(u + 3 + LEAD, i)
            dve.wait_ge(unit_used, U_K)
            add_to_x(x_added, lambda t, half: bank[2 * half + t][:])

            dve.wait_ge(x_added, 8)
            squares(2)
            scale_x(2)
            norm_lo(2, R_KVN, alt_hi, alt_lo)
            norm_lo(3, R_NORM + 2 * KD, act_hi, act_lo)
            v.memset(c_pos[:].bitcast(i32), 0).then_inc(c_blank, 1)
            v.memset(c_neg[:].bitcast(i32), 0).then_inc(c_blank, 1)
            dve.wait_ge(f_done, 1)
            dve.wait_ge(bf_loaded, 16)
            link(v.tensor_scalar(f_s[:, 0, :], bank[6][0:NHEADS, 0:T], bf_col[:, 0:1], None, ALU.add))
            v.scalar_tensor_tensor(out=f_s[:, 1, :], in0=f_s[:, 0, :], scalar=-1.0, in1=f_s[:, 0, :], op0=ALU.mult,
                                   op1=ALU.max).then_inc(f_abs, 1)
            link(v.tensor_scalar(f_s[:, 6, :], f_s[:, 0, :], 0.0, None, ALU.min))
            split_lo(U_K + LEAD)
            dve.wait_ge(f_exp, 1)
            link(log1p_terms(lambda n: f_s[:, n, :], f_s[:, 6, :], 1.0, f_s[:, 7, :]))
            v.tensor_tensor_scan(f_s[:, 0, :], ones[0:NHEADS, :], f_s[:, 7, :], 0.0, ALU.mult, ALU.add).then_inc(c_ready, 1)
            for k in range(1, 12):
                if k == 3:
                    dve.wait_ge(c_hi_done, 2)
                    v.tensor_tensor(c_pos[32:32 + NHEADS, :], f_s[:, 0, :], c_pos[0:NHEADS, :].bitcast(f32), ALU.subtract).then_inc(c_lo_done, 1)
                    v.tensor_tensor(c_neg[32:32 + NHEADS, :], c_pos[0:NHEADS, :].bitcast(f32), f_s[:, 0, :], ALU.subtract).then_inc(c_lo_done, 1)
                split_lo(U_K + k + LEAD)

            for i in range(NHEADS + 5):
                if i < NHEADS:
                    dve.wait_ge(s_done, i + 1)
                    for t, cut in enumerate((slice(0, P), slice(P, 3 * P))):
                        last = v.tensor_reduce(negmax[:, i % PS, t:t + 1], bank[i % 2][:, cut], AX.X, ALU.max, negate=True)
                    last.then_inc(s_ready, 1)
                if 1 <= i <= NHEADS:
                    b = (i - 1) % PS
                    dve.wait_ge(p_exp, 2 * i)
                    link(v.reciprocal(pinv[:, b, :], psums[:, b, :]))
                    v.tensor_scalar(prob[:, b, 0:P], prob[:, b, 0:P], pinv[:, b, 0:1], None, ALU.mult)
                    v.tensor_scalar(prob[:, b, P:3 * P], prob[:, b, P:3 * P], pinv[:, b, 1:2], None, ALU.mult).then_inc(p_norm, 1)
                if i % 4 == 0 and 4 <= i <= 16:
                    split_lo(U_G + i // 4 - 1 + LEAD)
                if i >= 5 and i % 2 == 1:
                    hp = (i - 5) // 2
                    dve.wait_ge(pv_done, 2 * hp + 2)
                    dve.wait_ge(tg_ready, hp // 2 + 1)
                    v.scalar_tensor_tensor(out=q_T[:, hp, :], in0=tg[:, hp, :], scalar=1.0, in1=bank[4 + hp % 2][:, 0:T],
                                           op0=ALU.add, op1=ALU.mult).then_inc(o_ready, 1)
                if i >= 6 and i % 2 == 0:
                    hp = (i - 6) // 2
                    dve.wait_ge(alt_hi_done, 2 + hp + 1)
                    v.scalar_tensor_tensor(out=alt_lo[:, hp, :], in0=q_T[:, hp, :], scalar=0.5, in1=alt_hi[:, hp, :].bitcast(f32),
                                           op0=ALU.mult, op1=ALU.subtract).then_inc(alt_lo_done, 1)
            for k in range(4):
                if k == 2:
                    dve.wait_ge(unit_used, U_O + 2)
                    add_to_x(x_added, lambda t, half: bank[2 * half + t][:], (0,))
                split_lo(U_O + k + LEAD)
            dve.wait_ge(unit_used, U_O + 4)
            add_to_x(x_added, lambda t, half: bank[2 * half + t][:], (1,))

            dve.wait_ge(x_added, 12)
            squares(3)
            scale_x(3)
            norm_lo(4, R_NORM + 3 * KD, act_hi, act_lo)
            dve.wait_ge(xs_hi_done, 1)
            v.tensor_tensor(alt_lo[:].rearrange("p c n -> p (c n)"), xs[:].rearrange("p t d -> p (t d)"),
                            alt_hi[:].rearrange("p c n -> p (c n)").bitcast(f32), ALU.subtract).then_inc(src_ready, 1)
            LOG, GT, EQ, MASK, INC, EXP, GATE, OFF = range(8)
            both = lambda n: route[:, n, :, :]

            def per_token(col):
                return col.to_broadcast([P, NT, NE])

            dve.wait_ge(logits_done, 1)
            v.tensor_copy(logit_T[:], bank[4][0:NE, 0:T]).then_inc(logitT_ready, 1)
            dve.wait_ge(logits_done, 2)
            link(v.tensor_copy(both(LOG), bank[5][:, 0:NT * NE].rearrange("p (t e) -> p t e", t=NT)))
            for t in range(NT):
                last = v.max(top8[:, t, :], route[:, LOG, t, :])
            link(last)
            v.tensor_scalar(rcol[:, 0, :], top8[:, :, 0], -1.0, None, ALU.mult).then_inc(v1_ready, 1)
            v.tensor_tensor(both(GT), both(LOG), per_token(top8[:, :, 1:2]), ALU.is_gt)
            link(v.tensor_tensor(both(EQ), both(LOG), per_token(top8[:, :, 1:2]), ALU.is_equal))
            for t in range(NT):
                v.tensor_tensor_scan(route[:, INC, t, :], ones[:, 0:NE], route[:, EQ, t, :], 0.0, ALU.mult, ALU.add)
            link(v.tensor_reduce(rcol[:, 1, :], both(GT), AX.X, ALU.add))
            link(v.tensor_scalar(rcol[:, 2, :], rcol[:, 1, :], -1.0, 2.0, ALU.mult, ALU.add))
            for t in range(NT):
                last = v.scalar_tensor_tensor(out=route[:, INC, t, :], in0=route[:, INC, t, :], scalar=rcol[:, 2, t:t + 1],
                                              in1=route[:, EQ, t, :], op0=ALU.is_le, op1=ALU.mult)
            link(last)
            v.tensor_tensor(both(MASK), both(INC), both(GT), ALU.add).then_inc(mask_ready, 1)
            dve.wait_ge(mask_ready, 1)
            v.tensor_scalar(both(OFF), both(MASK), 1000.0, -1000.0, ALU.mult, ALU.add)
            v.memset(gate_of[:, :, 2 * NE:], 0.0)
            v.memset(slot_of[:, :, 2 * NE:], -1000.0)
            dve.wait_ge(e_ready, 2)
            link(v.tensor_tensor(both(GATE), both(EXP), both(MASK), ALU.mult))
            link(v.tensor_reduce(rcol[:, 3, :], both(GATE), AX.X, ALU.add))
            link(v.reciprocal(rcol[:, 1, :], rcol[:, 3, :]))
            for t in range(NT):
                for first in (0, NE):
                    v.tensor_scalar(gate_of[:, t, first:first + NE], route[:, GATE, t, :], rcol[:, 1, t:t + 1], None, ALU.mult)
            dve.wait_ge(rank_done, 1)
            link(v.tensor_tensor(slot_of[:, :, 0:NE], both(OFF), bank[5][:, 0:NT * NE].rearrange("p (t e) -> p t e", t=NT), ALU.add))
            link(v.tensor_scalar(slot_of[:, :, NE:2 * NE], slot_of[:, :, 0:NE], float(P), None, ALU.subtract))
            link(v.tensor_reduce(njobs_f[:, 0:1], bank[5][:, NT * NE:NT * NE + NE], AX.X, ALU.max))
            link(v.tensor_scalar(njobs_f[:, 1:2], njobs_f[:, 0:1], float(P), float(NE), ALU.is_gt, ALU.mult))
            v.tensor_scalar(njobs[:], njobs_f[:, 1:2], float(NE), None, ALU.add).then_inc(njobs_ready, 1)

            def build_sel(j):
                for t in range(NT):
                    slot, gate = slot_of[:, t, bass.ds(j, 1)], gate_of[:, t, bass.ds(j, 1)]
                    v.tensor_scalar(sel[:, t, :], iota[:], slot, None, ALU.is_equal)
                    last = v.tensor_scalar(sel_g[:, t, :], iota[:], slot, gate, ALU.is_equal, ALU.mult)
                last.then_inc(sel_built, 1)

            def tokens_lo(j):
                for c in range(KD):
                    if c % 4 == 0:
                        dve.wait_ge(tok_hi_done, KD * j + c + 4)
                    part = (slice(None), c // 2, slice((c % 2) * P, (c % 2 + 1) * P))
                    v.scalar_tensor_tensor(out=act_lo[part], in0=bank[6 + c // 4][:, (c % 4) * P:(c % 4 + 1) * P],
                                           scalar=cols[:, R_NORM + 3 * KD + c:R_NORM + 3 * KD + c + 1],
                                           in1=act_hi[part].bitcast(f32), op0=ALU.mult, op1=ALU.subtract).then_inc(tok_lo_done, 1)

            def y_lo_part(j):
                for half in range(2):
                    dve.wait_ge(yhi_done, 2 * j + half + 1)
                    cut = slice(HALF * half, HALF * half + HALF)
                    v.scalar_tensor_tensor(out=y_lo[:, cut], in0=bank[half][:], scalar=gslot[:, 0:1],
                                           in1=y_hi[:, cut].bitcast(f32), op0=ALU.mult, op1=ALU.subtract).then_inc(ylo_done, 1)

            def add_scattered(j):
                for half in range(2):
                    for t in range(NT):
                        dve.wait_ge(scattered, 4 * j + 2 * half + t + 1)
                        part = x[:, t, HALF * half:HALF * half + HALF]
                        v.tensor_tensor(part, part, bank[4 + 2 * half + t][:], ALU.add).then_inc(moe_added, 1)

            build_sel(0)
            v.memset(sel_T[:].bitcast(i32), 0)
            v.memset(gslot[:], 0.0).then_inc(selT_ready, 1)
            v.memset(bank[0][:], 0.0).then_inc(moe_blank, 1)
            v.memset(bank[1][:], 0.0).then_inc(moe_blank, 1)
            tokens_lo(0)
            jobs = dve.value_load(njobs[0:1, 0:1], min_val=NE, max_val=2 * NE)
            with dve.Fori(0, jobs) as j:
                for k in range(JU):
                    if k == 0:
                        y_lo_part(j)
                    if k == 4 or (k >= 8 and k % 6 == 2 and k // 6 < CH):
                        c = 0 if k == 4 else k // 6
                        dve.wait_ge(e_silu, CH * j + c + 1)
                        dve.wait_ge(unit_used, U_MOE + JU * j + k)
                        if c:
                            dve.wait_ge(e_T, CH * j + c)
                        v.tensor_tensor(hid[:], silu[:], bank[3][:], ALU.mult).then_inc(e_h, 1)
                    if k == 5:
                        add_scattered(j)
                    if (k >= 6 and k % 6 == 0) or k == JU - 3:
                        c = k // 6 - 1 if k < JU - 3 else CH - 1
                        dve.wait_ge(e_hid_hi, CH * j + c + 1)
                        v.tensor_tensor(hid_lo[:, c % 2, :], bank[4 + c % 2][:], hid_hi[:, c % 2, :].bitcast(f32),
                                        ALU.subtract).then_inc(e_hid_lo, 1)
                    if k == 9:
                        dve.wait_ge(selg_T, j + 1)
                        v.tensor_reduce(gslot[:], bank[6][:, 0:T], AX.X, ALU.add)
                        v.tensor_scalar(sel_T[:], bank[6][:, 0:T], 0.0, None, ALU.is_gt).then_inc(selT_ready, 1)
                    if k == 20:
                        build_sel(j + 1)
                    if k == JU - 2:
                        tokens_lo(j + 1)
                    split_lo(U_MOE + k + LEAD, J6 * j)
            y_lo_part(jobs)
            add_scattered(jobs)
            dve.wait_ge(moe_added, 4 * jobs + 4)
            squares(4)
            dve.wait_ge(rstd_ready, 5)
            dve.wait_ge(gfin_loaded, 16)
            for t in range(NT):
                v.scalar_tensor_tensor(out=xs[:, t, :], in0=x[:, t, :], scalar=rstd[:, 4, t:t + 1], in1=gfin_bc[:],
                                       op0=ALU.mult, op1=ALU.mult).then_inc(out_ready, 1)

        @block.tensor
        def _(pe):
            t_ = nc.tensor

            def mm3(dst, l_hi, l_lo, r_hi, r_lo, start, stop):
                t_.matmul(dst, l_lo, r_hi, start=start, stop=False)
                t_.matmul(dst, l_hi, r_lo, start=False, stop=False)
                return t_.matmul(dst, l_hi, r_hi, start=False, stop=stop)

            def unit_ready(u, n=0):
                pe.wait_ge(lo_done, units(u, n) + 1)

            def stationary_unit(u, n, a_hi, a_lo, dst, first_count=None):
                unit_ready(u, n)
                for f in range(2):
                    for k in range(KD):
                        if first_count is not None and f == 0:
                            pe.wait_ge(act_lo_done, first_count + k + 1)
                        w = slice(k * 256 + f * P, k * 256 + f * P + P)
                        last = mm3(dst[:, f * T:(f + 1) * T], w_hi[:, u % SPL, w], w_lo[:, u % SPL, w],
                                   a_hi[:, k, :], a_lo[:, k, :], k == 0, k == KD - 1)
                last.then_inc(unit_used, 1)

            def moving_unit(u, a_hi, a_lo, k_half, dst, before_k=None):
                unit_ready(u)
                for k in range(4):
                    kk = 4 * k_half + k
                    if before_k:
                        before_k(kk)
                    for t in range(NT):
                        w = slice(k * 512, k * 512 + 512)
                        last = mm3(dst[t][:], a_hi[:, kk, t * P:(t + 1) * P], a_lo[:, kk, t * P:(t + 1) * P],
                                   w_hi[:, u % SPL, w], w_lo[:, u % SPL, w], kk == 0, kk == KD - 1)
                last.then_inc(unit_used, 1)

            def transpose_x(n):
                for t in range(NT):
                    pe.wait_ge(xs_ready, 2 * n + t + 1)
                    for c in range(KD):
                        dst = bank[c // 2][:, (c % 2) * T + t * P:(c % 2) * T + (t + 1) * P]
                        last = t_.transpose(dst, xs[:, t, c * P:(c + 1) * P], ident[:])
                        if t == NT - 1 and c % 2:
                            last.then_inc(norm_T, 1)

            pe.wait_ge(rows_loaded, 6 * 16)
            pe.wait_ge(consts, 5)
            t_.transpose(bank[7][:, 0:R_END], rows[0:R_END, :], ident[0:R_END, 0:R_END]).then_inc(rows_T, 1)

            transpose_x(0)
            pe.wait_ge(gatew_loaded, 16)
            pe.wait_ge(cols_ready, 1)

            def lru_gates(c):
                pe.wait_ge(xc_ready, c + 1)
                if c >= 4:
                    pe.wait_ge(sig_done, 2 * (c - 4) + 2)
                else:
                    pe.wait_ge(act_lo_done, KD)
                for g in range(2):
                    last = t_.matmul(bank[c % 4][:, g * T:(g + 1) * T], gate_w[:, g * KD + c, :], xc[:, c, :], start=True, stop=True)
                last.then_inc(gates_done, 1)

            for u in range(8):
                if u >= 4:
                    pe.wait_ge(xb_ready, u - 3)
                stationary_unit(u, 0, act_hi, act_lo, bank[4 + u % 4], 0 if u == 0 else None)
                if 2 <= u <= 5:
                    lru_gates(2 * u - 4)
                    lru_gates(2 * u - 3)
            pe.wait_ge(sig_done, 2 * KD)
            for c in range(4):
                moving_unit(U_OUT + c, alt_hi, alt_lo, c % 2, [bank[2 * (c // 2)], bank[2 * (c // 2) + 1]],
                            (lambda kk: pe.wait_ge(alt_lo_done, kk // 4 + 1)) if c < 2 else None)

            pe.wait_ge(x_added, 4)
            pe.wait_ge(gelu_done, 4)
            transpose_x(1)

            def ff_gate_up(u, n, m, first_count=None):
                stationary_unit(u, n, act_hi, act_lo, bank[4 + 2 * (m % 2)], first_count)
                stationary_unit(u + 1, n, act_hi, act_lo, bank[5 + 2 * (m % 2)])

            def ff_down(u, n, p, m, first, last_one):
                unit_ready(u, n)
                pe.wait_ge(hid_lo_done, p + 1)
                for k in range(2):
                    for t in range(NT):
                        h = slice(k * T + t * P, k * T + (t + 1) * P)
                        for half in range(2):
                            w = slice(k * D + half * HALF, k * D + half * HALF + HALF)
                            last = mm3(bank[2 * half + t][:], hid_hi[:, m % 2, h], hid_lo[:, m % 2, h],
                                       w_hi[:, u % SPL, w], w_lo[:, u % SPL, w], first and k == 0, last_one and k == 1)
                last.then_inc(unit_used, 1)

            ff_gate_up(U_FF, 0, 0, KD)
            ff_gate_up(U_FF + 2, 0, 1)
            pe.wait_ge(act_lo_done, 2 * KD)
            ff_down(U_FF + 4, 0, 0, 0, True, False)
            with pe.Fori(0, (PAIRS - 3) // 2) as i:
                for m in (2, 3):
                    u = U_FF + 3 * m - 1
                    pe.wait_ge(h_done, 2 * i + m - 1)
                    ff_gate_up(u, i, m)
                    ff_down(u + 2, i, 2 * i + m - 1, m - 1, False, False)
            u = U_FF + 3 * (PAIRS - 1) - 1
            pe.wait_ge(h_done, PAIRS - 2)
            ff_gate_up(u, 0, PAIRS - 1)
            ff_down(u + 2, 0, PAIRS - 2, PAIRS - 2, False, False)
            ff_down(u + 3, 0, PAIRS - 1, PAIRS - 1, False, True)

            pe.wait_ge(x_added, 8)
            transpose_x(2)
            pe.wait_ge(small_lo, 2)
            pe.wait_ge(act_lo_done, 3 * KD)
            for k in range(KD):
                last = mm3(bank[6][0:NHEADS, 0:T], wf_hi[:, k, :], wf_lo[:, k, :], alt_hi[:, k, :], alt_lo[:, k, :], k == 0, k == KD - 1)
            last.then_inc(f_done, 1)
            for c in range(4):
                if c >= 2:
                    pe.wait_ge(k_ready, c - 1)
                stationary_unit(U_K + c, 0, alt_hi, alt_lo, bank[4 + c % 2])
            pe.wait_ge(act_lo_done, 4 * KD)
            for c in range(4):
                moving_unit(U_V + c, alt_hi, alt_lo, c % 2, [bank[2 * (c // 2)], bank[2 * (c // 2) + 1]])
            for c in range(4):
                pe.wait_ge(k_ready if c < 2 else q_ready, 3 + c if c < 2 else c - 1)
                stationary_unit(U_Q + c, 0, act_hi, act_lo, bank[4 + c % 2])

            pe.wait_ge(v_ready, 4)
            pe.wait_ge(consts_v, 4)
            pe.wait_ge(c_lo_done, 2)
            for i in range(NHEADS + 3):
                if i < NHEADS:
                    rows_h = slice(HD * (i % 2), HD * (i % 2) + HD)
                    hp = i // 2
                    if i % 4 == 0:
                        pe.wait_ge(q_ready, i // 4 + 1)
                    if i >= 2:
                        pe.wait_ge(p_exp, 2 * (i - 2) + 2)
                    for t in range(NT):
                        keys, queries = slice(0, P * (t + 1)), slice(P * t, P * (t + 1))
                        dst = bank[i % 2][:, P * t:P * t + P * (t + 1)]
                        head = head_1[:, i:i + 1]
                        t_.matmul(dst, c_pos[:, queries], head.to_broadcast([P, P * (t + 1)]), start=True, stop=False)
                        t_.matmul(dst, head.to_broadcast([P, P]), c_neg[:, keys], start=False, stop=False)
                        t_.matmul(bank[i % 2][:, 2 * P * t:2 * P * t + P], ident_bf[:], mask_bf[:], start=False, stop=False)
                        last = t_.matmul(dst, q_T[rows_h, hp, queries], k_T[rows_h, hp, keys], start=False, stop=True)
                    last.then_inc(s_done, 1)
                if i % 4 == 1 and i // 4 < 4:
                    c = i // 4
                    if c >= 2:
                        pe.wait_ge(tg_ready, c - 1)
                    stationary_unit(U_G + c, 0, act_hi, act_lo, bank[6 + c % 2])
                if 2 <= i <= NHEADS + 1:
                    h = i - 2
                    pe.wait_ge(p_norm, h + 1)
                    if h >= 2:
                        pe.wait_ge(pt_ready, h - 1)
                    for n in range(3):
                        last = t_.transpose(bank[2 + h % 2][:, n * P:(n + 1) * P], prob[:, h % PS, n * P:(n + 1) * P], ident[:])
                    last.then_inc(pt_done, 1)
                if i >= 3:
                    h = i - 3
                    hp = h // 2
                    pe.wait_ge(pt_ready, h + 1)
                    if h % 2 == 0 and hp >= 2:
                        pe.wait_ge(o_ready, hp - 1)
                    o = bank[4 + hp % 2][HD * (h % 2):HD * (h % 2) + HD, :]
                    t_.matmul(o[:, 0:T], v_sb[:, 0, h * HD:(h + 1) * HD], prob_T[:, h % 2, 0:T], start=True, stop=False)
                    t_.matmul(o[:, P:T], v_sb[:, 1, h * HD:(h + 1) * HD], prob_T[:, h % 2, T:3 * P], start=False, stop=True).then_inc(pv_done, 1)
            for c in range(4):
                moving_unit(U_O + c, alt_hi, alt_lo, c % 2, [bank[2 * (c // 2)], bank[2 * (c // 2) + 1]],
                            (lambda kk: pe.wait_ge(alt_lo_done, 2 + kk + 1)) if c < 2 else None)

            pe.wait_ge(x_added, 12)
            transpose_x(3)
            pe.wait_ge(act_lo_done, 5 * KD)
            for k in range(KD):
                last = mm3(bank[4][0:NE, 0:T], rt_hi[:, k, :], rt_lo[:, k, :], act_hi[:, k, :], act_lo[:, k, :], k == 0, k == KD - 1)
            last.then_inc(logits_done, 1)
            pe.wait_ge(logitT_ready, 1)
            for t in range(NT):
                last = t_.transpose(bank[5][:, t * NE:(t + 1) * NE], logit_T[:, t * P:(t + 1) * P], ident[0:NE, 0:NE])
            last.then_inc(logits_done, 1)
            pe.wait_ge(mask_ready, 1)
            m0, m1 = route[:, 3, 0, :], route[:, 3, 1, :]
            t_.matmul(bank[5][:, 0:NE], before[:], m0, start=True, stop=True)
            t_.matmul(bank[5][:, NE:2 * NE], ones[:, 0:P], m0, start=True, stop=False)
            t_.matmul(bank[5][:, NE:2 * NE], before[:], m1, start=False, stop=True)
            t_.matmul(bank[5][:, 2 * NE:3 * NE], ones[:, 0:P], m0, start=True, stop=False)
            t_.matmul(bank[5][:, 2 * NE:3 * NE], ones[:, 0:P], m1, start=False, stop=True).then_inc(rank_done, 1)

            src_hi = alt_hi[:].rearrange("p c n -> p (c n)")
            src_lo = alt_lo[:].rearrange("p c n -> p (c n)")

            def gather():
                for c in range(KD):
                    dst = bank[6 + c // 4][:, (c % 4) * P:(c % 4 + 1) * P]
                    for t in range(NT):
                        w = slice(t * D + c * P, t * D + (c + 1) * P)
                        t_.matmul(dst, src_lo[:, w], sel[:, t, :], start=(t == 0), stop=False)
                        last = t_.matmul(dst, src_hi[:, w], sel[:, t, :], start=False, stop=(t == NT - 1))
                last.then_inc(gathered, 1)

            def scatter(j):
                pe.wait_ge(ylo_done, 2 * j + 2)
                for half in range(2):
                    w = slice(HALF * half, HALF * half + HALF)
                    for t in range(NT):
                        dst = bank[4 + 2 * half + t][:]
                        t_.matmul(dst, sel_T[:, t * P:(t + 1) * P], y_lo[:, w], start=True, stop=False)
                        t_.matmul(dst, sel_T[:, t * P:(t + 1) * P], y_hi[:, w], start=False, stop=True).then_inc(scattered, 1)

            def expert_in(u, n, dst, k_half):
                unit_ready(u, n)
                for k in range(4):
                    kk = 4 * k_half + k
                    s = (slice(None), kk // 2, slice((kk % 2) * P, (kk % 2 + 1) * P))
                    w = slice(k * 512, k * 512 + 512)
                    last = mm3(dst[:], act_hi[s], act_lo[s], w_hi[:, u % SPL, w], w_lo[:, u % SPL, w], kk == 0, kk == KD - 1)
                last.then_inc(unit_used, 1)

            def expert_out(u, n, c, k_half):
                unit_ready(u, n)
                for k in range(2):
                    h = slice((2 * k_half + k) * P, (2 * k_half + k + 1) * P)
                    for half in range(2):
                        w = slice(k * D + half * HALF, k * D + half * HALF + HALF)
                        first, final = c == 0 and k_half == 0 and k == 0, c == CH - 1 and k_half == 1 and k == 1
                        last = mm3(bank[half][:], hid_hi[:, c % 2, h], hid_lo[:, c % 2, h],
                                   w_hi[:, u % SPL, w], w_lo[:, u % SPL, w], first, final)
                last.then_inc(unit_used, 1)

            def hidden_T(j, c):
                pe.wait_ge(e_h, CH * j + c + 1)
                for n in range(4):
                    last = t_.transpose(bank[4 + c % 2][:, n * P:(n + 1) * P], hid[:, n * P:(n + 1) * P], ident[:])
                last.then_inc(e_T, 1)

            pe.wait_ge(src_ready, 1)
            pe.wait_ge(sel_built, 1)
            gather()
            pe.wait_ge(njobs_ready, 1)
            jobs = pe.value_load(njobs[0:1, 0:1], min_val=NE, max_val=2 * NE)
            with pe.Fori(0, jobs) as j:
                n = J6 * j
                pe.wait_ge(tok_lo_done, KD * j + KD)
                for c in range(CH):
                    u = U_MOE + (6 * c - 2 if c else 0)
                    if c:
                        pe.wait_ge(e_silu, CH * j + c)
                    expert_in(u, n, bank[2], 0)
                    expert_in(u + 1, n, bank[2], 1)
                    if c == 1:
                        pe.wait_ge(moe_added, 4 * j + 4)
                    if c:
                        hidden_T(j, c - 1)
                    expert_in(u + 2, n, bank[3], 0)
                    expert_in(u + 3, n, bank[3], 1)
                    if c == 0:
                        scatter(j)
                    if c == 1:
                        for t in range(NT):
                            last = t_.transpose(bank[6][:, t * P:(t + 1) * P], sel_g[:, t, :], ident[:])
                        last.then_inc(selg_T, 1)
                    if c:
                        pe.wait_ge(e_hid_lo, CH * j + c)
                        expert_out(u + 4, n, c - 1, 0)
                        if c == CH - 1:
                            hidden_T(j, c)
                            pe.wait_ge(sel_built, j + 2)
                            pe.wait_ge(selT_ready, j + 2)
                            gather()
                        expert_out(u + 5, n, c - 1, 1)
                pe.wait_ge(e_hid_lo, CH * j + CH)
                expert_out(U_MOE + JU - 2, n, CH - 1, 0)
                expert_out(U_MOE + JU - 1, n, CH - 1, 1)
            pe.wait_ge(tok_lo_done, KD * jobs + KD)
            scatter(jobs)


_INS = ["x", "norm_g", "lru_w_in", "lru_conv_w", "lru_conv_b", "lru_gate_w", "lru_gate_b", "lru_lambda", "lru_w_out",
        "kv_norm_g", "w_kvf", "b_f", "fox_w_qg", "fox_w_o", "mlp_w_gu", "mlp_w_down", "moe_router", "moe_w_gu",
        "moe_w_down", "final_norm_g"]


def kernel(**inputs):
    import numpy as _np
    import concourse.bacc as _bacc
    from concourse.bass_utils import run_bass_kernel_spmd as _run

    nc = _bacc.Bacc("TRN2", target_bir_lowering=False, num_devices=1)
    arrays, args = {}, []
    for name in _INS:
        a = _np.ascontiguousarray(inputs[name])
        arrays[f"in_{name}"] = a
        args.append(nc.dram_tensor(f"in_{name}", a.shape, mybir.dt.from_np(a.dtype), kind="ExternalInput").ap())
    out = nc.dram_tensor("out_0", (1, T, D), mybir.dt.float32, kind="ExternalOutput").ap()
    yoco_kernel(nc, *args, out)
    r = _run(nc, [arrays], core_ids=[0])
    return r.results[0]["out_0"]
```

```python
from contextlib import ExitStack

import concourse.bass as bass
from concourse import mybir

P = 128
D = 1024
T = 256
NT = T // P
KD = D // P
NHEADS = 16
HD = D // NHEADS
D_FF = 2816
D_EXP = 3584
NE = 8
EPS = 1e-6
LRU_C = 8.0
CONV_W = 4
NEG = -1e30

UW = 2048
RAW = 6
SPL = 3
LEAD = SPL - 1
HALF = D // 2
PS = 3

U_XB, U_GB, U_OUT = 0, 4, 8
PAIRS = D_FF // (2 * P)
U_FF = 12
U_K = U_FF + 3 * PAIRS
U_V, U_Q, U_G, U_O = U_K + 4, U_K + 8, U_K + 12, U_K + 16
U_MOE = U_O + 4
CH = D_EXP // 512
JU = 6 * CH
J6 = JU // RAW

R_NORM, R_KVN, R_CB, R_CW, R_GB, R_LAM, R_END = 0, 32, 40, 48, 80, 96, 104
SLOT_COLS = 2 * NE + 1


def yoco_kernel(nc, x_in, norm_g, lru_w_in, lru_conv_w, lru_conv_b, lru_gate_w, lru_gate_b, lru_lambda,
                lru_w_out, kv_norm_g, w_kvf, b_f, fox_w_qg, fox_w_o, mlp_w_gu, mlp_w_down,
                moe_router, moe_w_gu, moe_w_down, final_norm_g, out):
    f32, f32r, bf16, i32 = mybir.dt.float32, mybir.dt.float32r, mybir.dt.bfloat16, mybir.dt.int32
    ALU, ACT, AX = mybir.AluOpType, mybir.ActivationFunctionType, mybir.AxisListType

    ctx = ExitStack()
    with ctx:
        def sb(name, shape, dt=f32, into=ctx):
            return into.enter_context(nc.sbuf_tensor(name, shape, dt))

        def sem(name):
            return ctx.enter_context(nc.semaphore(name))

        raw = sb("raw", [P, RAW, UW])
        w_hi = sb("w_hi", [P, SPL, UW], f32r)
        w_lo = sb("w_lo", [P, SPL, UW], f32r)
        act_hi = sb("act_hi", [P, KD, T], f32r)
        act_lo = sb("act_lo", [P, KD, T], f32r)
        alt_hi = sb("alt_hi", [P, KD, T], f32r)
        alt_lo = sb("alt_lo", [P, KD, T], f32r)
        x = sb("x", [P, NT, D])
        xs = sb("xs", [P, NT, D])
        ident = sb("ident", [P, P])
        ident_bf = sb("ident_bf", [P, P], bf16)
        ones = sb("ones", [P, T])
        upto = sb("upto", [P, P])
        before = sb("before", [P, P])
        maskf = sb("maskf", [P, P])
        mask_bf = sb("mask_bf", [P, P], bf16)
        iota = sb("iota", [P, P])
        rows = sb("rows", [P, P])
        cols = sb("cols", [P, R_END])
        wf_raw = sb("wf_raw", [P, KD, NHEADS])
        wf_hi = sb("wf_hi", [P, KD, NHEADS], f32r)
        wf_lo = sb("wf_lo", [P, KD, NHEADS], f32r)
        rt_raw = sb("rt_raw", [P, KD, NE])
        rt_hi = sb("rt_hi", [P, KD, NE], f32r)
        rt_lo = sb("rt_lo", [P, KD, NE], f32r)
        bf_col = sb("bf_col", [NHEADS, 1])
        head_1 = sb("head_1", [P, NHEADS])
        ss = sb("ss", [P, 5, NT])
        msq = sb("msq", [P, 5, NT])
        rstd = sb("rstd", [P, 5, NT])
        neghalf = sb("neghalf", [P, NT])
        lam_s = sb("lam_s", [P, 8, KD])
        m4ls = sb("m4ls", [P, KD])
        negmax = sb("negmax", [P, PS, NT])
        psums = sb("psums", [P, PS, NT])
        pinv = sb("pinv", [P, PS, NT])
        route = sb("route", [P, 12, NT, NE])
        top8 = sb("top8", [P, NT, 8])
        rcol = sb("rcol", [P, 4, NT])
        logit_T = sb("logit_T", [NE, T])
        slot_of = sb("slot_of", [P, NT, SLOT_COLS])
        gate_of = sb("gate_of", [P, NT, SLOT_COLS])
        njobs_f = sb("njobs_f", [P, 2])
        njobs = sb("njobs", [P, 1], i32)
        gslot = sb("gslot", [P, 1])

        with ExitStack() as lru:
            xb_pad = sb("xb_pad", [P, KD, T + CONV_W - 1], f32, lru)
            xc = sb("xc", [P, KD, T], f32, lru)
            rc = sb("rc", [P, KD, T], f32, lru)
            gelu = sb("gelu", [P, KD, T], f32, lru)
            gate_w = sb("gate_w", [P, 2 * KD, P], f32, lru)
            i_sb = sb("i_sb", [P, 2, 2, T], f32, lru)
        th = xs[:, :, :].rearrange("p t d -> p (t d)").rearrange("p (c n) -> p c n", c=KD)
        with ExitStack() as att:
            k_T = sb("k_T", [P, KD, T], f32, att)
            q_T = sb("q_T", [P, KD, T], f32, att)
            v_sb = sb("v_sb", [P, NT, D], f32, att)
            f_s = sb("f_s", [NHEADS, 8, T], f32, att)
            c_pos = sb("c_pos", [P, T], f32r, att)
            c_neg = sb("c_neg", [P, T], f32r, att)
            c_sel = sb("c_sel", [P, 2, T], f32r, att)
            prob = sb("prob", [P, PS, 3 * P], f32, att)
            prob_T = sb("prob_T", [P, 2, 3 * P], f32, att)
        tg = th
        with ExitStack() as ffn:
            hid_hi = sb("hid_hi", [P, 2, 512], f32r, ffn)
            hid_lo = sb("hid_lo", [P, 2, 512], f32r, ffn)
            silu = sb("silu", [P, 512], f32, ffn)
            hid = sb("hid", [P, 512], f32, ffn)
            y_hi = sb("y_hi", [P, D], f32r, ffn)
            y_lo = sb("y_lo", [P, D], f32r, ffn)
            sel = sb("sel", [P, NT, P], f32r, ffn)
            sel_g = sb("sel_g", [P, NT, P], f32, ffn)
            sel_T = sb("sel_T", [P, T], f32r, ffn)
            gfin_bc = sb("gfin_bc", [P, D], f32, ffn)

        bank = [ctx.enter_context(nc.psum_tensor(f"bank{i}", [P, 512], f32)) for i in range(8)]

        raw_full = [sem(f"raw_full{i}") for i in range(RAW)]
        hi_done, lo_done, unit_used = sem("hi_done"), sem("lo_done"), sem("unit_used")
        x_loaded, rows_loaded, bf_loaded, gatew_loaded = (sem(n) for n in ("x_loaded", "rows_loaded", "bf_loaded", "gatew_loaded"))
        smallw_loaded, gfin_loaded, stored = (sem(n) for n in ("smallw_loaded", "gfin_loaded", "stored"))
        blank, consts, consts_v = sem("blank"), sem("consts"), sem("consts_v")
        rows_T, cols_ready = sem("rows_T"), sem("cols_ready")
        small_hi, small_lo = sem("small_hi"), sem("small_lo")
        lam_abs, lam_exp = sem("lam_abs"), sem("lam_exp")
        sq_act, sq_dve, msq_ready, rstd_ready, xs_ready = (sem(n) for n in ("sq_act", "sq_dve", "msq_ready", "rstd_ready", "xs_ready"))
        norm_T, act_hi_done, act_lo_done = sem("norm_T"), sem("act_hi_done"), sem("act_lo_done")
        link_v = sem("link_v")
        pad_ready, xb_ready, tap0_ready, xc_ready, gates_done = (sem(n) for n in ("pad_ready", "xb_ready", "tap0_ready", "xc_ready", "gates_done"))
        sig_done, loga_ready, decay_done, bx_done, sqrt_done, gelu_done = (sem(n) for n in ("sig_done", "loga_ready", "decay_done", "bx_done", "sqrt_done", "gelu_done"))
        yl_ready, alt_hi_done, alt_lo_done, x_added = (sem(n) for n in ("yl_ready", "alt_hi_done", "alt_lo_done", "x_added"))
        silu_done, h_done, hid_hi_done, hid_lo_done = (sem(n) for n in ("silu_done", "h_done", "hid_hi_done", "hid_lo_done"))
        f_done, f_abs, f_exp, c_blank, c_ready, c_hi_done, c_lo_done, c_sel_ready = (sem(n) for n in ("f_done", "f_abs", "f_exp", "c_blank", "c_ready", "c_hi_done", "c_lo_done", "c_sel_ready"))
        k_ready, v_ready, q_ready, tg_ready = (sem(n) for n in ("k_ready", "v_ready", "q_ready", "tg_ready"))
        s_done, s_ready, p_exp, p_norm, pt_done, pt_ready, pv_done, o_ready = (sem(n) for n in ("s_done", "s_ready", "p_exp", "p_norm", "pt_done", "pt_ready", "pv_done", "o_ready"))
        logits_done, logitT_ready, v1_ready, e_ready, mask_ready, rank_done, njobs_ready = (sem(n) for n in ("logits_done", "logitT_ready", "v1_ready", "e_ready", "mask_ready", "rank_done", "njobs_ready"))
        xs_hi_done, src_ready, moe_blank = sem("xs_hi_done"), sem("src_ready"), sem("moe_blank")
        sel_built, gathered, tok_hi_done, tok_lo_done = (sem(n) for n in ("sel_built", "gathered", "tok_hi_done", "tok_lo_done"))
        selg_T, selT_ready, yhi_done, ylo_done, scattered, moe_added = (sem(n) for n in ("selg_T", "selT_ready", "yhi_done", "ylo_done", "scattered", "moe_added"))
        e_silu, e_h, e_T, e_hid_hi, e_hid_lo = (sem(n) for n in ("e_silu", "e_h", "e_T", "e_hid_hi", "e_hid_lo"))
        out_ready = sem("out_ready")

        def cols256(w, c):
            return w.rearrange("(k p) n -> p k n", p=P)[:, :, bass.ds(c * 256, 256)]

        def square(w, col_half, k_half):
            return w.rearrange("(k p) n -> p k n", p=P)[:, 4 * k_half:4 * k_half + 4, HALF * col_half:HALF * col_half + HALF]

        w_in, w_out, w_gu, w_dn = lru_w_in[0], lru_w_out[0], mlp_w_gu[0], mlp_w_down[0]
        w_qg, w_o = fox_w_qg[0], fox_w_o[0]
        dn_v = w_dn.rearrange("(k p) n -> p k n", p=P)
        e_gu = moe_w_gu[0].rearrange("e (k p) n -> e p k n", p=P)
        e_dn = moe_w_down[0].rearrange("e (k p) n -> e p k n", p=P)

        def raw_count(u, n):
            return 16 * (u // RAW + 1 + n)

        def units(u, n=0):
            return u + RAW * n

        block = ctx.enter_context(nc.Block())

        @block.sync
        def _(sp):
            def load(u, n, width, src):
                if not (isinstance(n, int) and u + RAW * n < RAW):
                    sp.wait_ge(lo_done, units(u, n) - RAW + 1)
                dst = raw[:, u % RAW, :].rearrange("p (k n) -> p k n", n=width)
                sp.dma_start(dst, src).then_inc(raw_full[u % RAW], 16)

            for t in range(NT):
                sp.dma_start(x[:, t, :], x_in[0, t * P:(t + 1) * P, :]).then_inc(x_loaded, 16)
            for row, src in ((R_NORM, norm_g.rearrange("l s (c p) -> (l s c) p", p=P)),
                             (R_KVN, kv_norm_g.rearrange("(c p) -> c p", p=P)),
                             (R_CB, lru_conv_b[0].rearrange("(c p) -> c p", p=P)),
                             (R_CW, lru_conv_w[0].rearrange("w (c p) -> (w c) p", p=P)),
                             (R_GB, lru_gate_b[0].rearrange("g (c p) -> (g c) p", p=P)),
                             (R_LAM, lru_lambda[0].rearrange("(c p) -> c p", p=P))):
                sp.dma_start(rows[row:row + src.shape[0], :], src).then_inc(rows_loaded, 16)
            for c in range(8):
                load(U_XB + c, 0, 256, cols256(w_in, c))
            for c in range(4):
                load(U_OUT + c, 0, HALF, square(w_out, c // 2, c % 2))
            load(U_FF, 0, 256, cols256(w_gu, 0))
            load(U_FF + 1, 0, 256, cols256(w_gu, PAIRS))
            with sp.Fori(0, (PAIRS - 1) // 2) as i:
                for m in range(2):
                    u = U_FF + 2 + 3 * m
                    load(u, i, 256, cols256(w_gu, 2 * i + 1 + m))
                    load(u + 1, i, 256, cols256(w_gu, 2 * i + 1 + m + PAIRS))
                    load(u + 2, i, D, dn_v[:, bass.ds(4 * i + 2 * m, 2), :])
            load(U_K - 1, 0, D, dn_v[:, 2 * PAIRS - 2:2 * PAIRS, :])
            for c in range(4):
                load(U_K + c, 0, 256, cols256(w_kvf, c))
            for c in range(4):
                load(U_V + c, 0, HALF, square(w_kvf[:, D:2 * D], c // 2, c % 2))
            for c in range(8):
                load(U_Q + c, 0, 256, cols256(w_qg, c))
            for c in range(4):
                load(U_O + c, 0, HALF, square(w_o, c // 2, c % 2))

            def expert_unit(e, k):
                c, part = (0, k // 2) if k < 4 else ((k - 4) // 6 + 1, (k - 4) % 6 // 2)
                if k >= JU - 2:
                    c, part = CH, 2
                half = k % 2
                if part < 2:
                    lo = part * D_EXP + 512 * c
                    return e_gu[e][:, 4 * half:4 * half + 4, lo:lo + 512], 512
                lo = 4 * (c - 1) + 2 * half
                return e_dn[e][:, lo:lo + 2, :], D

            def expert(j, e, first, last):
                for k in range(first, last):
                    src, width = expert_unit(e, k)
                    load(U_MOE + k, J6 * j, width, src)

            with sp.Fori(0, NE) as j:
                expert(j, j, 0, JU)
            expert(NE, 0, 0, LEAD)
            sp.wait_ge(njobs_ready, 1)
            jobs = sp.value_load(njobs[0:1, 0:1], min_val=NE, max_val=2 * NE)
            with sp.If(jobs > NE):
                with sp.Fori(NE, 2 * NE - 1) as j:
                    expert(j, j - NE, LEAD, JU)
                    expert(j + 1, j - NE + 1, 0, LEAD)
                expert(2 * NE - 1, NE - 1, LEAD, JU)
                expert(2 * NE, 0, 0, LEAD)
            for t in range(NT):
                sp.wait_ge(out_ready, t + 1)
                sp.dma_start(out[0, t * P:(t + 1) * P, :], xs[:, t, :]).then_inc(stored, 16)
            sp.wait_ge(stored, NT * 16)

        @block.gpsimd
        def _(pool):
            g = nc.gpsimd
            g.memset(ident[:], 0.0).then_inc(blank, 1)
            g.memset(ones[:], 1.0).then_inc(blank, 1)
            g.memset(maskf[:], 0.0).then_inc(blank, 1)
            g.memset(neghalf[:], -0.5).then_inc(blank, 1)
            g.memset(xb_pad[:, :, 0:CONV_W - 1], 0.0).then_inc(pad_ready, 1)
            g.iota(iota[:], [[1, P]], base=0, channel_multiplier=0,
                   allow_small_or_imprecise_dtypes=True).then_inc(consts, 1)
            pool.wait_ge(blank, 4)
            g.affine_select(out=ident[:], in_=ident[:], compare_op=ALU.not_equal, fill=1.0, base=0,
                            pattern=[[-1, P]], channel_multiplier=1).then_inc(consts, 1)
            g.affine_select(out=upto[:], in_=ones[:, 0:P], compare_op=ALU.is_ge, fill=0.0, base=0,
                            pattern=[[1, P]], channel_multiplier=-1).then_inc(consts, 1)
            g.affine_select(out=before[:], in_=ones[:, 0:P], compare_op=ALU.is_ge, fill=0.0, base=-1,
                            pattern=[[1, P]], channel_multiplier=-1).then_inc(consts, 1)
            g.affine_select(out=maskf[:], in_=maskf[:], compare_op=ALU.is_ge, fill=NEG, base=0,
                            pattern=[[-1, P]], channel_multiplier=1).then_inc(consts, 1)

            def norm_scale(n):
                pool.wait_ge(sq_act, n + 1)
                pool.wait_ge(sq_dve, n + 1)
                g.tensor_scalar(msq[:, n, :], ss[:, n, :], 1.0 / D, EPS, ALU.mult, ALU.add).then_inc(msq_ready, 1)
                pool.wait_ge(msq_ready, n + 1)
                g.tensor_tensor(rstd[:, n, :], msq[:, n, :], neghalf[:], ALU.pow).then_inc(rstd_ready, 1)

            norm_scale(0)
            for j in range(KD // 2):
                pool.wait_ge(sig_done, 4 * (j + 1))
                part = xc[:, 2 * j:2 * j + 2, :]
                g.tensor_tensor(part, i_sb[:, j % 2, :, :], part, ALU.mult).then_inc(bx_done, 1)
            norm_scale(1)
            norm_scale(2)
            norm_scale(3)
            pool.dma_start(gfin_bc[:], final_norm_g.partition_broadcast(P)).then_inc(gfin_loaded, 16)
            pool.wait_ge(xs_hi_done, 1)
            g.tensor_tensor(alt_lo[:].rearrange("p c n -> p (c n)"), xs[:].rearrange("p t d -> p (t d)"),
                            alt_hi[:].rearrange("p c n -> p (c n)").bitcast(f32), ALU.subtract).then_inc(src_ready, 1)
            norm_scale(4)

        @block.scalar
        def _(act):
            a = nc.scalar
            def split_hi(u, n=0):
                act.wait_ge(raw_full[u % RAW], raw_count(u, n))
                if not (isinstance(n, int) and u + RAW * n < SPL):
                    act.wait_ge(unit_used, units(u, n) - SPL + 1)
                a.activation(w_hi[:, u % SPL, :], raw[:, u % RAW, :], ACT.Copy).then_inc(hi_done, 1)

            def squares(n):
                a.activation(xs[:, 0, :], x[:, 0, :], ACT.Square, accum_out=ss[:, n, 0:1]).then_inc(sq_act, 1)

            def norm_hi(m, gain, hi, lo_before=None):
                for c in range(KD):
                    if lo_before is not None:
                        if c % 2 == 0:
                            act.wait_ge(act_lo_done, lo_before + c + 2)
                    elif c % 2 == 0:
                        act.wait_ge(norm_T, 4 * m + c // 2 + 1)
                    a.activation(hi[:, c, :], bank[c // 2][:, (c % 2) * T:(c % 2 + 1) * T], ACT.Copy,
                                 scale=cols[:, gain + c:gain + c + 1]).then_inc(act_hi_done, 1)

            act.wait_ge(x_loaded, 32)
            squares(0)
            act.dma_start(gate_w[:, :, :], lru_gate_w[0].rearrange("g n d e -> d (g n) e")).then_inc(gatew_loaded, 16)
            act.dma_start(wf_raw[:], w_kvf.rearrange("(k p) n -> p k n", p=P)[:, :, 2 * D:]).then_inc(smallw_loaded, 16)
            act.dma_start(rt_raw[:], moe_router[0].rearrange("(k p) n -> p k n", p=P)).then_inc(smallw_loaded, 16)
            act.dma_start(bf_col[:], b_f.rearrange("(h o) -> h o", o=1)).then_inc(bf_loaded, 16)
            split_hi(0)
            act.wait_ge(cols_ready, 1)
            norm_hi(0, R_NORM, act_hi)
            split_hi(1)
            act.wait_ge(lam_abs, 1)
            a.activation(lam_s[:, 1, :], lam_s[:, 0, :], ACT.Exp, scale=-1.0).then_inc(lam_exp, 1)

            def gate_sigmoids(j):
                for c in (2 * j, 2 * j + 1):
                    act.wait_ge(gates_done, c + 1)
                    if j >= 2:
                        act.wait_ge(bx_done, j - 1)
                    a.activation(th[:, c, :], bank[c % 4][:, 0:T], ACT.Sigmoid,
                                 bias=cols[:, R_GB + c:R_GB + c + 1]).then_inc(sig_done, 1)
                    a.activation(i_sb[:, j % 2, c % 2, :], bank[c % 4][:, T:2 * T], ACT.Sigmoid,
                                 bias=cols[:, R_GB + KD + c:R_GB + KD + c + 1]).then_inc(sig_done, 1)

            def decays(h):
                part = slice(4 * h, 4 * h + 4)
                act.wait_ge(loga_ready, h + 1)
                a.activation(xb_pad[:, part, 0:T], th[:, part, :], ACT.Exp, scale=-2.0).then_inc(decay_done, 1)
                act.wait_ge(decay_done, 2 * h + 1)
                a.activation(th[:, part, :], th[:, part, :], ACT.Tanh).then_inc(decay_done, 1)
                act.wait_ge(decay_done, 2 * h + 2)
                a.activation(th[:, part, :], th[:, part, :], ACT.Sqrt).then_inc(sqrt_done, 1)

            for k in range(U_FF):
                if 1 <= k <= 4:
                    act.wait_ge(unit_used, k)
                    a.activation(xb_pad[:, 2 * k - 2:2 * k, CONV_W - 1:], bank[4 + (k - 1) % 4][:].rearrange("p (c n) -> p c n", c=2),
                                 ACT.Copy).then_inc(xb_ready, 1)
                    act.wait_ge(xb_ready, k)
                    act.wait_ge(pad_ready, 1)
                    for c in (2 * k - 2, 2 * k - 1):
                        a.activation(xc[:, c, :], xb_pad[:, c, 0:T], ACT.Identity, scale=cols[:, R_CW + c:R_CW + c + 1],
                                     bias=cols[:, R_CB + c:R_CB + c + 1]).then_inc(tap0_ready, 1)
                if k < 6:
                    split_hi(k + LEAD)
                if k == 1:
                    act.wait_ge(smallw_loaded, 32)
                    a.activation(wf_hi[:], wf_raw[:], ACT.Copy).then_inc(small_hi, 1)
                    a.activation(rt_hi[:], rt_raw[:], ACT.Copy).then_inc(small_hi, 1)
                if 2 <= k <= 5:
                    gate_sigmoids(k - 2)
                if k == 5:
                    split_hi(6 + LEAD)
                if k in (4, 5):
                    decays(k - 4)
                if 5 <= k <= 8:
                    c = k - 5
                    act.wait_ge(unit_used, U_GB + c + 1)
                    a.activation(gelu[:, 2 * c:2 * c + 2, :], bank[4 + c][:].rearrange("p (c n) -> p c n", c=2),
                                 ACT.Gelu_apprx_tanh).then_inc(gelu_done, 1)
                if k in (7, 8):
                    for c in (2 * k - 14, 2 * k - 13):
                        act.wait_ge(yl_ready, c + 1)
                        a.activation(alt_hi[:, 2 * c:2 * c + 2, :], gelu[:, 2 * c:2 * c + 2, :], ACT.Copy).then_inc(alt_hi_done, 1)
                if k >= 7:
                    split_hi(k + LEAD)

            act.wait_ge(x_added, 3)
            squares(1)
            norm_hi(1, R_NORM + KD, act_hi)
            split_hi(U_FF + LEAD)

            def ff_silu(u_gate, n, p, m):
                act.wait_ge(unit_used, units(u_gate, n) + 1)
                if not (isinstance(p, int) and p == 0):
                    act.wait_ge(h_done, p)
                a.activation(silu[:], bank[4 + 2 * (m % 2)][:], ACT.Silu).then_inc(silu_done, 1)

            def ff_hid(p, m):
                act.wait_ge(h_done, p + 1)
                a.activation(hid_hi[:, m % 2, :], hid[:], ACT.Copy).then_inc(hid_hi_done, 1)

            ff_silu(U_FF, 0, 0, 0)
            split_hi(U_FF + 1 + LEAD)
            ff_hid(0, 0)
            split_hi(U_FF + 2 + LEAD)
            with act.Fori(0, (PAIRS - 1) // 2) as i:
                for m in (1, 2):
                    u = U_FF + 3 * m - 1
                    p = 2 * i + m
                    ff_silu(u, i, p, m)
                    split_hi(u + 1 + LEAD, i)
                    act.wait_ge(unit_used, units(u, i))
                    ff_hid(p, m)
                    split_hi(u + 2 + LEAD, i)
                    split_hi(u + 3 + LEAD, i)

            act.wait_ge(x_added, 6)
            squares(2)
            norm_hi(2, R_KVN, alt_hi)
            norm_hi(2, R_NORM + 2 * KD, act_hi, 2 * KD)
            act.wait_ge(f_abs, 1)
            a.activation(f_s[:, 2, :], f_s[:, 1, :], ACT.Exp, scale=-1.0).then_inc(f_exp, 1)
            split_hi(U_K + LEAD)
            for k in range(1, 13):
                if k == 6:
                    act.wait_ge(c_ready, 1)
                    act.wait_ge(c_blank, 6)
                    a.activation(c_pos[0:NHEADS, :], f_s[:, 0, :], ACT.Copy).then_inc(c_hi_done, 1)
                    a.activation(c_neg[64:64 + NHEADS, :], f_s[:, 0, :], ACT.Copy, scale=-1.0).then_inc(c_hi_done, 1)
                if 1 <= k <= 4:
                    act.wait_ge(unit_used, U_K + k)
                    a.activation(k_T[:, 2 * k - 2:2 * k, :], bank[4 + (k - 1) % 2][:].rearrange("p (c n) -> p c n", c=2),
                                 ACT.Copy).then_inc(k_ready, 1)
                if k in (6, 8):
                    half = (k - 6) // 2
                    act.wait_ge(unit_used, U_K + k)
                    for t in range(NT):
                        a.activation(v_sb[:, t, HALF * half:HALF * half + HALF], bank[2 * half + t][:], ACT.Copy).then_inc(v_ready, 1)
                if 9 <= k <= 12:
                    act.wait_ge(unit_used, U_K + k)
                    a.activation(q_T[:, 2 * (k - 9):2 * (k - 9) + 2, :], bank[4 + (k - 9) % 2][:].rearrange("p (c n) -> p c n", c=2),
                                 ACT.Copy, scale=HD ** -0.5).then_inc(q_ready, 1)
                if k < 12:
                    split_hi(U_K + k + LEAD)
            for i in range(NHEADS + 5):
                if i < NHEADS:
                    act.wait_ge(s_ready, i + 1)
                    if i >= PS:
                        act.wait_ge(pt_done, i - PS + 1)
                    for t, cut in enumerate((slice(0, P), slice(P, 3 * P))):
                        a.activation(prob[:, i % PS, cut], bank[i % 2][:, cut], ACT.Exp, bias=negmax[:, i % PS, t:t + 1],
                                     accum_out=psums[:, i % PS, t:t + 1]).then_inc(p_exp, 1)
                if 5 <= i <= 17 and i % 4 == 1:
                    split_hi(U_G + (i - 5) // 4 + LEAD)
                if 2 <= i <= NHEADS + 1:
                    h = i - 2
                    act.wait_ge(pt_done, h + 1)
                    if h >= 2:
                        act.wait_ge(pv_done, h - 1)
                    a.activation(prob_T[:, h % 2, :], bank[2 + h % 2][:, 0:3 * P], ACT.Copy).then_inc(pt_ready, 1)
                if i % 4 == 2 and i // 4 < 4:
                    c = i // 4
                    act.wait_ge(unit_used, U_G + c + 1)
                    a.activation(tg[:, 2 * c:2 * c + 2, :], bank[6 + c % 2][:].rearrange("p (c n) -> p c n", c=2),
                                 ACT.Tanh, scale=0.5).then_inc(tg_ready, 1)
                if i >= 6 and i % 2 == 0:
                    hp = (i - 6) // 2
                    act.wait_ge(o_ready, hp + 1)
                    a.activation(alt_hi[:, hp, :], q_T[:, hp, :], ACT.Copy, scale=0.5).then_inc(alt_hi_done, 1)
            for k in range(4):
                split_hi(U_O + k + LEAD)

            act.wait_ge(x_added, 11)
            squares(3)
            act.wait_ge(xs_ready, 2 * 3 + 2)
            a.activation(alt_hi[:].rearrange("p c n -> p (c n)"), xs[:].rearrange("p t d -> p (t d)"), ACT.Copy).then_inc(xs_hi_done, 1)
            norm_hi(3, R_NORM + 3 * KD, act_hi)
            act.wait_ge(v1_ready, 1)
            for t in range(NT):
                a.activation(route[:, 5, t, :], route[:, 0, t, :], ACT.Exp, bias=rcol[:, 0, t:t + 1]).then_inc(e_ready, 1)

            def tokens_hi(j):
                for c in range(KD):
                    if c % 4 == 0:
                        act.wait_ge(gathered, 2 * j + c // 4 + 1)
                    a.activation(act_hi[:, c // 2, (c % 2) * P:(c % 2 + 1) * P], bank[6 + c // 4][:, (c % 4) * P:(c % 4 + 1) * P],
                                 ACT.Copy, scale=cols[:, R_NORM + 3 * KD + c:R_NORM + 3 * KD + c + 1]).then_inc(tok_hi_done, 1)

            def y_hi_part(j):
                act.wait_ge(unit_used, U_MOE + JU * j)
                act.wait_ge(selT_ready, j + 1)
                for half in range(2):
                    a.activation(y_hi[:, HALF * half:HALF * half + HALF], bank[half][:], ACT.Copy, scale=gslot[:, 0:1]).then_inc(yhi_done, 1)

            tokens_hi(0)
            act.wait_ge(moe_blank, 2)
            act.wait_ge(njobs_ready, 1)
            jobs = act.value_load(njobs[0:1, 0:1], min_val=NE, max_val=2 * NE)
            with act.Fori(0, jobs) as j:
                for k in range(JU):
                    c = (k - 2) // 6 if k >= 2 else 0
                    if k == 0:
                        y_hi_part(j)
                    if k == 2 or (k >= 6 and k % 6 == 0 and k // 6 < CH):
                        c = k // 6
                        act.wait_ge(unit_used, U_MOE + JU * j + k)
                        if c:
                            act.wait_ge(e_h, CH * j + c)
                        a.activation(silu[:], bank[2][:], ACT.Silu).then_inc(e_silu, 1)
                    if (k >= 6 and k % 6 == 0) or k == JU - 3:
                        c = k // 6 - 1 if k < JU - 3 else CH - 1
                        act.wait_ge(e_T, CH * j + c + 1)
                        a.activation(hid_hi[:, c % 2, :], bank[4 + c % 2][:], ACT.Copy).then_inc(e_hid_hi, 1)
                    if k == JU - 2:
                        tokens_hi(j + 1)
                    split_hi(U_MOE + k + LEAD, J6 * j)
            y_hi_part(jobs)
            act.wait_ge(moe_added, 4 * jobs + 4)
            squares(4)

        @block.vector
        def _(dve):
            v = nc.vector
            chain = [0]

            def link(ins):
                chain[0] += 1
                ins.then_inc(link_v, 1)
                dve.wait_ge(link_v, chain[0])

            def split_lo(u, n=0):
                dve.wait_ge(hi_done, units(u, n) + 1)
                v.tensor_tensor(w_lo[:, u % SPL, :], raw[:, u % RAW, :], w_hi[:, u % SPL, :].bitcast(f32),
                                ALU.subtract).then_inc(lo_done, 1)

            def squares(n):
                v.tensor_tensor_reduce(out=xs[:, 1, :], in0=x[:, 1, :], in1=x[:, 1, :], scale=1.0, scalar=0.0,
                                       op0=ALU.mult, op1=ALU.add, accum_out=ss[:, n, 1:2]).then_inc(sq_dve, 1)

            def scale_x(n):
                dve.wait_ge(rstd_ready, n + 1)
                for t in range(NT):
                    v.tensor_scalar(xs[:, t, :], x[:, t, :], rstd[:, n, t:t + 1], None, ALU.mult).then_inc(xs_ready, 1)

            def norm_lo(i, gain, hi, lo):
                for c in range(KD):
                    if c % 2 == 0:
                        dve.wait_ge(act_hi_done, KD * i + c + 2)
                    v.scalar_tensor_tensor(out=lo[:, c, :], in0=bank[c // 2][:, (c % 2) * T:(c % 2 + 1) * T],
                                           scalar=cols[:, gain + c:gain + c + 1], in1=hi[:, c, :].bitcast(f32),
                                           op0=ALU.mult, op1=ALU.subtract).then_inc(act_lo_done, 1)

            def log1p_ratio(s):
                link(v.tensor_scalar(s(3), s(2), 2.0, None, ALU.add))
                link(v.reciprocal(s(4), s(3)))
                link(v.tensor_tensor(s(3), s(2), s(4), ALU.mult))
                link(v.tensor_tensor(s(4), s(3), s(3), ALU.mult))

            def log1p_series(s, powers):
                for n in powers:
                    if n == 15:
                        link(v.tensor_scalar(s(5), s(4), 1.0 / n, None, ALU.mult))
                    else:
                        link(v.scalar_tensor_tensor(out=s(5), in0=s(5), scalar=1.0 / n, in1=s(4), op0=ALU.add, op1=ALU.mult))

            def log_sigmoid(s, z_min, out_scale, out):
                link(v.scalar_tensor_tensor(out=s(5), in0=s(5), scalar=1.0, in1=s(3), op0=ALU.add, op1=ALU.mult))
                link(v.scalar_tensor_tensor(out=s(5), in0=s(5), scalar=-2.0, in1=z_min, op0=ALU.mult, op1=ALU.add))
                link(v.tensor_scalar(out, s(5), out_scale, None, ALU.mult))

            def add_to_x(count_sem, banks, halves=(0, 1)):
                for t in range(NT):
                    for half in halves:
                        part = x[:, t, HALF * half:HALF * half + HALF]
                        v.tensor_tensor(part, part, banks(t, half), ALU.add).then_inc(count_sem, 1)

            dve.wait_ge(x_loaded, 32)
            squares(0)
            dve.wait_ge(consts, 5)
            v.tensor_copy(ident_bf[:], ident[:]).then_inc(consts_v, 1)
            v.tensor_copy(mask_bf[:], maskf[:]).then_inc(consts_v, 1)
            link(v.memset(head_1[:], 0.0))
            for row in (0, 32, 64, 96):
                v.tensor_copy(head_1[row:row + NHEADS, :], ident[row:row + NHEADS, row:row + NHEADS]).then_inc(consts_v, 1)
            dve.wait_ge(rows_T, 1)
            link(v.tensor_copy(cols[:], bank[7][:, 0:R_END]))
            lam = cols[:, R_LAM:R_LAM + KD]
            v.scalar_tensor_tensor(out=lam_s[:, 0, :], in0=lam, scalar=-1.0, in1=lam, op0=ALU.mult,
                                   op1=ALU.max).then_inc(lam_abs, 1)
            v.tensor_scalar(lam_s[:, 6, :], lam, 0.0, None, ALU.min).then_inc(cols_ready, 1)
            scale_x(0)
            split_lo(0)
            norm_lo(0, R_NORM, act_hi, act_lo)
            split_lo(1)
            dve.wait_ge(lam_exp, 1)
            lam_step = lambda n: lam_s[:, n - 1, :]
            log1p_ratio(lam_step)
            log1p_series(lam_step, (15, 13, 11, 9, 7, 5, 3))
            log_sigmoid(lam_step, lam_s[:, 6, :], -LRU_C / 2, m4ls[:])

            dve.wait_ge(pad_ready, 1)

            def gated(c):
                part = slice(2 * c, 2 * c + 2)
                dve.wait_ge(gelu_done, c + 1)
                v.tensor_tensor(gelu[:, part, :], gelu[:, part, :], rc[:, part, :], ALU.mult).then_inc(yl_ready, 1)

            def gated_lo(c):
                part = slice(2 * c, 2 * c + 2)
                dve.wait_ge(alt_hi_done, c + 1)
                v.tensor_tensor(alt_lo[:, part, :], gelu[:, part, :], alt_hi[:, part, :].bitcast(f32), ALU.subtract).then_inc(alt_lo_done, 1)

            for k in range(U_FF):
                if 1 <= k <= 4:
                    dve.wait_ge(xb_ready, k)
                    pair = (2 * k - 2, 2 * k - 1)
                    dve.wait_ge(tap0_ready, 2 * k)
                    for w in range(1, CONV_W):
                        for c in pair:
                            tap = cols[:, R_CW + KD * w + c:R_CW + KD * w + c + 1]
                            last = v.scalar_tensor_tensor(out=xc[:, c, :], in0=xb_pad[:, c, w:w + T], scalar=tap,
                                                          in1=xc[:, c, :], op0=ALU.mult, op1=ALU.add)
                            if w == CONV_W - 1:
                                last.then_inc(xc_ready, 1)
                        if w < CONV_W - 1:
                            link(last)
                if k == 5:
                    split_lo(k + LEAD)
                if k in (4, 5):
                    h = k - 4
                    part = slice(4 * h, 4 * h + 4)
                    dve.wait_ge(sig_done, 8 * h + 8)
                    v.tensor_tensor(th[:, part, :], th[:, part, :], m4ls[:, part].rearrange("p (c o) -> p c o", o=1).to_broadcast([P, 4, T]),
                                    ALU.mult).then_inc(loga_ready, 1)
                if k in (5, 6):
                    h = k - 5
                    part = slice(4 * h, 4 * h + 4)
                    dve.wait_ge(sqrt_done, h + 1)
                    dve.wait_ge(bx_done, 2 * h + 2)
                    link(v.scalar_tensor_tensor(out=rc[:, part, :], in0=xb_pad[:, part, 0:T], scalar=1.0, in1=th[:, part, :],
                                                op0=ALU.add, op1=ALU.mult))
                    link(v.tensor_tensor(xc[:, part, :], rc[:, part, :], xc[:, part, :], ALU.mult))
                    for c in range(4 * h, 4 * h + 4):
                        last = v.tensor_tensor_scan(rc[:, c, :], xb_pad[:, c, 0:T], xc[:, c, :], 0.0, ALU.mult, ALU.add)
                    link(last)
                if k == 5:
                    split_lo(6 + LEAD)

                if k == 6:
                    gated(0)
                    gated(1)
                if k == 7:
                    gated(2)
                    gated_lo(0)
                    gated_lo(1)
                if k == 8:
                    gated(3)
                    gated_lo(2)
                    gated_lo(3)
                if k == 9:
                    dve.wait_ge(small_hi, 2)
                    v.tensor_tensor(wf_lo[:], wf_raw[:], wf_hi[:].bitcast(f32), ALU.subtract).then_inc(small_lo, 1)
                    v.tensor_tensor(rt_lo[:], rt_raw[:], rt_hi[:].bitcast(f32), ALU.subtract).then_inc(small_lo, 1)
                if k == 10:
                    dve.wait_ge(unit_used, U_OUT + 2)
                    add_to_x(x_added, lambda t, half: bank[2 * half + t][:], (0,))
                if k not in (5, 6):
                    split_lo(k + LEAD)
            dve.wait_ge(unit_used, U_OUT + 4)
            add_to_x(x_added, lambda t, half: bank[2 * half + t][:], (1,))

            dve.wait_ge(x_added, 4)
            squares(1)
            scale_x(1)
            norm_lo(1, R_NORM + KD, act_hi, act_lo)
            split_lo(U_FF + LEAD)
            split_lo(U_FF + 1 + LEAD)

            def ff_hid(u_up, n, p, m):
                dve.wait_ge(silu_done, p + 1)
                dve.wait_ge(unit_used, units(u_up, n) + 1)
                if not (isinstance(p, int) and p == 0):
                    dve.wait_ge(hid_lo_done, p)
                v.tensor_tensor(hid[:], silu[:], bank[5 + 2 * (m % 2)][:], ALU.mult).then_inc(h_done, 1)
                dve.wait_ge(hid_hi_done, p + 1)
                v.tensor_tensor(hid_lo[:, m % 2, :], hid[:], hid_hi[:, m % 2, :].bitcast(f32), ALU.subtract).then_inc(hid_lo_done, 1)

            ff_hid(U_FF + 1, 0, 0, 0)
            split_lo(U_FF + 2 + LEAD)
            with dve.Fori(0, (PAIRS - 1) // 2) as i:
                for m in (1, 2):
                    u = U_FF + 3 * m - 1
                    split_lo(u + 1 + LEAD, i)
                    ff_hid(u + 1, i, 2 * i + m, m)
                    split_lo(u + 2 + LEAD, i)
                    split_lo(u + 3 + LEAD, i)
            dve.wait_ge(unit_used, U_K)
            add_to_x(x_added, lambda t, half: bank[2 * half + t][:])

            dve.wait_ge(x_added, 8)
            squares(2)
            scale_x(2)
            norm_lo(2, R_KVN, alt_hi, alt_lo)
            norm_lo(3, R_NORM + 2 * KD, act_hi, act_lo)
            v.memset(c_pos[:].bitcast(i32), 0).then_inc(c_blank, 1)
            v.memset(c_neg[:].bitcast(i32), 0).then_inc(c_blank, 1)
            dve.wait_ge(c_blank, 2)
            for c_rows, row in ((c_pos, 64), (c_pos, 96), (c_neg, 0), (c_neg, 32)):
                v.tensor_copy(c_rows[row:row + NHEADS, :], ones[row:row + NHEADS, :]).then_inc(c_blank, 1)
            dve.wait_ge(f_done, 1)
            dve.wait_ge(bf_loaded, 16)
            link(v.tensor_scalar(f_s[:, 0, :], bank[6][0:NHEADS, 0:T], bf_col[:, 0:1], None, ALU.add))
            v.scalar_tensor_tensor(out=f_s[:, 1, :], in0=f_s[:, 0, :], scalar=-1.0, in1=f_s[:, 0, :], op0=ALU.mult,
                                   op1=ALU.max).then_inc(f_abs, 1)
            link(v.tensor_scalar(f_s[:, 6, :], f_s[:, 0, :], 0.0, None, ALU.min))
            split_lo(U_K + LEAD)
            f_step = lambda n: f_s[:, n, :]
            for k in range(1, 12):
                if k == 1:
                    dve.wait_ge(f_exp, 1)
                    log1p_ratio(f_step)
                if k == 2:
                    log1p_series(f_step, (15, 13, 11, 9))
                if k == 3:
                    log1p_series(f_step, (7, 5, 3))
                if k == 4:
                    log_sigmoid(f_step, f_s[:, 6, :], 1.0, f_s[:, 7, :])
                    v.tensor_tensor_scan(f_s[:, 0, :], ones[0:NHEADS, :], f_s[:, 7, :], 0.0, ALU.mult, ALU.add).then_inc(c_ready, 1)
                if k == 7:
                    dve.wait_ge(c_hi_done, 2)
                    v.tensor_tensor(c_pos[32:32 + NHEADS, :], f_s[:, 0, :], c_pos[0:NHEADS, :].bitcast(f32), ALU.subtract).then_inc(c_lo_done, 1)
                    v.tensor_tensor(c_neg[96:96 + NHEADS, :], c_pos[0:NHEADS, :].bitcast(f32), f_s[:, 0, :], ALU.subtract).then_inc(c_lo_done, 1)
                split_lo(U_K + k + LEAD)

            def select_head(h):
                v.tensor_scalar(c_sel[:, h % 2, :], c_pos[:].bitcast(f32), head_1[:, h:h + 1], None, ALU.mult).then_inc(c_sel_ready, 1)

            dve.wait_ge(consts_v, 6)
            dve.wait_ge(c_lo_done, 2)
            select_head(0)
            select_head(1)
            for i in range(NHEADS + 6):
                if i < NHEADS:
                    dve.wait_ge(s_done, i + 1)
                    if i + 2 < NHEADS:
                        select_head(i + 2)
                    for t, cut in enumerate((slice(0, P), slice(P, 3 * P))):
                        last = v.tensor_reduce(negmax[:, i % PS, t:t + 1], bank[i % 2][:, cut], AX.X, ALU.max, negate=True)
                    last.then_inc(s_ready, 1)
                if 1 <= i <= NHEADS:
                    b = (i - 1) % PS
                    dve.wait_ge(p_exp, 2 * i)
                    link(v.reciprocal(pinv[:, b, :], psums[:, b, :]))
                    v.tensor_scalar(prob[:, b, 0:P], prob[:, b, 0:P], pinv[:, b, 0:1], None, ALU.mult)
                    v.tensor_scalar(prob[:, b, P:3 * P], prob[:, b, P:3 * P], pinv[:, b, 1:2], None, ALU.mult).then_inc(p_norm, 1)
                if 5 <= i <= 17 and i % 4 == 1:
                    split_lo(U_G + (i - 5) // 4 + LEAD)
                if 5 <= i <= NHEADS + 3 and i % 2 == 1:
                    hp = (i - 5) // 2
                    dve.wait_ge(pv_done, 2 * hp + 2)
                    dve.wait_ge(tg_ready, hp // 2 + 1)
                    v.scalar_tensor_tensor(out=q_T[:, hp, :], in0=tg[:, hp, :], scalar=1.0, in1=bank[4 + hp % 2][:, 0:T],
                                           op0=ALU.add, op1=ALU.mult).then_inc(o_ready, 1)
                if i >= 7 and i % 2 == 1:
                    hp = (i - 7) // 2
                    dve.wait_ge(alt_hi_done, 4 + hp + 1)
                    v.scalar_tensor_tensor(out=alt_lo[:, hp, :], in0=q_T[:, hp, :], scalar=0.5, in1=alt_hi[:, hp, :].bitcast(f32),
                                           op0=ALU.mult, op1=ALU.subtract).then_inc(alt_lo_done, 1)
            for k in range(4):
                if k == 2:
                    dve.wait_ge(unit_used, U_O + 2)
                    add_to_x(x_added, lambda t, half: bank[2 * half + t][:], (0,))
                split_lo(U_O + k + LEAD)
            dve.wait_ge(unit_used, U_O + 4)
            add_to_x(x_added, lambda t, half: bank[2 * half + t][:], (1,))

            dve.wait_ge(x_added, 12)
            squares(3)
            scale_x(3)
            norm_lo(4, R_NORM + 3 * KD, act_hi, act_lo)
            LOG, GT, EQ, MASK, INC, EXP, GATE, OFF = range(8)
            both = lambda n: route[:, n, :, :]

            def per_token(col):
                return col.to_broadcast([P, NT, NE])

            dve.wait_ge(logits_done, 1)
            v.tensor_copy(logit_T[:], bank[4][0:NE, 0:T]).then_inc(logitT_ready, 1)
            dve.wait_ge(logits_done, 2)
            link(v.tensor_copy(both(LOG), bank[5][:, 0:NT * NE].rearrange("p (t e) -> p t e", t=NT)))
            for t in range(NT):
                last = v.max(top8[:, t, :], route[:, LOG, t, :])
            link(last)
            v.tensor_scalar(rcol[:, 0, :], top8[:, :, 0], -1.0, None, ALU.mult).then_inc(v1_ready, 1)
            v.tensor_tensor(both(GT), both(LOG), per_token(top8[:, :, 1:2]), ALU.is_gt)
            link(v.tensor_tensor(both(EQ), both(LOG), per_token(top8[:, :, 1:2]), ALU.is_equal))
            for t in range(NT):
                v.tensor_tensor_scan(route[:, INC, t, :], ones[:, 0:NE], route[:, EQ, t, :], 0.0, ALU.mult, ALU.add)
            link(v.tensor_reduce(rcol[:, 1, :], both(GT), AX.X, ALU.add))
            link(v.tensor_scalar(rcol[:, 2, :], rcol[:, 1, :], -1.0, 2.0, ALU.mult, ALU.add))
            for t in range(NT):
                last = v.scalar_tensor_tensor(out=route[:, INC, t, :], in0=route[:, INC, t, :], scalar=rcol[:, 2, t:t + 1],
                                              in1=route[:, EQ, t, :], op0=ALU.is_le, op1=ALU.mult)
            link(last)
            v.tensor_tensor(both(MASK), both(INC), both(GT), ALU.add).then_inc(mask_ready, 1)
            dve.wait_ge(mask_ready, 1)
            v.tensor_scalar(both(OFF), both(MASK), 1000.0, -1000.0, ALU.mult, ALU.add)
            v.memset(gate_of[:, :, 2 * NE:], 0.0)
            v.memset(slot_of[:, :, 2 * NE:], -1000.0)
            dve.wait_ge(e_ready, 2)
            link(v.tensor_tensor(both(GATE), both(EXP), both(MASK), ALU.mult))
            link(v.tensor_reduce(rcol[:, 3, :], both(GATE), AX.X, ALU.add))
            link(v.reciprocal(rcol[:, 1, :], rcol[:, 3, :]))
            for t in range(NT):
                for first in (0, NE):
                    v.tensor_scalar(gate_of[:, t, first:first + NE], route[:, GATE, t, :], rcol[:, 1, t:t + 1], None, ALU.mult)
            dve.wait_ge(rank_done, 1)
            link(v.tensor_tensor(slot_of[:, :, 0:NE], both(OFF), bank[5][:, 0:NT * NE].rearrange("p (t e) -> p t e", t=NT), ALU.add))
            link(v.tensor_scalar(slot_of[:, :, NE:2 * NE], slot_of[:, :, 0:NE], float(P), None, ALU.subtract))
            link(v.tensor_reduce(njobs_f[:, 0:1], bank[5][:, NT * NE:NT * NE + NE], AX.X, ALU.max))
            link(v.tensor_scalar(njobs_f[:, 1:2], njobs_f[:, 0:1], float(P), float(NE), ALU.is_gt, ALU.mult))
            v.tensor_scalar(njobs[:], njobs_f[:, 1:2], float(NE), None, ALU.add).then_inc(njobs_ready, 1)

            def build_sel(j):
                for t in range(NT):
                    slot, gate = slot_of[:, t, bass.ds(j, 1)], gate_of[:, t, bass.ds(j, 1)]
                    v.tensor_scalar(sel[:, t, :], iota[:], slot, None, ALU.is_equal)
                    last = v.tensor_scalar(sel_g[:, t, :], iota[:], slot, gate, ALU.is_equal, ALU.mult)
                last.then_inc(sel_built, 1)

            def tokens_lo(j):
                for c in range(KD):
                    if c % 4 == 0:
                        dve.wait_ge(tok_hi_done, KD * j + c + 4)
                    part = (slice(None), c // 2, slice((c % 2) * P, (c % 2 + 1) * P))
                    v.scalar_tensor_tensor(out=act_lo[part], in0=bank[6 + c // 4][:, (c % 4) * P:(c % 4 + 1) * P],
                                           scalar=cols[:, R_NORM + 3 * KD + c:R_NORM + 3 * KD + c + 1],
                                           in1=act_hi[part].bitcast(f32), op0=ALU.mult, op1=ALU.subtract).then_inc(tok_lo_done, 1)

            def y_lo_part(j):
                for half in range(2):
                    dve.wait_ge(yhi_done, 2 * j + half + 1)
                    cut = slice(HALF * half, HALF * half + HALF)
                    v.scalar_tensor_tensor(out=y_lo[:, cut], in0=bank[half][:], scalar=gslot[:, 0:1],
                                           in1=y_hi[:, cut].bitcast(f32), op0=ALU.mult, op1=ALU.subtract).then_inc(ylo_done, 1)

            def add_scattered(j):
                for half in range(2):
                    for t in range(NT):
                        dve.wait_ge(scattered, 4 * j + 2 * half + t + 1)
                        part = x[:, t, HALF * half:HALF * half + HALF]
                        v.tensor_tensor(part, part, bank[4 + 2 * half + t][:], ALU.add).then_inc(moe_added, 1)

            build_sel(0)
            v.memset(sel_T[:].bitcast(i32), 0)
            v.memset(gslot[:], 0.0).then_inc(selT_ready, 1)
            v.memset(bank[0][:], 0.0).then_inc(moe_blank, 1)
            v.memset(bank[1][:], 0.0).then_inc(moe_blank, 1)
            tokens_lo(0)
            jobs = dve.value_load(njobs[0:1, 0:1], min_val=NE, max_val=2 * NE)
            with dve.Fori(0, jobs) as j:
                for k in range(JU):
                    if k == 0:
                        y_lo_part(j)
                    if k == 4 or (k >= 8 and k % 6 == 2 and k // 6 < CH):
                        c = 0 if k == 4 else k // 6
                        dve.wait_ge(e_silu, CH * j + c + 1)
                        dve.wait_ge(unit_used, U_MOE + JU * j + k)
                        if c:
                            dve.wait_ge(e_T, CH * j + c)
                        v.tensor_tensor(hid[:], silu[:], bank[3][:], ALU.mult).then_inc(e_h, 1)
                    if k == 5:
                        add_scattered(j)
                    if (k >= 6 and k % 6 == 0) or k == JU - 3:
                        c = k // 6 - 1 if k < JU - 3 else CH - 1
                        dve.wait_ge(e_hid_hi, CH * j + c + 1)
                        v.tensor_tensor(hid_lo[:, c % 2, :], bank[4 + c % 2][:], hid_hi[:, c % 2, :].bitcast(f32),
                                        ALU.subtract).then_inc(e_hid_lo, 1)
                    if k == 9:
                        dve.wait_ge(selg_T, j + 1)
                        v.tensor_reduce(gslot[:], bank[6][:, 0:T], AX.X, ALU.add)
                        v.tensor_scalar(sel_T[:], bank[6][:, 0:T], 0.0, None, ALU.is_gt).then_inc(selT_ready, 1)
                    if k == 20:
                        build_sel(j + 1)
                    if k == JU - 2:
                        tokens_lo(j + 1)
                    split_lo(U_MOE + k + LEAD, J6 * j)
            y_lo_part(jobs)
            add_scattered(jobs)
            dve.wait_ge(moe_added, 4 * jobs + 4)
            squares(4)
            dve.wait_ge(rstd_ready, 5)
            dve.wait_ge(gfin_loaded, 16)
            for t in range(NT):
                v.scalar_tensor_tensor(out=xs[:, t, :], in0=x[:, t, :], scalar=rstd[:, 4, t:t + 1], in1=gfin_bc[:],
                                       op0=ALU.mult, op1=ALU.mult).then_inc(out_ready, 1)

        @block.tensor
        def _(pe):
            t_ = nc.tensor

            def mm3(dst, l_hi, l_lo, r_hi, r_lo, start, stop):
                t_.matmul(dst, l_lo, r_hi, start=start, stop=False)
                t_.matmul(dst, l_hi, r_lo, start=False, stop=False)
                return t_.matmul(dst, l_hi, r_hi, start=False, stop=stop)

            def unit_ready(u, n=0):
                pe.wait_ge(lo_done, units(u, n) + 1)

            def stationary_unit(u, n, a_hi, a_lo, dst, first_count=None):
                unit_ready(u, n)
                for f in range(2):
                    for k in range(KD):
                        if first_count is not None and f == 0:
                            pe.wait_ge(act_lo_done, first_count + k + 1)
                        w = slice(k * 256 + f * P, k * 256 + f * P + P)
                        last = mm3(dst[:, f * T:(f + 1) * T], w_hi[:, u % SPL, w], w_lo[:, u % SPL, w],
                                   a_hi[:, k, :], a_lo[:, k, :], k == 0, k == KD - 1)
                last.then_inc(unit_used, 1)

            def moving_unit(u, a_hi, a_lo, k_half, dst, before_k=None):
                unit_ready(u)
                for k in range(4):
                    kk = 4 * k_half + k
                    if before_k:
                        before_k(kk)
                    for t in range(NT):
                        w = slice(k * 512, k * 512 + 512)
                        last = mm3(dst[t][:], a_hi[:, kk, t * P:(t + 1) * P], a_lo[:, kk, t * P:(t + 1) * P],
                                   w_hi[:, u % SPL, w], w_lo[:, u % SPL, w], kk == 0, kk == KD - 1)
                last.then_inc(unit_used, 1)

            def keep_warm(n, b=7):
                for _ in range(n):
                    t_.matmul(bank[b][:, 0:T], ones[:, 0:P], ones[:], start=True, stop=True)

            def transpose_x(n):
                for t in range(NT):
                    pe.wait_ge(xs_ready, 2 * n + t + 1)
                    for c in range(KD):
                        dst = bank[c // 2][:, (c % 2) * T + t * P:(c % 2) * T + (t + 1) * P]
                        last = t_.transpose(dst, xs[:, t, c * P:(c + 1) * P], ident[:])
                        if t == NT - 1 and c % 2:
                            last.then_inc(norm_T, 1)

            pe.wait_ge(consts, 5)
            keep_warm(4, 6)
            pe.wait_ge(rows_loaded, 6 * 16)
            t_.transpose(bank[7][:, 0:R_END], rows[0:R_END, :], ident[0:R_END, 0:R_END]).then_inc(rows_T, 1)
            keep_warm(2, 6)

            transpose_x(0)
            pe.wait_ge(cols_ready, 1)

            def lru_gates(c):
                pe.wait_ge(xc_ready, c + 1)
                if c == 0:
                    pe.wait_ge(gatew_loaded, 16)
                if c >= 4:
                    pe.wait_ge(sig_done, 2 * (c - 4) + 2)
                else:
                    pe.wait_ge(act_lo_done, KD)
                for g in range(2):
                    last = t_.matmul(bank[c % 4][:, g * T:(g + 1) * T], gate_w[:, g * KD + c, :], xc[:, c, :], start=True, stop=True)
                last.then_inc(gates_done, 1)

            for u in range(8):
                if u >= 4:
                    pe.wait_ge(xb_ready, u - 3)
                stationary_unit(u, 0, act_hi, act_lo, bank[4 + u % 4], 0 if u == 0 else None)
                if 1 <= u <= 4:
                    lru_gates(2 * u - 2)
                    lru_gates(2 * u - 1)
            pe.wait_ge(sig_done, 2 * KD)
            for c in range(4):
                moving_unit(U_OUT + c, alt_hi, alt_lo, c % 2, [bank[2 * (c // 2)], bank[2 * (c // 2) + 1]],
                            (lambda kk: pe.wait_ge(alt_lo_done, kk // 2 + 1)) if c < 2 else None)

            pe.wait_ge(gelu_done, 4)
            keep_warm(7)
            pe.wait_ge(x_added, 4)
            transpose_x(1)

            def ff_gate_up(u, n, m, first_count=None):
                stationary_unit(u, n, act_hi, act_lo, bank[4 + 2 * (m % 2)], first_count)
                stationary_unit(u + 1, n, act_hi, act_lo, bank[5 + 2 * (m % 2)])

            def ff_down(u, n, p, m, first, last_one):
                unit_ready(u, n)
                pe.wait_ge(hid_lo_done, p + 1)
                for k in range(2):
                    for t in range(NT):
                        h = slice(k * T + t * P, k * T + (t + 1) * P)
                        for half in range(2):
                            w = slice(k * D + half * HALF, k * D + half * HALF + HALF)
                            last = mm3(bank[2 * half + t][:], hid_hi[:, m % 2, h], hid_lo[:, m % 2, h],
                                       w_hi[:, u % SPL, w], w_lo[:, u % SPL, w], first and k == 0, last_one and k == 1)
                last.then_inc(unit_used, 1)

            ff_gate_up(U_FF, 0, 0, KD)
            ff_gate_up(U_FF + 2, 0, 1)
            pe.wait_ge(act_lo_done, 2 * KD)
            ff_down(U_FF + 4, 0, 0, 0, True, False)
            with pe.Fori(0, (PAIRS - 3) // 2) as i:
                for m in (2, 3):
                    u = U_FF + 3 * m - 1
                    pe.wait_ge(h_done, 2 * i + m - 1)
                    ff_gate_up(u, i, m)
                    ff_down(u + 2, i, 2 * i + m - 1, m - 1, False, False)
            u = U_FF + 3 * (PAIRS - 1) - 1
            pe.wait_ge(h_done, PAIRS - 2)
            ff_gate_up(u, 0, PAIRS - 1)
            ff_down(u + 2, 0, PAIRS - 2, PAIRS - 2, False, False)
            ff_down(u + 3, 0, PAIRS - 1, PAIRS - 1, False, True)

            keep_warm(9)
            pe.wait_ge(x_added, 8)
            transpose_x(2)
            pe.wait_ge(small_lo, 2)
            for k in range(KD):
                pe.wait_ge(act_lo_done, 2 * KD + k + 1)
                last = mm3(bank[6][0:NHEADS, 0:T], wf_hi[:, k, :], wf_lo[:, k, :], alt_hi[:, k, :], alt_lo[:, k, :], k == 0, k == KD - 1)
            last.then_inc(f_done, 1)
            for c in range(4):
                if c >= 2:
                    pe.wait_ge(k_ready, c - 1)
                stationary_unit(U_K + c, 0, alt_hi, alt_lo, bank[4 + c % 2])
            pe.wait_ge(act_lo_done, 4 * KD)
            for c in range(4):
                moving_unit(U_V + c, alt_hi, alt_lo, c % 2, [bank[2 * (c // 2)], bank[2 * (c // 2) + 1]])
            for c in range(4):
                pe.wait_ge(k_ready if c < 2 else q_ready, 3 + c if c < 2 else c - 1)
                stationary_unit(U_Q + c, 0, act_hi, act_lo, bank[4 + c % 2])

            pe.wait_ge(v_ready, 4)
            pe.wait_ge(consts_v, 2)
            pe.wait_ge(c_lo_done, 2)
            for i in range(NHEADS + 3):
                if i < NHEADS:
                    rows_h = slice(HD * (i % 2), HD * (i % 2) + HD)
                    hp = i // 2
                    if i % 4 == 0:
                        pe.wait_ge(q_ready, i // 4 + 1)
                    if i >= 2:
                        pe.wait_ge(p_exp, 2 * (i - 2) + 2)
                    pe.wait_ge(c_sel_ready, i + 1)
                    for t in range(NT):
                        keys, queries = slice(0, P * (t + 1)), slice(P * t, P * (t + 1))
                        dst = bank[i % 2][:, P * t:P * t + P * (t + 1)]
                        t_.matmul(dst, c_sel[:, i % 2, queries], c_neg[:, keys], start=True, stop=False)
                        t_.matmul(bank[i % 2][:, 2 * P * t:2 * P * t + P], ident_bf[:], mask_bf[:], start=False, stop=False)
                        last = t_.matmul(dst, q_T[rows_h, hp, queries], k_T[rows_h, hp, keys], start=False, stop=True)
                    last.then_inc(s_done, 1)
                if i % 4 == 1 and i // 4 < 4:
                    c = i // 4
                    if c >= 2:
                        pe.wait_ge(tg_ready, c - 1)
                    stationary_unit(U_G + c, 0, act_hi, act_lo, bank[6 + c % 2])
                if 2 <= i <= NHEADS + 1:
                    h = i - 2
                    pe.wait_ge(p_norm, h + 1)
                    if h >= 2:
                        pe.wait_ge(pt_ready, h - 1)
                    for n in range(3):
                        last = t_.transpose(bank[2 + h % 2][:, n * P:(n + 1) * P], prob[:, h % PS, n * P:(n + 1) * P], ident[:])
                    last.then_inc(pt_done, 1)
                if i >= 3:
                    h = i - 3
                    hp = h // 2
                    pe.wait_ge(pt_ready, h + 1)
                    if h % 2 == 0 and hp >= 2:
                        pe.wait_ge(o_ready, hp - 1)
                    o = bank[4 + hp % 2][HD * (h % 2):HD * (h % 2) + HD, :]
                    t_.matmul(o[:, 0:T], v_sb[:, 0, h * HD:(h + 1) * HD], prob_T[:, h % 2, 0:T], start=True, stop=False)
                    t_.matmul(o[:, P:T], v_sb[:, 1, h * HD:(h + 1) * HD], prob_T[:, h % 2, T:3 * P], start=False, stop=True).then_inc(pv_done, 1)
            for c in range(4):
                moving_unit(U_O + c, alt_hi, alt_lo, c % 2, [bank[2 * (c // 2)], bank[2 * (c // 2) + 1]],
                            (lambda kk: pe.wait_ge(alt_lo_done, 4 + kk + 1)) if c < 2 else None)

            keep_warm(7)
            pe.wait_ge(x_added, 12)
            transpose_x(3)
            keep_warm(4)
            for k in range(KD):
                pe.wait_ge(act_lo_done, 4 * KD + k + 1)
                last = mm3(bank[4][0:NE, 0:T], rt_hi[:, k, :], rt_lo[:, k, :], act_hi[:, k, :], act_lo[:, k, :], k == 0, k == KD - 1)
            last.then_inc(logits_done, 1)
            keep_warm(1)
            pe.wait_ge(logitT_ready, 1)
            for t in range(NT):
                last = t_.transpose(bank[5][:, t * NE:(t + 1) * NE], logit_T[:, t * P:(t + 1) * P], ident[0:NE, 0:NE])
            last.then_inc(logits_done, 1)
            keep_warm(4)
            pe.wait_ge(mask_ready, 1)
            m0, m1 = route[:, 3, 0, :], route[:, 3, 1, :]
            t_.matmul(bank[5][:, 0:NE], before[:], m0, start=True, stop=True)
            t_.matmul(bank[5][:, NE:2 * NE], ones[:, 0:P], m0, start=True, stop=False)
            t_.matmul(bank[5][:, NE:2 * NE], before[:], m1, start=False, stop=True)
            t_.matmul(bank[5][:, 2 * NE:3 * NE], ones[:, 0:P], m0, start=True, stop=False)
            t_.matmul(bank[5][:, 2 * NE:3 * NE], ones[:, 0:P], m1, start=False, stop=True).then_inc(rank_done, 1)

            src_hi = alt_hi[:].rearrange("p c n -> p (c n)")
            src_lo = alt_lo[:].rearrange("p c n -> p (c n)")

            def gather():
                for c in range(KD):
                    dst = bank[6 + c // 4][:, (c % 4) * P:(c % 4 + 1) * P]
                    for t in range(NT):
                        w = slice(t * D + c * P, t * D + (c + 1) * P)
                        t_.matmul(dst, src_lo[:, w], sel[:, t, :], start=(t == 0), stop=False)
                        last = t_.matmul(dst, src_hi[:, w], sel[:, t, :], start=False, stop=(t == NT - 1))
                    if c % 4 == 3:
                        last.then_inc(gathered, 1)

            def scatter(j):
                pe.wait_ge(ylo_done, 2 * j + 2)
                for half in range(2):
                    w = slice(HALF * half, HALF * half + HALF)
                    for t in range(NT):
                        dst = bank[4 + 2 * half + t][:]
                        t_.matmul(dst, sel_T[:, t * P:(t + 1) * P], y_lo[:, w], start=True, stop=False)
                        t_.matmul(dst, sel_T[:, t * P:(t + 1) * P], y_hi[:, w], start=False, stop=True).then_inc(scattered, 1)

            def expert_in(u, n, dst, k_half):
                unit_ready(u, n)
                for k in range(4):
                    kk = 4 * k_half + k
                    s = (slice(None), kk // 2, slice((kk % 2) * P, (kk % 2 + 1) * P))
                    w = slice(k * 512, k * 512 + 512)
                    last = mm3(dst[:], act_hi[s], act_lo[s], w_hi[:, u % SPL, w], w_lo[:, u % SPL, w], kk == 0, kk == KD - 1)
                last.then_inc(unit_used, 1)

            def expert_out(u, n, c, k_half):
                unit_ready(u, n)
                for k in range(2):
                    h = slice((2 * k_half + k) * P, (2 * k_half + k + 1) * P)
                    for half in range(2):
                        w = slice(k * D + half * HALF, k * D + half * HALF + HALF)
                        first, final = c == 0 and k_half == 0 and k == 0, c == CH - 1 and k_half == 1 and k == 1
                        last = mm3(bank[half][:], hid_hi[:, c % 2, h], hid_lo[:, c % 2, h],
                                   w_hi[:, u % SPL, w], w_lo[:, u % SPL, w], first, final)
                last.then_inc(unit_used, 1)

            def hidden_T(j, c):
                pe.wait_ge(e_h, CH * j + c + 1)
                for n in range(4):
                    last = t_.transpose(bank[4 + c % 2][:, n * P:(n + 1) * P], hid[:, n * P:(n + 1) * P], ident[:])
                last.then_inc(e_T, 1)

            pe.wait_ge(src_ready, 1)
            keep_warm(5)
            pe.wait_ge(sel_built, 1)
            gather()
            keep_warm(7, 3)
            pe.wait_ge(njobs_ready, 1)
            jobs = pe.value_load(njobs[0:1, 0:1], min_val=NE, max_val=2 * NE)
            with pe.Fori(0, jobs) as j:
                n = J6 * j
                pe.wait_ge(tok_lo_done, KD * j + 4)
                for c in range(CH):
                    u = U_MOE + (6 * c - 2 if c else 0)
                    if c:
                        pe.wait_ge(e_silu, CH * j + c)
                    expert_in(u, n, bank[2], 0)
                    if c == 0:
                        pe.wait_ge(tok_lo_done, KD * j + KD)
                    expert_in(u + 1, n, bank[2], 1)
                    if c == 1:
                        pe.wait_ge(moe_added, 4 * j + 4)
                    if c:
                        hidden_T(j, c - 1)
                    expert_in(u + 2, n, bank[3], 0)
                    expert_in(u + 3, n, bank[3], 1)
                    if c == 0:
                        scatter(j)
                    if c == 1:
                        for t in range(NT):
                            last = t_.transpose(bank[6][:, t * P:(t + 1) * P], sel_g[:, t, :], ident[:])
                        last.then_inc(selg_T, 1)
                    if c:
                        pe.wait_ge(e_hid_lo, CH * j + c)
                        expert_out(u + 4, n, c - 1, 0)
                        if c == CH - 1:
                            hidden_T(j, c)
                            pe.wait_ge(sel_built, j + 2)
                            pe.wait_ge(selT_ready, j + 2)
                            gather()
                        expert_out(u + 5, n, c - 1, 1)
                pe.wait_ge(e_hid_lo, CH * j + CH)
                expert_out(U_MOE + JU - 2, n, CH - 1, 0)
                expert_out(U_MOE + JU - 1, n, CH - 1, 1)
            pe.wait_ge(tok_lo_done, KD * jobs + KD)
            scatter(jobs)


_INS = ["x", "norm_g", "lru_w_in", "lru_conv_w", "lru_conv_b", "lru_gate_w", "lru_gate_b", "lru_lambda", "lru_w_out",
        "kv_norm_g", "w_kvf", "b_f", "fox_w_qg", "fox_w_o", "mlp_w_gu", "mlp_w_down", "moe_router", "moe_w_gu",
        "moe_w_down", "final_norm_g"]


def kernel(**inputs):
    import numpy as _np
    import concourse.bacc as _bacc
    from concourse.bass_utils import run_bass_kernel_spmd as _run

    nc = _bacc.Bacc("TRN2", target_bir_lowering=False, num_devices=1)
    arrays, args = {}, []
    for name in _INS:
        a = _np.ascontiguousarray(inputs[name])
        arrays[f"in_{name}"] = a
        args.append(nc.dram_tensor(f"in_{name}", a.shape, mybir.dt.from_np(a.dtype), kind="ExternalInput").ap())
    out = nc.dram_tensor("out_0", (1, T, D), mybir.dt.float32, kind="ExternalOutput").ap()
    yoco_kernel(nc, *args, out)
    r = _run(nc, [arrays], core_ids=[0])
    return r.results[0]["out_0"]
```
